# Optimizing a Trainium2 kernel written in Bass

```python
import math
import jax, jax.numpy as jnp
from jax import lax
import numpy as np

D_MODEL = 1024
BATCH = 1
SEQ = 512
DEPTH = 2

CHUNK = 64
Q_BLOCK = 128
N_A_LAYERS = DEPTH // 2
N_B_LAYERS = DEPTH - N_A_LAYERS
SSM_GROUP = 16
N_GROUPS = D_MODEL // SSM_GROUP
SSM_STATE = 64
HEAD_DIM = 64
N_HEADS = D_MODEL // HEAD_DIM
D_FF = 2816
CONV_W = 3
EPS = 1e-6
DT_MIN = 1e-3
DT_MAX = 1e-1


def rms_norm(x, g):
    xf = x.astype(jnp.float32)
    y = xf * lax.rsqrt(jnp.mean(xf * xf, axis=-1, keepdims=True) + EPS)
    return (y * g.astype(jnp.float32)).astype(x.dtype)

def s5_mixer(xn, w_in, lam_re, lam_im, b_re, b_im, c_re, c_im, d_skip, log_dt, w_glu):
    f32 = jnp.float32
    bsz, seq, _ = xn.shape
    u = (xn @ w_in).astype(f32)
    lam = lax.complex(lam_re.astype(f32), lam_im.astype(f32))
    dt = jnp.exp(log_dt.astype(f32))[:, None]
    a_bar = jnp.exp(lam * dt)
    b_mat = lax.complex(b_re.astype(f32), b_im.astype(f32))
    b_bar = ((a_bar - 1.0) / lam)[..., None] * b_mat
    c_mat = lax.complex(c_re.astype(f32), c_im.astype(f32))
    n_chunks = seq // CHUNK
    u_c = u.reshape(bsz, n_chunks, CHUNK, N_GROUPS, SSM_GROUP).transpose(1, 2, 0, 3, 4)
    a_elems = jnp.broadcast_to(a_bar, (CHUNK, 1, N_GROUPS, SSM_STATE))

    def binop(left, right):
        a_l, b_l = left
        a_r, b_r = right
        return a_r * a_l, a_r * b_l + b_r

    def chunk_step(h0, u_t):
        bu = jnp.einsum('tbgh,gph->tbgp', u_t.astype(jnp.complex64), b_bar)
        a_cum, s = lax.associative_scan(binop, (a_elems, bu), axis=0)
        s = s + a_cum * h0[None]
        y = jnp.einsum('tbgp,ghp->tbgh', s, c_mat).real
        return s[-1], y

    h0 = jnp.zeros((bsz, N_GROUPS, SSM_STATE), jnp.complex64)
    _, y = lax.scan(chunk_step, h0, u_c)
    y = y.transpose(2, 0, 1, 3, 4).reshape(bsz, seq, D_MODEL)
    y = y + d_skip.astype(f32) * u
    g = jax.nn.gelu(y).astype(xn.dtype)
    val, gate = jnp.split(g @ w_glu, 2, axis=-1)
    return val * jax.nn.sigmoid(gate)

def shared_kv(h, kv_norm, w_kv, k_norm):
    bsz, seq, _ = h.shape
    k, v = jnp.split(rms_norm(h, kv_norm) @ w_kv, 2, axis=-1)
    k = rms_norm(k.reshape(bsz, seq, N_HEADS, HEAD_DIM), k_norm)
    v = v.reshape(bsz, seq, N_HEADS, HEAD_DIM)
    return k, v

def stick_breaking_attention(q, k, v):
    seq = q.shape[1]
    scale = HEAD_DIM ** -0.5
    outs = []
    for i in range(seq // Q_BLOCK):
        q0 = i * Q_BLOCK
        kv_len = q0 + Q_BLOCK
        z = jnp.einsum('bqhd,bkhd->bhqk', q[:, q0:kv_len], k[:, :kv_len]).astype(jnp.float32) * scale
        q_pos = q0 + jnp.arange(Q_BLOCK)[:, None]
        k_pos = jnp.arange(kv_len)[None, :]
        causal = k_pos < q_pos
        log_beta = jax.nn.log_sigmoid(z)
        log_1m = jnp.where(causal, log_beta - z, 0.0)
        later = lax.cumsum(log_1m, axis=3, reverse=True) - log_1m
        w = jnp.where(causal, jnp.exp(log_beta + later), 0.0)
        outs.append(jnp.einsum('bhqk,bkhd->bqhd', w.astype(v.dtype), v[:, :kv_len]))
    return jnp.concatenate(outs, axis=1)

def sb_mixer(xn, w_q, q_norm, k, v, w_o):
    bsz, seq, _ = xn.shape
    q = rms_norm((xn @ w_q).reshape(bsz, seq, N_HEADS, HEAD_DIM), q_norm)
    o = stick_breaking_attention(q, k, v)
    return o.reshape(bsz, seq, D_MODEL) @ w_o

def conv_ffn(xn, w_up, conv_w, conv_b, w_down):
    seq = xn.shape[1]
    val, gate = jnp.split(xn @ w_up, 2, axis=-1)
    gp = jnp.pad(gate, ((0, 0), (CONV_W - 1, 0), (0, 0)))
    gc = conv_b + conv_w[0] * gp[:, 0:seq]
    for j in range(1, CONV_W):
        gc = gc + conv_w[j] * gp[:, j:j + seq]
    return (jax.nn.silu(gc) * val) @ w_down

def first_inputs(seed: int = 0) -> dict:
    key = jax.random.key(seed)
    ks = iter(jax.random.split(key, 32))

    def nrm(shape, scale):
        return scale * jax.random.normal(next(ks), shape, jnp.float32)

    def gain(shape):
        return 1.0 + nrm(shape, 0.02)

    d, f = D_MODEL, D_FF
    na, nb = N_A_LAYERS, N_B_LAYERS
    G, P, H = N_GROUPS, SSM_STATE, SSM_GROUP
    n_idx = jnp.arange(P, dtype=jnp.float32)
    x = nrm((BATCH, SEQ, d), 1.0)
    a_norm = gain((na, d))
    a_w_in = nrm((na, d, d), d ** -0.5)
    a_lam_re = -0.5 + nrm((na, G, P), 0.01)
    a_lam_im = math.pi * n_idx + nrm((na, G, P), 0.01)
    a_b_re = nrm((na, G, P, H), (2 * H) ** -0.5)
    a_b_im = nrm((na, G, P, H), (2 * H) ** -0.5)
    a_c_re = nrm((na, G, H, P), P ** -0.5)
    a_c_im = nrm((na, G, H, P), P ** -0.5)
    a_d = nrm((na, d), 1.0)
    a_log_dt = jax.random.uniform(next(ks), (na, G), jnp.float32, math.log(DT_MIN), math.log(DT_MAX))
    a_w_glu = nrm((na, d, 2 * d), d ** -0.5)
    kv_norm = gain((d,))
    w_kv = nrm((d, 2 * d), d ** -0.5)
    k_norm = gain((HEAD_DIM,))
    b_norm = gain((nb, d))
    b_w_q = nrm((nb, d, d), d ** -0.5)
    b_q_norm = gain((nb, HEAD_DIM))
    b_w_o = nrm((nb, d, d), d ** -0.5)
    ffn_norm = gain((DEPTH, d))
    ffn_w_up = nrm((DEPTH, d, 2 * f), d ** -0.5)
    ffn_conv_w = nrm((DEPTH, CONV_W, f), CONV_W ** -0.5)
    ffn_conv_b = nrm((DEPTH, f), 0.02)
    ffn_w_down = nrm((DEPTH, f, d), f ** -0.5)
    return {"x": x, "a_norm": a_norm, "a_w_in": a_w_in, "a_lam_re": a_lam_re, "a_lam_im": a_lam_im,
            "a_b_re": a_b_re, "a_b_im": a_b_im, "a_c_re": a_c_re, "a_c_im": a_c_im, "a_d": a_d,
            "a_log_dt": a_log_dt, "a_w_glu": a_w_glu, "kv_norm": kv_norm, "w_kv": w_kv, "k_norm": k_norm,
            "b_norm": b_norm, "b_w_q": b_w_q, "b_q_norm": b_q_norm, "b_w_o": b_w_o,
            "ffn_norm": ffn_norm, "ffn_w_up": ffn_w_up, "ffn_conv_w": ffn_conv_w,
            "ffn_conv_b": ffn_conv_b, "ffn_w_down": ffn_w_down}

def first_block(x, a_norm, a_w_in, a_lam_re, a_lam_im, a_b_re, a_b_im, a_c_re, a_c_im, a_d,
              a_log_dt, a_w_glu, kv_norm, w_kv, k_norm, b_norm, b_w_q, b_q_norm, b_w_o,
              ffn_norm, ffn_w_up, ffn_conv_w, ffn_conv_b, ffn_w_down):
    h = x
    k = None
    v = None
    for layer in range(DEPTH):
        if layer < N_A_LAYERS:
            i = layer
            h = h + s5_mixer(rms_norm(h, a_norm[i]), a_w_in[i], a_lam_re[i], a_lam_im[i],
                             a_b_re[i], a_b_im[i], a_c_re[i], a_c_im[i], a_d[i], a_log_dt[i], a_w_glu[i])
        else:
            j = layer - N_A_LAYERS
            if j == 0:
                k, v = shared_kv(h, kv_norm, w_kv, k_norm)
            h = h + sb_mixer(rms_norm(h, b_norm[j]), b_w_q[j], b_q_norm[j], k, v, b_w_o[j])
        h = h + conv_ffn(rms_norm(h, ffn_norm[layer]), ffn_w_up[layer], ffn_conv_w[layer],
                         ffn_conv_b[layer], ffn_w_down[layer])
    return h


N_B_LAYERS_2 = DEPTH // 2
N_A_LAYERS_2 = DEPTH - N_B_LAYERS_2

SSM_EXPAND = 2
SSM_D_INNER = SSM_EXPAND * D_MODEL
SSM_HEAD_DIM = 64
SSM_HEADS = SSM_D_INNER // SSM_HEAD_DIM
SSM_GROUPS = 8
SSM_HEADS_PER_GROUP = SSM_HEADS // SSM_GROUPS
SSM_STATE_2 = 128
SSM_CONV = 4
SSM_CONV_DIM = SSM_D_INNER + 2 * SSM_GROUPS * SSM_STATE_2
SSM_IN_DIM = 2 * SSM_D_INNER + 2 * SSM_GROUPS * SSM_STATE_2 + SSM_HEADS
SSD_CHUNK = CHUNK

DIFF_HEAD_DIM = 64
DIFF_V_DIM = 2 * DIFF_HEAD_DIM
DIFF_HEADS = D_MODEL // DIFF_V_DIM
DIFF_WIDTH = DIFF_HEADS * DIFF_V_DIM
KV_DIM = DIFF_HEADS * 2 * DIFF_HEAD_DIM + DIFF_WIDTH
ALIBI_MAX_EXP = 8.0

EPS_2 = 1e-5


def rms_norm_2(x, g):
    xf = x.astype(jnp.float32)
    y = xf * lax.rsqrt(jnp.mean(xf * xf, axis=-1, keepdims=True) + EPS_2)
    return (y * g.astype(jnp.float32)).astype(x.dtype)

def gated_group_rms_norm(y, z, g):
    u = y.astype(jnp.float32) * jax.nn.silu(z.astype(jnp.float32))
    shp = u.shape
    u = u.reshape(shp[:-1] + (SSM_GROUPS, SSM_D_INNER // SSM_GROUPS))
    u = u * lax.rsqrt(jnp.mean(u * u, axis=-1, keepdims=True) + EPS_2)
    return u.reshape(shp) * g.astype(jnp.float32)

def causal_depthwise_conv(u, w, bias):
    c = u.shape[-1]
    out = lax.conv_general_dilated(
        u, w[:, None, :].astype(u.dtype), window_strides=(1,),
        padding=[(SSM_CONV - 1, 0)], dimension_numbers=("NWC", "WIO", "NWC"),
        feature_group_count=c)
    return out + bias.astype(u.dtype)

def ssd_chunked_scan(xdt, adt, bm, cm):
    b, s = xdt.shape[:2]
    nc = s // SSD_CHUNK

    def to_chunks(t):
        return jnp.moveaxis(t.reshape((b, nc, SSD_CHUNK) + t.shape[2:]), 1, 0)

    causal = jnp.tril(jnp.ones((SSD_CHUNK, SSD_CHUNK), dtype=bool))[None, :, :, None, None]

    def step(state, inp):
        x_c, a_c, b_c, c_c = inp
        acs = jnp.cumsum(a_c, axis=1)
        seg = acs[:, :, None] - acs[:, None, :]
        decay = jnp.exp(jnp.where(causal, seg, -jnp.inf))
        cb = jnp.einsum("blgn,bsgn->blsg", c_c, b_c)
        y_diag = jnp.einsum("blsgr,bsgrp->blgrp", cb[..., None] * decay, x_c)
        y_off = jnp.einsum("blgn,bgrpn->blgrp", c_c, state) * jnp.exp(acs)[..., None]
        to_end = jnp.exp(acs[:, -1:] - acs)
        new_state = (state * jnp.exp(acs[:, -1])[..., None, None]
                     + jnp.einsum("blgn,blgrp->bgrpn", b_c, x_c * to_end[..., None]))
        return new_state, y_diag + y_off

    state0 = jnp.zeros((b, SSM_GROUPS, SSM_HEADS_PER_GROUP, SSM_HEAD_DIM, SSM_STATE_2), jnp.float32)
    _, ys = lax.scan(step, state0, (to_chunks(xdt), to_chunks(adt), to_chunks(bm), to_chunks(cm)))
    return jnp.moveaxis(ys, 0, 1).reshape(xdt.shape)

def mamba2_layer(x, norm_g, w_in, conv_w, conv_b, dt_bias, a_log, d_skip, gate_norm_g, w_out):
    b, s, _ = x.shape
    G, R, P, N = SSM_GROUPS, SSM_HEADS_PER_GROUP, SSM_HEAD_DIM, SSM_STATE_2
    h = rms_norm_2(x, norm_g)
    zxbcdt = h @ w_in
    z = zxbcdt[..., :SSM_D_INNER]
    xbc = zxbcdt[..., SSM_D_INNER:SSM_D_INNER + SSM_CONV_DIM]
    dt_raw = zxbcdt[..., SSM_D_INNER + SSM_CONV_DIM:]
    xbc = jax.nn.silu(causal_depthwise_conv(xbc, conv_w, conv_b))
    gn = G * N
    xs = xbc[..., :SSM_D_INNER].reshape(b, s, G, R, P).astype(jnp.float32)
    bm = xbc[..., SSM_D_INNER:SSM_D_INNER + gn].reshape(b, s, G, N).astype(jnp.float32)
    cm = xbc[..., SSM_D_INNER + gn:].reshape(b, s, G, N).astype(jnp.float32)
    dt = jax.nn.softplus(dt_raw.astype(jnp.float32) + dt_bias.astype(jnp.float32)).reshape(b, s, G, R)
    a = -jnp.exp(a_log.astype(jnp.float32)).reshape(G, R)
    y = ssd_chunked_scan(xs * dt[..., None], a * dt, bm, cm)
    y = y + d_skip.astype(jnp.float32).reshape(G, R, 1) * xs
    y = gated_group_rms_norm(y.reshape(b, s, SSM_D_INNER), z, gate_norm_g).astype(x.dtype)
    return x + y @ w_out

def shared_kv_2(x, kv_norm_g, w_kv):
    b, s, _ = x.shape
    kv = rms_norm_2(x, kv_norm_g) @ w_kv
    k = kv[..., :DIFF_HEADS * 2 * DIFF_HEAD_DIM].reshape(b, s, DIFF_HEADS, 2, DIFF_HEAD_DIM)
    v = kv[..., DIFF_HEADS * 2 * DIFF_HEAD_DIM:].reshape(b, s, DIFF_HEADS, DIFF_V_DIM)
    return k.transpose(0, 2, 3, 1, 4), v.transpose(0, 2, 1, 3)

def diff_attention_layer(x, k, v, norm_g, w_in, lam_qk, sub_g, w_out, lambda_init):
    b, s, _ = x.shape
    H, d = DIFF_HEADS, DIFF_HEAD_DIM
    nblk = s // Q_BLOCK
    qg = rms_norm_2(x, norm_g) @ w_in
    q = qg[..., :DIFF_WIDTH].reshape(b, nblk, Q_BLOCK, H, 2, d).transpose(1, 0, 3, 4, 2, 5)
    gate = qg[..., DIFF_WIDTH:]
    lf = lam_qk.astype(jnp.float32)
    lam = jnp.exp(jnp.sum(lf[0] * lf[1])) - jnp.exp(jnp.sum(lf[2] * lf[3])) + lambda_init
    slopes = 2.0 ** (-ALIBI_MAX_EXP * jnp.arange(1, H + 1, dtype=jnp.float32) / H)
    key_pos = jnp.arange(s)
    scale = 1.0 / math.sqrt(d)

    def attend_block(args):
        qb, blk = args
        qpos = blk * Q_BLOCK + jnp.arange(Q_BLOCK)
        dist = jnp.abs(qpos[:, None] - key_pos[None, :]).astype(jnp.float32)
        allowed = (key_pos // CHUNK)[None, :] <= (qpos // CHUNK)[:, None]
        scores = jnp.einsum("bhiqd,bhikd->bhiqk", qb, k).astype(jnp.float32) * scale
        scores = scores - slopes[None, :, None, None, None] * dist
        probs = jax.nn.softmax(jnp.where(allowed, scores, -jnp.inf), axis=-1)
        weights = probs[:, :, 0] - lam * probs[:, :, 1]
        return jnp.einsum("bhqk,bhke->bqhe", weights.astype(v.dtype), v)

    out = lax.map(attend_block, (q, jnp.arange(nblk)))
    out = jnp.moveaxis(out, 0, 1).reshape(b, s, H, DIFF_V_DIM)
    out = (rms_norm_2(out, sub_g) * (1.0 - lambda_init)).reshape(b, s, DIFF_WIDTH)
    return x + (out * jax.nn.silu(gate)) @ w_out

def second_inputs(seed: int = 0) -> dict:
    key = jax.random.key(seed)
    ks = jax.random.split(key, 18)
    f32 = jnp.float32

    def nrm(k, shape, scale):
        return jax.random.normal(k, shape, f32) * scale

    def gain(k, shape):
        return 1.0 + 0.05 * jax.random.normal(k, shape, f32)

    x = jax.random.normal(ks[0], (BATCH, SEQ, D_MODEL), f32)
    a_norm_g = gain(ks[1], (N_A_LAYERS_2, D_MODEL))
    a_w_in = nrm(ks[2], (N_A_LAYERS_2, D_MODEL, SSM_IN_DIM), D_MODEL ** -0.5)
    a_conv_w = nrm(ks[3], (N_A_LAYERS_2, SSM_CONV, SSM_CONV_DIM), SSM_CONV ** -0.5)
    a_conv_b = nrm(ks[4], (N_A_LAYERS_2, SSM_CONV_DIM), 0.01)
    u = jax.random.uniform(ks[5], (N_A_LAYERS_2, SSM_HEADS), f32)
    dt0 = jnp.exp(u * (math.log(DT_MAX) - math.log(DT_MIN)) + math.log(DT_MIN))
    a_dt_bias = dt0 + jnp.log(-jnp.expm1(-dt0))
    a_a_log = jnp.log(jax.random.uniform(ks[6], (N_A_LAYERS_2, SSM_HEADS), f32, 1.0, 16.0))
    a_d_skip = gain(ks[7], (N_A_LAYERS_2, SSM_HEADS))
    a_gate_norm_g = gain(ks[8], (N_A_LAYERS_2, SSM_D_INNER))
    a_w_out = nrm(ks[9], (N_A_LAYERS_2, SSM_D_INNER, D_MODEL), SSM_D_INNER ** -0.5)
    kv_norm_g = gain(ks[10], (D_MODEL,))
    w_kv = nrm(ks[11], (D_MODEL, KV_DIM), D_MODEL ** -0.5)
    b_norm_g = gain(ks[12], (N_B_LAYERS_2, D_MODEL))
    b_w_in = nrm(ks[13], (N_B_LAYERS_2, D_MODEL, 2 * DIFF_WIDTH), D_MODEL ** -0.5)
    b_lambda = nrm(ks[14], (N_B_LAYERS_2, 4, DIFF_HEAD_DIM), 0.1)
    b_sub_g = gain(ks[15], (N_B_LAYERS_2, DIFF_V_DIM))
    b_w_out = nrm(ks[16], (N_B_LAYERS_2, DIFF_WIDTH, D_MODEL), DIFF_WIDTH ** -0.5)
    final_norm_g = gain(ks[17], (D_MODEL,))
    return {"x": x, "a_norm_g": a_norm_g, "a_w_in": a_w_in, "a_conv_w": a_conv_w,
            "a_conv_b": a_conv_b, "a_dt_bias": a_dt_bias, "a_a_log": a_a_log,
            "a_d_skip": a_d_skip, "a_gate_norm_g": a_gate_norm_g, "a_w_out": a_w_out,
            "kv_norm_g": kv_norm_g, "w_kv": w_kv, "b_norm_g": b_norm_g, "b_w_in": b_w_in,
            "b_lambda": b_lambda, "b_sub_g": b_sub_g, "b_w_out": b_w_out,
            "final_norm_g": final_norm_g}

def second_block(x, a_norm_g, a_w_in, a_conv_w, a_conv_b, a_dt_bias, a_a_log, a_d_skip,
              a_gate_norm_g, a_w_out, kv_norm_g, w_kv, b_norm_g, b_w_in, b_lambda,
              b_sub_g, b_w_out, final_norm_g):
    k = v = None
    for i in range(DEPTH):
        if i < N_A_LAYERS_2:
            x = mamba2_layer(x, a_norm_g[i], a_w_in[i], a_conv_w[i], a_conv_b[i],
                             a_dt_bias[i], a_a_log[i], a_d_skip[i], a_gate_norm_g[i], a_w_out[i])
            if i == N_A_LAYERS_2 - 1:
                k, v = shared_kv_2(x, kv_norm_g, w_kv)
        else:
            j = i - N_A_LAYERS_2
            lambda_init = 0.8 - 0.6 * math.exp(-0.3 * i)
            x = diff_attention_layer(x, k, v, b_norm_g[j], b_w_in[j], b_lambda[j],
                                     b_sub_g[j], b_w_out[j], lambda_init)
    return rms_norm_2(x, final_norm_g)


def setup_inputs(seed=0):
    out = dict(first_inputs(seed))
    for name, value in second_inputs(seed + 1).items():
        if name != "x":
            out[name + "_2"] = value
    return out


def reference(
    x, a_norm, a_w_in, a_lam_re, a_lam_im, a_b_re, a_b_im, a_c_re, a_c_im, a_d, a_log_dt,
    a_w_glu, kv_norm, w_kv, k_norm, b_norm, b_w_q, b_q_norm, b_w_o, ffn_norm, ffn_w_up,
    ffn_conv_w, ffn_conv_b, ffn_w_down, a_norm_g_2, a_w_in_2, a_conv_w_2, a_conv_b_2,
    a_dt_bias_2, a_a_log_2, a_d_skip_2, a_gate_norm_g_2, a_w_out_2, kv_norm_g_2, w_kv_2,
    b_norm_g_2, b_w_in_2, b_lambda_2, b_sub_g_2, b_w_out_2, final_norm_g_2,
):
    x = first_block(
        x, a_norm, a_w_in, a_lam_re, a_lam_im, a_b_re, a_b_im, a_c_re, a_c_im, a_d, a_log_dt,
        a_w_glu, kv_norm, w_kv, k_norm, b_norm, b_w_q, b_q_norm, b_w_o, ffn_norm, ffn_w_up,
        ffn_conv_w, ffn_conv_b, ffn_w_down,
    )
    return second_block(
        x, a_norm_g_2, a_w_in_2, a_conv_w_2, a_conv_b_2, a_dt_bias_2, a_a_log_2, a_d_skip_2,
        a_gate_norm_g_2, a_w_out_2, kv_norm_g_2, w_kv_2, b_norm_g_2, b_w_in_2, b_lambda_2,
        b_sub_g_2, b_w_out_2, final_norm_g_2,
    )


_drawn_inputs = setup_inputs


def setup_inputs(seed=0):
    import zlib

    import numpy as np

    out = dict(_drawn_inputs(seed))
    spreads = {}
    factors = {'a_norm': 4.833,
     'a_lam_re': 8.0,
     'kv_norm': 4.156,
     'k_norm': 8.0,
     'b_norm': 8.0,
     'b_q_norm': 8.0,
     'ffn_conv_b': 3.42,
     'a_conv_b_2': 6.801,
     'a_d_skip_2': 3.691,
     'kv_norm_g_2': 4.271,
     'b_norm_g_2': 4.195,
     'b_lambda_2': 8.0,
     'b_sub_g_2': 7.287}
    for name, (base, spread) in spreads.items():
        noise = np.random.default_rng([zlib.crc32(name.encode()), seed]).standard_normal(out[name].shape)
        drawn = base * np.exp(spread * noise) if base else spread * noise
        out[name] = __import__('jax').numpy.asarray(drawn.astype(out[name].dtype))
    for name, factor in factors.items():
        out[name] = (out[name] * factor).astype(out[name].dtype)
    return out
```

```python
import math
from contextlib import ExitStack

import numpy as np

import concourse.bass as bass
from concourse import mybir

P = 128
T = 512
D = 1024
F_FF = 2816
NF = F_FF // P
HALF = NF // 2
G5 = 64
NQ = 8
F32 = mybir.dt.float32
R32 = mybir.dt.float32r
BF16 = mybir.dt.bfloat16
ALU = mybir.AluOpType
ACT = mybir.ActivationFunctionType
AX = mybir.AxisListType
LAMBDA_INIT = 0.8 - 0.6 * math.exp(-0.3)
STAGES = ("s5", "ffn0", "att1", "ffn1", "mamba", "att2")

PARAMS = [
    ("a_norm", 8), ("kv_norm", 8), ("b_norm", 8), ("ffn_norm0", 8), ("ffn_norm1", 8), ("a_d", 8),
    ("k_norm", 1), ("q_norm", 1), ("fcw0", 3 * NF), ("fcw1", 3 * NF), ("fcb0", NF), ("fcb1", NF),
    ("m_norm", 8), ("m_cw", 4 * 32), ("m_cb", 32), ("m_d", 16), ("m_gn", 16), ("m_dtb", 32), ("m_al", 32),
    ("kv2_norm", 8), ("b2_norm", 8), ("sub_g", 1), ("fin", 8), ("lam", 256),
    ("lre", G5), ("lim", G5), ("ldt", G5),
]
PCOL = {}
_n = 0
for _name, _w in PARAMS:
    PCOL[_name] = (_n, _w)
    _n += _w
NPAR = _n

CONSTS = [("ones", 128), ("bd64", 128), ("ident", 128), ("ntri", 128), ("nones", 128), ("upper", 128),
          ("slower", 128), ("nupper", 128), ("low", 128), ("alibi", 512)]
CCOL = {}
_n = 0
for _name, _w in CONSTS:
    CCOL[_name] = (_n, _w)
    _n += _w
NCON = _n


def constants():
    p = np.arange(P)[:, None]
    c = np.arange(P)[None, :]
    out = {
        "ones": np.ones((P, P)), "bd64": (p // 64 == c // 64), "ident": (p == c),
        "ntri": -1.0 * (p >= c), "nones": -np.ones((P, P)), "upper": (p <= c),
        "slower": (p > c), "nupper": -1.0 * (p <= c), "low": np.where(p > c, -1e30, 0.0),
    }
    k = np.arange(512)[None, :] - 384
    dist = -np.abs(p - k).astype(np.float64)
    blocked = np.floor_divide(k, 64) > (p // 64)
    out["alibi"] = np.where(blocked, -1e30, dist)
    return np.concatenate([out[n].astype(np.float32) for n, _ in CONSTS], axis=1)


class Tok:

    def __init__(self, sem):
        self.sem = sem
        self.val = None


class Queues:

    ENG = ("pe", "act", "dve", "pool", "sp")

    def __init__(self, nc, ctx):
        self.nc = nc
        self.q = {e: [] for e in self.ENG}
        self.sem = {e: ctx.enter_context(nc.semaphore(f"done_{e}")) for e in self.ENG if e != "sp"}
        self.ctx = ctx
        self.last = {}
        self.names = 0
        self.dma = {}

    def put(self, eng, fn, waits, inc=True, where=None, table=None):
        tok = Tok(eng) if inc else None
        (self.q[eng] if where is None else where).append((fn, [w for w in waits if w is not None], tok, table))
        if inc:
            self.last[eng] = tok
        return tok

    def dma_sem(self, name):
        self.dma[name] = [self.ctx.enter_context(self.nc.semaphore(name)), 0]
        return name

    def put_dma(self, eng, fn, name, waits, where=None):
        self.dma[name][1] += 16
        tok = Tok(name)
        tok.val = self.dma[name][1]
        (self.q[eng] if where is None else where).append((fn, [w for w in waits if w is not None], name, None))
        return tok

    def marker(self, eng):
        m = []
        self.q[eng].append(m)
        return m

    def flat(self, eng):
        for item in self.q[eng]:
            if isinstance(item, list):
                yield from item
            else:
                yield item

    def number(self):
        for eng in self.ENG:
            n = 0
            for _, _, tok, _ in self.flat(eng):
                if isinstance(tok, Tok):
                    n += 1
                    tok.val = n

    def play(self, eng, e):
        seen = {}
        loaded = None
        for fn, waits, tok, table in self.flat(eng):
            if table is not None and table != loaded:
                loaded = table
                if table == "log_exp":
                    e.preload_act_table_set("natural_log_exp_and_others")
            need = {}
            for w in waits:
                need[w.sem] = max(need.get(w.sem, 0), w.val)
            for s, v in need.items():
                if seen.get(s, 0) < v:
                    seen[s] = v
                    e.wait_ge(self.sem[s] if s in self.sem else self.dma[s][0], v)
            ins = fn(e)
            if isinstance(tok, Tok):
                ins.then_inc(self.sem[eng], 1)
            elif tok is not None:
                ins.then_inc(self.dma[tok][0], 16)


class Slots:

    def __init__(self, bufs):
        self.bufs = bufs
        self.free = [[] for _ in bufs]
        self.n = 0

    def take(self):
        i = self.n % len(self.bufs)
        assert self.n < len(self.bufs) or self.free[i], "taken again before its release was queued"
        self.n += 1
        waits = self.free[i]
        self.free[i] = []
        return self.bufs[i], waits, self.free[i]


def parted(slots, *sizes):
    out, a = [], 0
    for n in sizes:
        r = Slots(slots.bufs[a:a + n])
        r.free = slots.free[a:a + n]
        out.append(r)
        a += n
    return out


def rejoin(slots, *parts):
    slots.free = [f for r in parts for f in r.free]
    slots.n = len(slots.bufs) if all(slots.free) else 0


def interleave(*gens):
    gens = list(gens)
    while gens:
        for g in list(gens):
            if next(g, "end") == "end":
                gens.remove(g)


def build_program(nc, d, stages=STAGES):
    ctx = ExitStack()
    units = []
    with ctx:
        Q = Queues(nc, ctx)

        def V(fn, *w):
            return Q.put("dve", fn, w)

        def A(fn, *w, table=None):
            return Q.put("act", fn, w, table=table)

        def G(fn, *w):
            return Q.put("pool", fn, w)

        def PE(fn, *w, inc=False):
            return Q.put("pe", fn, w, inc=inc)

        def sb(c, name, shape, dt=F32):
            return c.enter_context(nc.sbuf_tensor(name, shape, dt))

        par = sb(ctx, "par", [P, NPAR])
        con = sb(ctx, "con", [P, NCON])
        h = sb(ctx, "h", [P, 8, T])
        xh = sb(ctx, "xh", [P, 8, T], R32)
        xl = sb(ctx, "xl", [P, 8, T], R32)
        RAW, NH, LA = 5, 4, 2
        raw = [sb(ctx, f"raw{i}", [P, 1024]) for i in range(RAW)]
        wh = [sb(ctx, f"wh{i}", [P, 1024], R32) for i in range(NH)]
        wl = [sb(ctx, f"wl{i}", [P, 1024], R32) for i in range(NH)]
        tmp = Slots([sb(ctx, f"tmp{i}", [P, T]) for i in range(5)])
        bank = Slots([ctx.enter_context(nc.psum_tensor(f"bank{i}", [P, T], F32)) for i in range(8)])

        def pc(name, i=0, n=1, rows=P):
            o = PCOL[name][0]
            return par[0:rows, o + i:o + i + n]

        def cc(name):
            o, n = CCOL[name]
            return con[:, o:o + n]

        Q.dma_sem("ld")
        Q.dma_sem("ldx")
        ld = Q.put_dma("sp", lambda e: e.dma_start(par[:, :], d["par"]), "ld", [])
        ld = Q.put_dma("sp", lambda e: e.dma_start(con[:, :], d["con"]), "ld", [])

        for i in range(RAW):
            Q.dma_sem(f"raw{i}")
        marks = []
        raw_free = {}
        w_free = {}

        def weights(key, cols):
            n = len(units)
            units.append((key, cols))
            off = sum(c for _, c in units[:-1]) * P
            ri, wi = n % RAW, n % NH
            marks.append((Q.marker("act"), Q.marker("dve")))
            ma, md = marks[max(0, n - LA)]
            src = d["w"][off:off + P * cols].rearrange("(p c) -> p c", p=P)
            got = Q.put_dma("sp", lambda e: e.dma_start(raw[ri][:, 0:cols], src), f"raw{ri}",
                            raw_free.get(n - RAW, []))
            free = w_free.get(n - NH, [])
            last = Q.last.get("act"), Q.last.get("dve")
            hi = Q.put("act", lambda e: e.activation(wh[wi][:, 0:cols], raw[ri][:, 0:cols], ACT.Copy),
                       [got, *free], where=ma)
            lo = Q.put("dve", lambda e: e.tensor_tensor(wl[wi][:, 0:cols], raw[ri][:, 0:cols],
                                                        wh[wi][:, 0:cols].bitcast(F32), ALU.subtract),
                       [hi, *free], where=md)
            Q.last["act"], Q.last["dve"] = last
            raw_free[n] = [hi, lo]
            w_free[n] = []
            return wh[wi], wl[wi], hi, lo, w_free[n]

        def pieces(kts):
            return [(0, kts)] if kts <= 8 else [(0, (kts + 1) // 2), ((kts + 1) // 2, kts)]

        def group(name, m, kts, x, k0=0, ring=None):
            b, bw, bf = (ring or bank).take()
            n = 0
            total = 3 * kts
            for a, z in pieces(kts):
                WH, WL, th, tl, wf = weights((name, "T", m, k0 + a, k0 + z), (z - a) * P)
                for k in range(a, z):
                    o = (k - a) * P
                    XH, XL, tx = x(k)
                    for W, X, tw in ((WH, XH, th), (WH, XL, th), (WL, XH, tl)):
                        last = n == total - 1
                        t = PE(lambda e, W=W, X=X, o=o, n=n, b=b: e.matmul(
                            b[:, :], W[:, o:o + P], X, start=(n == 0), stop=(n == total - 1)),
                            tw, *tx, *(bw if n == 0 else []), inc=last or (k == z - 1 and W is WL))
                        n += 1
                wf.append(t)
            return b, t, bf

        def xin(tx):
            return lambda k: (xh[:, k, :], xl[:, k, :], tx[k])

        def split(k, src, waits, xw, hi=None, lo=None):
            H = xh[:, k, :] if hi is None else hi
            L = xl[:, k, :] if lo is None else lo
            a = A(lambda e: e.activation(H, src, ACT.Copy), *waits, *xw)
            v = V(lambda e: e.tensor_tensor(L, src, H.bitcast(F32), ALU.subtract), a, *xw)
            return [a, v]

        xrel = [[] for _ in range(8)]

        def xuse(t):
            for k in range(8):
                xrel[k][:] = [t]

        def rsqrt(b, tb, bf, n, eps):
            v, w1, f1 = tmp.take()
            y, w2, f2 = tmp.take()
            t1 = V(lambda e: e.tensor_scalar(v[:, :], b[:, :], 1.0 / n, eps, ALU.mult, ALU.add), tb, *w1)
            bf.append(t1)
            t2 = A(lambda e: e.activation(y[:, :], v[:, :], ACT.Ln), t1, *w2, table="log_exp")
            t3 = A(lambda e: e.activation(y[:, :], y[:, :], ACT.Exp, scale=-0.5), t2, table="log_exp")
            s, w3, f3 = tmp.take()
            t4 = V(lambda e: e.scalar_tensor_tensor(out=s[:, :], in0=y[:, :], scalar=-0.5, in1=y[:, :],
                                                    op0=ALU.mult, op1=ALU.mult), t3, *w3)
            t5 = V(lambda e: e.tensor_tensor(s[:, :], s[:, :], v[:, :], ALU.mult), t4)
            f1.append(t5)
            t6 = V(lambda e: e.scalar_tensor_tensor(out=y[:, :], in0=s[:, :], scalar=1.5, in1=y[:, :],
                                                    op0=ALU.add, op1=ALU.mult), t5)
            f3.append(t6)
            return y, t6, f2

        def square_sum(srcs, lhs, ring=None):
            b, bw, bf = (ring or bank).take()
            for i, (src, ts) in enumerate(srcs):
                q, w, f = tmp.take()
                ta = A(lambda e, q=q, src=src: e.activation(q[:, :], src, ACT.Square), *ts, *w)
                t = PE(lambda e, q=q, i=i: e.matmul(b[:, :], lhs, q[:, :], start=(i == 0),
                                                    stop=(i == len(srcs) - 1)),
                       ta, ld, *(bw if i == 0 else []), inc=True)
                f.append(t)
            return b, t, bf

        rs_keep = sb(ctx, "rs_keep", [P, T])
        rs_free = []

        def rms(eps, th, src=None):
            src = h if src is None else src
            b, t, bf = square_sum([(src[:, k, :], th[k]) for k in range(8)], cc("ones"))
            y, ty, yf = rsqrt(b, t, bf, D, eps)
            t = V(lambda e: e.tensor_copy(rs_keep[:, :], y[:, :]), ty, *rs_free)
            rs_free.clear()
            yf.append(t)
            return t

        def normed(trs, gname, src=None, out=None):
            src = h if src is None else src
            tx = []
            for k in range(8):
                s, w, f = tmp.take()
                t = V(lambda e, k=k, s=s: e.scalar_tensor_tensor(
                    out=s[:, :], in0=src[:, k, :], scalar=pc(gname, k), in1=rs_keep[:, :],
                    op0=ALU.mult, op1=ALU.mult), trs, *w)
                rs_free.append(t)
                if out is None:
                    ts = split(k, s[:, :], [t], xrel[k])
                    f.extend(ts)
                    tx.append(ts)
                else:
                    out(k, s, t, f)
            return tx

        def add_h(m, b, t, bf, th):
            t2 = V(lambda e: e.tensor_tensor(h[:, m, :], h[:, m, :], b[:, :], ALU.add), t, *th[m])
            bf.append(t2)
            return [t2]

        def barrier():
            return [Q.last[e] for e in ("pe", "act", "dve", "pool") if e in Q.last]

        def s5(th_in):
            c5 = ExitStack()
            with c5:
                NC = 64
                xp = h
                U = sb(c5, "U", [P, G5, NC])
                t0 = barrier()
                ldx = Q.put_dma("sp", lambda e: e.dma_start(xp[:, :, :], d["xp"]), "ldx", [])
                w = G5
                sm = sb(c5, "s5small", [P, 24, w])
                pw = sb(c5, "pw", [P, 2, w, 9])
                cb_ = sb(c5, "coefb", [P, 2, w, 8])
                kk = sb(c5, "kk", [P, 2, NQ, 9])
                S = lambda i: sm[:, i, :]
                st = {}
                last = [ld]

                def v(fn, *ws):
                    last[0] = V(fn, last[0], *ws)
                    return last[0]

                def a(fn, *ws, table=None):
                    last[0] = A(fn, last[0], *ws, table=table)
                    return last[0]

                def tt(o, x, y, op):
                    return v(lambda e: e.tensor_tensor(o, x, y, op))

                def cmul(o, x, y, t1, t2):
                    tt(o[0], x[0], y[0], ALU.mult)
                    tt(t1, x[1], y[1], ALU.mult)
                    tt(o[1], x[0], y[1], ALU.mult)
                    tt(t2, x[1], y[0], ALU.mult)
                    tt(o[0], o[0], t1, ALU.subtract)
                    tt(o[1], o[1], t2, ALU.add)

                MAGIC = 12582912.0
                TP = 2.0 * math.pi
                TP1 = 6.28125
                TP2 = float(np.float32(TP - TP1))
                TP3 = TP - TP1 - TP2

                def reduced_sin(o, x, shift):
                    k = S(10)
                    v(lambda e: e.tensor_scalar(k, x, 1.0 / TP, shift / TP, ALU.mult, ALU.add))
                    v(lambda e: e.tensor_scalar(k, k, MAGIC, None, ALU.add))
                    v(lambda e: e.tensor_scalar(k, k, -MAGIC, None, ALU.add))
                    v(lambda e: e.scalar_tensor_tensor(out=o, in0=k, scalar=-TP1, in1=x,
                                                       op0=ALU.mult, op1=ALU.add))
                    v(lambda e: e.scalar_tensor_tensor(out=o, in0=k, scalar=-TP2, in1=o,
                                                       op0=ALU.mult, op1=ALU.add))
                    v(lambda e: e.scalar_tensor_tensor(out=o, in0=k, scalar=-TP3, in1=o,
                                                       op0=ALU.mult, op1=ALU.add))
                    if shift:
                        v(lambda e: e.tensor_scalar(o, o, shift, None, ALU.add))
                    v(lambda e: e.tensor_scalar(o, o, 3.1415925, -3.1415925, ALU.min, ALU.max))
                    a(lambda e: e.activation(o, o, ACT.Sin), table="sin")

                def prep():
                    lre, lim, ldt = pc("lre", 0, w), pc("lim", 0, w), pc("ldt", 0, w)
                    last[0] = A(lambda e: e.activation(S(0), ldt, ACT.Exp), ld, *t0, table="log_exp")
                    tt(S(1), lre, S(0), ALU.mult)
                    tt(S(2), lim, S(0), ALU.mult)
                    a(lambda e: e.activation(S(3), S(1), ACT.Exp), table="log_exp")
                    a(lambda e: e.activation(S(6), S(1), ACT.Exp, scale=8.0), table="log_exp")
                    reduced_sin(S(4), S(2), 0.0)
                    reduced_sin(S(5), S(2), math.pi / 2)
                    yield
                    v(lambda e: e.memset(pw[:, 0, :, 0], 1.0))
                    v(lambda e: e.memset(pw[:, 1, :, 0], 0.0))
                    tt(pw[:, 0, :, 1], S(3), S(5), ALU.mult)
                    tt(pw[:, 1, :, 1], S(3), S(4), ALU.mult)
                    for k in (1, 2, 4):
                        def view(z, i, n):
                            return pw[:, z, :, i:i + n]
                        def bc(z, i, n):
                            return pw[:, z, :, i:i + 1].broadcast_to([P, w, n])
                        t1 = cb_[:, 0, :, 0:k]
                        t2 = cb_[:, 1, :, 0:k]
                        cmul((view(0, k + 1, k), view(1, k + 1, k)), (view(0, 1, k), view(1, 1, k)),
                             (bc(0, k, k), bc(1, k, k)), t1, t2)
                    yield
                    tt(S(7), lre, lre, ALU.mult)
                    tt(S(8), lim, lim, ALU.mult)
                    tt(S(7), S(7), S(8), ALU.add)
                    v(lambda e: e.reciprocal(S(7), S(7)))
                    v(lambda e: e.tensor_scalar(S(8), pw[:, 0, :, 1], -1.0, None, ALU.add))
                    tt(S(11), S(8), lre, ALU.mult)
                    tt(S(12), pw[:, 1, :, 1], lim, ALU.mult)
                    tt(S(11), S(11), S(12), ALU.add)
                    tt(S(12), pw[:, 1, :, 1], lre, ALU.mult)
                    tt(S(13), S(8), lim, ALU.mult)
                    tt(S(12), S(12), S(13), ALU.subtract)
                    tt(S(11), S(11), S(7), ALU.mult)
                    tt(S(12), S(12), S(7), ALU.mult)
                    c_, s_ = 5, 4
                    for j in range(3):
                        co, so = (16, 17) if j % 2 else (14, 15)
                        tt(S(co), S(c_), S(c_), ALU.mult)
                        tt(S(18), S(s_), S(s_), ALU.mult)
                        tt(S(19), S(c_), S(s_), ALU.mult)
                        tt(S(co), S(co), S(18), ALU.subtract)
                        v(lambda e, so=so: e.tensor_scalar(S(so), S(19), 2.0, None, ALU.mult))
                        c_, s_ = co, so
                    yield
                    tmpc = U[:, 0:8, :].rearrange("p a b -> p (a b)").rearrange("p (a b) -> p a b", b=8)
                    tmpd = U[:, 8:16, :].rearrange("p a b -> p (a b)").rearrange("p (a b) -> p a b", b=8)

                    def b8(i):
                        return S(i).unsqueeze(2).broadcast_to([P, w, 8])
                    cmul((cb_[:, 0], cb_[:, 1]), (pw[:, 0, :, 0:8], pw[:, 1, :, 0:8]), (b8(11), b8(12)),
                         tmpc, tmpd)
                    st["prep"] = last[0]
                    yield

                def dense_u():
                    trs = rms(1e-6, [[ldx]] * 8, xp)
                    tx = normed(trs, "a_norm", xp)
                    tw = []
                    for m in range(8):
                        b, t, bf = group("a_w_in", m, 8, xin(tx))
                        s, sw, sf = ubuf.take()
                        t2 = A(lambda e, b=b, s=s: e.activation(s, b[:, :], ACT.Copy), t, *sw)
                        bf.append(t2)
                        st[("u", m)] = t2
                        tw.append(Q.put_dma("pool", lambda e, m=m, s=s: e.dma_start(
                            d["ud"][m * P:(m + 1) * P, :], s), f"ud{m % 2}", [t2]))
                        sf.append(tw[-1])
                        yield
                    xuse(t)
                    st["ud"] = tw[-2:]

                Q.dma_sem("ud0")
                Q.dma_sem("ud1")
                ustage = [sb(c5, f"ustage{i}", [P, T]) for i in range(2)]
                ubuf = Slots([u[:, :] for u in ustage])
                interleave(dense_u(), prep())

                Q.dma_sem("uload")
                for s in range(8):
                    src = d["ud"].rearrange("(g h) (s c) -> s h g c", h=16, s=8)
                    tu = Q.put_dma("pool", lambda e, s=s, src=src: e.dma_start(
                        U[s * 16:(s + 1) * 16, :, :], src[7 - s]), "uload", [*st["ud"], st["prep"]])

                W = NQ
                Bp = sb(c5, "Bp", [P, W, P])
                BT1 = sb(c5, "BT1", [P, W, P])
                CA = sb(c5, "CA", [P, W, 9 * 16])
                CBm = sb(c5, "CBm", [P, W, P])
                Mt = sb(c5, "Mt", [P, W, P])
                bc_in = sb(c5, "bcin", [P, 4, W, 16])
                rot = sb(c5, "rot", [P, 2, W, NC])
                big = [sb(c5, f"big{i}", [P, W, NC]) for i in range(3)]
                BT2 = CBm
                for n in ("bc5", "kd", "kdz", "mt", "yd", "yload", "ur0", "ur1"):
                    Q.dma_sem(n)
                z = V(lambda e: e.memset(BT1[0:16, :, 0:112], 0.0), *barrier())
                tz = []
                for q in range(G5 // W):
                    tz = [Q.put_dma("pool", lambda e, q=q: e.dma_start(
                        d["kd"][:, q * W:(q + 1) * W, 0:112], BT1[0:16, :, 0:112]), "kdz", [z])]
                prev = [*barrier(), *tz]
                for q in range(G5 // W):
                    gs = slice(q * W, (q + 1) * W)
                    tb = Q.put_dma("pool", lambda e, gs=gs: e.dma_start(bc_in[:, :, :, :], d["bc5"][:, :, gs, :]),
                                   "bc5", prev)

                    def stack(dst, top, bot, tw):
                        v(lambda e: e.tensor_scalar(dst[0:64], top[0][0:64], top[1], None, ALU.mult), *tw)
                        v(lambda e: e.tensor_scalar(dst[64:128], bot[0][64:128], bot[1], None, ALU.mult))

                    def combine(out, n, K1, K2, i1, i2, scratch):
                        sh = [P, W, n, 16]
                        v(lambda e: e.tensor_tensor(out, K1.unsqueeze(3).broadcast_to(sh),
                                                    bc_in[:, i1].unsqueeze(2).broadcast_to(sh), ALU.mult), tb)
                        v(lambda e: e.tensor_tensor(scratch, K2.unsqueeze(3).broadcast_to(sh),
                                                    bc_in[:, i2].unsqueeze(2).broadcast_to(sh), ALU.mult))
                        v(lambda e: e.tensor_tensor(out, out, scratch, ALU.add))

                    def hv(t, n, o=0):
                        return t[:, :, o * 16:(o + n) * 16].rearrange("p g (k h) -> p g k h", h=16)

                    K = kk
                    cr, ci = cb_[:, 0, gs, :], cb_[:, 1, gs, :]
                    stack(K[:, 0, :, 0:8], (cr, 1.0), (ci, 1.0), prev)
                    stack(K[:, 1, :, 0:8], (ci, -1.0), (cr, 1.0), [])
                    Kr = [K[:, i, :, 0:8] for i in range(2)]
                    combine(hv(Bp, 8), 8, Kr[0], Kr[1], 0, 1, hv(Mt, 8))
                    ar, ai = pw[:, 0, gs, :], pw[:, 1, gs, :]
                    stack(K[:, 0, :, :], (ar, 1.0), (ai, -1.0), [])
                    stack(K[:, 1, :, :], (ai, -1.0), (ar, -1.0), [])
                    combine(hv(CA, 8), 8, K[:, 0, :, 0:8], K[:, 1, :, 0:8], 2, 3, hv(Mt, 8))
                    combine(hv(CA, 1, 8), 1, K[:, 0, :, 8:9], K[:, 1, :, 8:9], 2, 3, hv(Mt, 1))
                    tCA = last[0]

                    ks = BT1[0:16, :, :]
                    for j in range(W // 4):
                        b, bw, bf = bank.take()
                        for i in range(4):
                            g = 4 * j + i
                            t = PE(lambda e, g=g, i=i, b=b: e.matmul(
                                b[0:16, i * P:(i + 1) * P], Bp[:, g, 0:16], CA[:, g, 0:P],
                                start=(i == 0), stop=True, skip_group_check=True),
                                tCA, *(bw if i == 0 else []), inc=(i == 3))
                        t2 = A(lambda e, j=j, b=b: e.activation(
                            ks[:, 4 * j:4 * j + 4, :], b[0:16, :].rearrange("p (g c) -> p g c", g=4), ACT.Copy),
                            t, *prev)
                        bf.append(t2)
                    tk = Q.put_dma("pool", lambda e, gs=gs: e.dma_start(d["kd"][:, gs, 112:240], ks), "kd", [t2])
                    for s in range(8):
                        tm = Q.put_dma("pool", lambda e, s=s, gs=gs: e.dma_start(
                            Mt[s * 16:(s + 1) * 16, :, :],
                            d["kd"][:, gs, s * 16:s * 16 + P]), "mt", [tk, tCA, *tz])

                    tt_ = []
                    for j in range(W // 4):
                        b, bw, bf = bank.take()
                        for i in range(4):
                            g = 4 * j + i
                            t = PE(lambda e, g=g, i=i, b=b: e.transpose(
                                b[:, i * P:(i + 1) * P], Bp[:, g, :], cc("ident")),
                                tCA, *(bw if i == 0 else []), inc=(i == 3))
                        bv = b[:, :].rearrange("p (g r c) -> p g r c", g=4, r=2)
                        o1 = BT1[:, 4 * j:4 * j + 4, :]
                        o2 = BT2[:, 4 * j:4 * j + 4, :].rearrange("p g (r c) -> p g r c", r=2)
                        A(lambda e, o1=o1, b=b: e.activation(
                            o1, b[:, :].rearrange("p (g c) -> p g c", g=4), ACT.Copy), t, tk)
                        A(lambda e, o2=o2, bv=bv: e.activation(o2[:, :, 0, :], bv[:, :, 1, :], ACT.Copy), t)
                        t2 = A(lambda e, o2=o2, bv=bv: e.activation(o2[:, :, 1, :], bv[:, :, 0, :], ACT.Copy,
                                                                    scale=-1.0), t)
                        bf.append(t2)
                        tt_.append(t2)

                    ro = [rot[:, 0], rot[:, 1]]
                    v(lambda e: e.memset(ro[0][:, :, 0:1], 1.0), *prev)
                    v(lambda e: e.memset(ro[1][:, :, 0:1], 0.0))
                    v(lambda e, gs=gs: e.tensor_copy(ro[0][:, :, 1:2], S(14)[:, gs].unsqueeze(2)))
                    v(lambda e, gs=gs: e.tensor_copy(ro[1][:, :, 1:2], S(15)[:, gs].unsqueeze(2)))
                    e0 = (sm[:, 20, 0:W].unsqueeze(2), sm[:, 21, 0:W].unsqueeze(2))
                    s1, s2 = sm[:, 22, 0:W].unsqueeze(2), sm[:, 23, 0:W].unsqueeze(2)
                    for lg in range(1, 6):
                        n = 1 << lg
                        hf = (ro[0][:, :, n // 2:n // 2 + 1], ro[1][:, :, n // 2:n // 2 + 1])
                        cmul(e0, hf, hf, s1, s2)
                        be = (e0[0].broadcast_to([P, W, n]), e0[1].broadcast_to([P, W, n]))
                        cmul((ro[0][:, :, n:2 * n], ro[1][:, :, n:2 * n]),
                             (ro[0][:, :, 0:n], ro[1][:, :, 0:n]), be, big[0][:, :, 0:n], big[1][:, :, 0:n])

                    vr = big[0]
                    for j in range(W // 8):
                        b1, w1, f1 = bank.take()
                        b2, w2, f2 = bank.take()
                        for b, bw, BT in ((b1, w1, BT1), (b2, w2, BT2)):
                            for i in range(8):
                                g = 8 * j + i
                                t = PE(lambda e, g=g, i=i, b=b, BT=BT, q=q: e.matmul(
                                    b[:, i * NC:(i + 1) * NC], BT[:, g, :], U[:, q * W + g, :],
                                    start=(i == 0), stop=True, skip_group_check=True),
                                    tt_[g // 4], tu, *(bw if i == 0 else []), inc=(i == 7))
                        js = slice(8 * j, 8 * j + 8)
                        bv1 = b1[:, :].rearrange("p (g c) -> p g c", g=8)
                        bv2 = b2[:, :].rearrange("p (g c) -> p g c", g=8)
                        f1.append(v(lambda e, js=js, bv1=bv1: e.tensor_tensor(vr[:, js, :], bv1, ro[0][:, js, :],
                                                                              ALU.mult), t))
                        f2.append(v(lambda e, js=js, bv2=bv2: e.tensor_tensor(big[1][:, js, :], bv2,
                                                                              ro[1][:, js, :], ALU.mult)))
                        tBT = t
                    tt(vr[:, :, :], vr[:, :, :], big[1][:, :, :], ALU.add)
                    rho = big[1]
                    v(lambda e, gs=gs: e.tensor_copy(rho[:, :, :], S(6)[:, gs].unsqueeze(2).broadcast_to([P, W, NC])))
                    v(lambda e: e.memset(rho[:, :, 0:1], 0.0))
                    fl = lambda x: x[:, :, :].rearrange("p g c -> p (g c)")
                    v(lambda e: e.tensor_tensor_scan(fl(big[2]), fl(rho), fl(vr), 0.0, ALU.mult, ALU.add))
                    G1, G2 = big[0], big[1]
                    for GG, r in ((G1, ro[0]), (G2, ro[1])):
                        v(lambda e, GG=GG: e.memset(GG[:, :, 0:1], 0.0))
                        v(lambda e, GG=GG, r=r: e.tensor_tensor(GG[:, :, 1:NC], big[2][:, :, 0:NC - 1],
                                                                r[:, :, 0:NC - 1], ALU.mult))
                    stack(K[:, 0, :, :], (ai, -1.0), (ar, -1.0), [])
                    stack(K[:, 1, :, :], (ar, -1.0), (ai, 1.0), [])
                    combine(hv(CBm, 8), 8, K[:, 0, :, 1:9], K[:, 1, :, 1:9], 2, 3, hv(Bp, 8))
                    tG = last[0]
                    Y = BT1[:, :, 0:NC]
                    for j in range(W // 8):
                        b, bw, bf = bank.take()
                        for i in range(8):
                            g = 8 * j + i
                            for n, (L, Rr) in enumerate(((Mt[:, g, :], U[:, q * W + g, :]),
                                                         (CA[:, g, 16:144], G1[:, g, :]),
                                                         (CBm[:, g, :], G2[:, g, :]))):
                                t = PE(lambda e, i=i, b=b, L=L, Rr=Rr, n=n: e.matmul(
                                    b[:, i * NC:(i + 1) * NC], L, Rr, start=(i == 0 and n == 0), stop=(n == 2),
                                    skip_group_check=True),
                                    tG, tm, *(bw if i == 0 and n == 0 else []), inc=(i == 7 and n == 2))
                        t2 = A(lambda e, j=j, b=b: e.activation(
                            Y[:, 8 * j:8 * j + 8, :], b[:, :].rearrange("p (g c) -> p g c", g=8), ACT.Copy),
                            t, tBT)
                        bf.append(t2)
                    yv = d["yd"].rearrange("(g h) (t c) -> t h g c", h=16, t=8)
                    for s in range(8):
                        tY = Q.put_dma("pool", lambda e, s=s, gs=gs, yv=yv: e.dma_start(
                            yv[s][:, gs, :], Y[s * 16:(s + 1) * 16, :, :]), "yd", [t2])
                    prev = [*barrier(), tY]
                for m in range(8):
                    dst = U[:, 8 * m:8 * m + 8, :].rearrange("p g c -> p (g c)")
                    tl = Q.put_dma("pool", lambda e, m=m, dst=dst: e.dma_start(
                        dst, d["yd"][m * P:(m + 1) * P, :]), "yload", prev)
                tx = []
                for m in range(8):
                    yv_ = U[:, 8 * m:8 * m + 8, :].rearrange("p g c -> p (g c)")
                    us, uw, uf = ubuf.take()
                    tu_ = Q.put_dma("pool", lambda e, m=m, us=us: e.dma_start(
                        us, d["ud"][m * P:(m + 1) * P, :]), f"ur{m % 2}", uw)
                    t = V(lambda e, m=m, yv_=yv_, us=us: e.scalar_tensor_tensor(
                        out=yv_, in0=us, scalar=pc("a_d", m), in1=yv_, op0=ALU.mult, op1=ALU.add),
                        tl, tu_)
                    uf.append(t)
                    t = A(lambda e, yv_=yv_: e.activation(yv_, yv_, ACT.Gelu_apprx_tanh), t, table="gelu")
                    tx.append(split(m, yv_, [t], xrel[m]))
                th = []
                for m in range(8):
                    bv_, tv, fv = group("a_w_glu", m, 8, xin(tx))
                    bg, tg, fg = group("a_w_glu", 8 + m, 8, xin(tx))
                    s, sw, sf = tmp.take()
                    ta = A(lambda e, s=s, bg=bg: e.activation(s[:, :], bg[:, :], ACT.Sigmoid), tg, *sw, table="sigmoid")
                    fg.append(ta)
                    t1 = V(lambda e, s=s, bv_=bv_: e.tensor_tensor(s[:, :], s[:, :], bv_[:, :], ALU.mult), ta, tv)
                    fv.append(t1)
                    t1 = V(lambda e, s=s, m=m: e.tensor_tensor(s[:, :], s[:, :], xp[:, m, :], ALU.add), t1, ldx)
                    t2 = V(lambda e, s=s, m=m: e.tensor_copy(
                        h[:, m, :].rearrange("p (c s) -> p s c", s=8),
                        s[:, :].rearrange("p (s c) -> p s c", s=8)), t1)
                    sf.append(t2)
                    th.append([t2])
                xuse(tg)
                return th

        def ffn(layer, th):
            cf = ExitStack()
            with cf:
                hi = sb(cf, f"fh{layer}", [P, 13, T], R32)
                lo = sb(cf, f"fl{layer}", [P, 13, T], R32)
                gts = [sb(cf, f"fg{layer}_{i}", [P, T]) for i in range(3)]
                t0 = barrier()
                act = Slots([(hi[:, i, :], lo[:, i, :]) for i in range(13)])
                gt = Slots(gts)
                for f in act.free:
                    f.extend(t0)
                for f in gt.free:
                    f.extend(t0)
                tx = normed(rms(1e-6, th), f"ffn_norm{layer}")
                cw, cbn = f"fcw{layer}", f"fcb{layer}"

                for half in range(2):
                    xa = []
                    for f in range(half * HALF, (half + 1) * HALF):
                        bg, tg, fg = group(f"up{layer}", NF + f, 8, xin(tx))
                        raw_, w1, f1 = gt.take()
                        t1 = A(lambda e, r=raw_, b=bg: e.activation(r[:, :], b[:, :], ACT.Copy), tg, *w1)
                        fg.append(t1)
                        bv_, tv, fv = group(f"up{layer}", f, 8, xin(tx))
                        g, w2, f2 = tmp.take()
                        t2 = V(lambda e, g=g, r=raw_, f=f: e.tensor_scalar(
                            g[:, :], r[:, :], pc(cw, 2 * NF + f), pc(cbn, f), ALU.mult, ALU.add), t1, ld, *w2)
                        t3 = V(lambda e, g=g, r=raw_, f=f: e.scalar_tensor_tensor(
                            out=g[:, 1:T], in0=r[:, 0:T - 1], scalar=pc(cw, NF + f), in1=g[:, 1:T],
                            op0=ALU.mult, op1=ALU.add), t2)
                        t4 = V(lambda e, g=g, r=raw_, f=f: e.scalar_tensor_tensor(
                            out=g[:, 2:T], in0=r[:, 0:T - 2], scalar=pc(cw, f), in1=g[:, 2:T],
                            op0=ALU.mult, op1=ALU.add), t3)
                        f1.append(t4)
                        t5 = A(lambda e, g=g: e.activation(g[:, :], g[:, :], ACT.Silu), t4, table="silu")
                        t6 = V(lambda e, g=g, b=bv_: e.tensor_tensor(g[:, :], g[:, :], b[:, :], ALU.mult), t5, tv)
                        fv.append(t6)
                        (H, L), w3, f3 = act.take()
                        ts = split(0, g[:, :], [t6], w3, H, L)
                        f2.extend(ts)
                        xa.append((H, L, ts, f3))
                    for m in range(8):
                        b, t, bf = group(f"down{layer}", m, HALF, lambda k: xa[k][:3], k0=half * HALF)
                        th[m] = add_h(m, b, t, bf, th)
                    for x in xa:
                        x[3].append(t)
                xuse(t)
                return th

        def values(name, c0, tx, Vt, tv_w):
            out = []
            for half in range(2):
                bs = [bank.take() for _ in range(4)]
                for u in range(4):
                    WH, WL, t1, t2, wf = weights((name, "N", c0 + half * 512, 2 * u, 2 * u + 2), 1024)
                    for kk_ in range(2):
                        k = 2 * u + kk_
                        for tt_ in range(4):
                            b, bw, bf = bs[tt_]
                            for n, (X, W) in enumerate(((xh, WH), (xl, WH), (xh, WL))):
                                last = k == 7 and n == 2
                                t = PE(lambda e, b=b, X=X, W=W, k=k, kk_=kk_, tt_=tt_, n=n: e.matmul(
                                    b[:, :], X[:, k, tt_ * P:(tt_ + 1) * P], W[:, kk_ * 512:(kk_ + 1) * 512],
                                    start=(k == 0 and n == 0), stop=(k == 7 and n == 2)),
                                    t1, t2, *tx[k], *(bw if k == 0 and n == 0 else []),
                                    inc=last or (kk_ == 1 and tt_ == 3 and n == 2))
                            if last:
                                bs[tt_] = (b, t, bf)
                    wf.append(t)
                for tt_ in range(4):
                    b, t, bf = bs[tt_]
                    t2 = A(lambda e, b=b, tt_=tt_, half=half: e.activation(
                        Vt[:, tt_, half * 512:(half + 1) * 512], b[:, :], ACT.Copy), t, *tv_w)
                    bf.append(t2)
                    out.append(t2)
            return out, t

        def att1(th):
            ca = ExitStack()
            with ca:
                kT = sb(ca, "kT", [P, 8, T])
                qT = sb(ca, "qT", [P, 8, T])
                Vt = sb(ca, "Vt", [P, 4, D])
                spb = [sb(ca, f"sp{i}", [P, 1280]) for i in range(2)]
                wwb = [sb(ca, f"ww{i}", [P, 1280]) for i in range(2)]
                idb = sb(ca, "idb", [P, P], BF16)
                mkb = sb(ca, "mkb", [P, P], BF16)
                t0 = barrier()
                V(lambda e: e.tensor_copy(idb[:, :], cc("ident")), ld, *t0)
                tmk = V(lambda e: e.tensor_scalar(mkb[:, :], cc("ntri"), 1e30, None, ALU.mult), ld)

                def head_norm(dst, m, b, t, bf, gname, scale):
                    t1 = A(lambda e: e.activation(dst[:, m, :], b[:, :], ACT.Copy), t, *t0)
                    bf.append(t1)
                    b2, t2, f2 = square_sum([(dst[:, m, :], [t1])], cc("bd64"))
                    y, t3, yf = rsqrt(b2, t2, f2, 64, 1e-6)
                    t4 = V(lambda e: e.scalar_tensor_tensor(out=dst[:, m, :], in0=dst[:, m, :],
                                                            scalar=pc(gname), in1=y[:, :],
                                                            op0=ALU.mult, op1=ALU.mult), t3)
                    yf.append(t4)
                    if scale:
                        t4 = V(lambda e: e.tensor_scalar(dst[:, m, :], dst[:, m, :], scale, None, ALU.mult), t4)
                    return t4

                trs = rms(1e-6, th)
                tx = normed(trs, "kv_norm")
                tk = []
                for m in range(8):
                    b, t, bf = group("w_kv", m, 8, xin(tx))
                    tk.append(head_norm(kT, m, b, t, bf, "k_norm", None))
                tv, t = values("w_kv", D, tx, Vt, t0)
                xuse(t)
                tx = normed(trs, "b_norm")
                tq = []
                for m in range(8):
                    b, t, bf = group("b_w_q", m, 8, xin(tx))
                    tq.append(head_norm(qT, m, b, t, bf, "q_norm", 0.125))
                xuse(t)

                PL = {0: (0, 0), 1: (1, 0), 3: (1, 384), 2: (2, 0)}
                OF = {0: 0, 1: 512, 3: 896, 2: 1024}
                N = {j: T - P * j for j in range(4)}
                sps, wws = Slots(spb), Slots(wwb)
                for s_ in (sps, wws):
                    for f in s_.free:
                        f.extend(t0)
                txo = []
                st = {}

                def scores(hd):
                    r = slice(64 * (hd % 2), 64 * (hd % 2) + 64)
                    m = hd // 2
                    bs = [bank.take() for _ in range(3)]
                    for j in (0, 1, 3, 2):
                        bi, o = PL[j]
                        b, bw, bf = bs[bi]
                        t = PE(lambda e, b=b, o=o, j=j, r=r, m=m: e.matmul(
                            b[:, o:o + N[j]], kT[r, m, j * P:(j + 1) * P], qT[r, m, j * P:T],
                            start=(o == 0), stop=False, skip_group_check=True),
                            tk[m], tq[m], *(bw if o == 0 else []))
                        t = PE(lambda e, b=b, o=o: e.matmul(
                            b[:, o:o + P], idb[:, :], mkb[:, :], start=False, stop=False, skip_group_check=True),
                            tmk, inc=True)
                    sp, w, f = sps.take()
                    tg = []
                    for bi, (o, n) in enumerate(((0, 512), (512, 512), (1024, 256))):
                        b = bs[bi][0]
                        sv = sp[:, o:o + n]
                        s, sw, sf = tmp.take()
                        t1 = A(lambda e, s=s, b=b, n=n: e.activation(s[:, 0:n], b[:, 0:n], ACT.Abs), t, *sw)
                        t2 = A(lambda e, s=s, n=n: e.activation(s[:, 0:n], s[:, 0:n], ACT.Exp, scale=-1.0), t1, table="log_exp")
                        t3 = A(lambda e, s=s, n=n: e.activation(s[:, 0:n], s[:, 0:n], ACT.Ln, bias=1.0), t2, table="log_exp")
                        t4 = V(lambda e, s=s, n=n, b=b, sv=sv: e.scalar_tensor_tensor(
                            out=sv, in0=b[:, 0:n], scalar=0.0, in1=s[:, 0:n], op0=ALU.max, op1=ALU.add),
                            t3, *w)
                        sf.append(t4)
                    st[hd] = (bs, sp, f, [t4])

                def sums(hd):
                    bs, sp, f, tg = st[hd]
                    for i in range(4):
                        bi, o = PL[i]
                        b = bs[bi][0]
                        for j in range(i, 4):
                            L = cc("ntri") if j == i else cc("nones")
                            oo = o + P * (j - i)
                            t = PE(lambda e, b=b, oo=oo, j=j, L=L, i=i: e.matmul(
                                b[:, oo:oo + N[j]], L, sp[:, OF[j]:OF[j] + N[j]], start=False,
                                stop=(j == 3), skip_group_check=True), *tg, inc=True)
                    f.append(t)
                    ww, w, f2 = wws.take()
                    tg = []
                    for bi, (o, n) in enumerate(((0, 512), (512, 512), (1024, 256))):
                        b, _, bf = bs[bi]
                        t1 = A(lambda e, b=b, n=n, o=o: e.activation(ww[:, o:o + n], b[:, 0:n], ACT.Exp), t, *w, table="log_exp")
                        bf.append(t1)
                    st[hd] = (ww, f2, [t1])

                def mix(hd):
                    ww, f, tg = st[hd]
                    r = slice(64 * (hd % 2), 64 * (hd % 2) + 64)
                    if hd % 2 == 0:
                        st["o"] = bank.take()
                    b, bw, bf = st["o"]
                    for j in range(4):
                        t = PE(lambda e, j=j, b=b, r=r, hd=hd: e.matmul(
                            b[r, j * P:T], Vt[:, j, hd * 64:(hd + 1) * 64], ww[:, OF[j]:OF[j] + N[j]],
                            start=(j == 0), stop=(j == 3), skip_group_check=True),
                            *tg, *tv, *(bw if j == 0 and hd % 2 == 0 else []), inc=(j == 3))
                    f.append(t)
                    if hd % 2:
                        m = hd // 2
                        a = A(lambda e: e.activation(xh[:, m, :], b[:, :], ACT.Copy), t, *xrel[m])
                        v = V(lambda e: e.tensor_tensor(xl[:, m, :], b[:, :], xh[:, m, :].bitcast(F32),
                                                        ALU.subtract), a, *xrel[m])
                        bf.append(v)
                        txo.append([a, v])

                for s in range(18):
                    if s < 16:
                        scores(s)
                    if 1 <= s < 17:
                        sums(s - 1)
                    if s >= 2:
                        mix(s - 2)
                for m in range(8):
                    b, t, bf = group("b_w_o", m, 8, xin(txo))
                    th[m] = add_h(m, b, t, bf, th)
                xuse(t)
                return th

        def mamba(th):
            cm = ExitStack()
            with cm:
                xs = [sb(cm, f"mx{i}", [P, 2, T]) for i in range(2)]
                xt = [sb(cm, f"mxt{i}", [P, 4, 256]) for i in range(2)]
                zs = [sb(cm, f"mz{i}", [P, 2, T]) for i in range(2)]
                cbs = [sb(cm, f"mcb{i}", [P, 10, P]) for i in range(2)]
                Eb = [sb(cm, f"mE{i}", [P, 10, P]) for i in range(2)]
                bcT = [sb(cm, f"mbc{i}", [P, T]) for i in range(2)]
                uh = sb(cm, "muh", [P, 8, T], R32)
                ul = sb(cm, "mul", [P, 8, T], R32)
                dtk = sb(cm, "dtk", [P, 4, 32])
                adt = sb(cm, "adt", [P, 4, 32])
                aneg = sb(cm, "aneg", [P, 32])
                bias = sb(cm, "mbias", [P, 10, 32])
                acsT = sb(cm, "acsT", [32, T])
                t0 = barrier()
                E_, cbS, bcS, uS = Slots(Eb), Slots(cbs), Slots(bcT), Slots(list(range(8)))
                for s_ in (E_, cbS, bcS, uS):
                    for f in s_.free:
                        f.extend(t0)
                gS = Slots([0, 1])
                for f in gS.free:
                    f.extend(t0)
                tx = normed(rms(1e-5, th), "m_norm")

                bk, by = parted(bank, 6, 2)

                WH, WL, w1, w2, wf = weights(("a_w_in_2", "N32", 6144, 0, 8), 256)
                b, bw, bf = bk.take()
                for tb in range(4):
                    for k in range(8):
                        for n, (X, W) in enumerate(((xh, WH), (xl, WH), (xh, WL))):
                            t = PE(lambda e, tb=tb, k=k, n=n, X=X, W=W, b=b: e.matmul(
                                b[:, tb * 32:(tb + 1) * 32], X[:, k, tb * P:(tb + 1) * P],
                                W[:, k * 32:(k + 1) * 32], start=(tb == 0 and k == 0 and n == 0),
                                stop=(k == 7 and n == 2), skip_group_check=True),
                                w1, w2, *tx[k], *(bw if tb == 0 and k == 0 and n == 0 else []),
                                inc=(k == 7 and n == 2))
                wf.append(t)
                s, sw, sf = tmp.take()
                xb = s[:, 0:128].rearrange("p (t h) -> p t h", t=4)
                xe = s[:, 128:256].rearrange("p (t h) -> p t h", t=4)
                t = V(lambda e, b=b: e.tensor_tensor(xb, b[:, 0:128].rearrange("p (t h) -> p t h", t=4),
                                                pc("m_dtb", 0, 32).unsqueeze(1).broadcast_to([P, 4, 32]),
                                                ALU.add), t, ld, *sw)
                bf.append(t)
                t = A(lambda e: e.activation(xe, xb, ACT.Abs), t)
                t = A(lambda e: e.activation(xe, xe, ACT.Exp, scale=-1.0), t, table="log_exp")
                t = A(lambda e: e.activation(xe, xe, ACT.Ln, bias=1.0), t, table="log_exp")
                t = V(lambda e: e.scalar_tensor_tensor(out=dtk[:, :, :], in0=xb, scalar=0.0, in1=xe,
                                                       op0=ALU.max, op1=ALU.add), t, *t0)
                sf.append(t)
                tdt = t
                t = A(lambda e: e.activation(aneg[:, :], pc("m_al", 0, 32), ACT.Exp), ld, *t0, table="log_exp")
                t = V(lambda e: e.scalar_tensor_tensor(
                    out=adt[:, :, :], in0=dtk[:, :, :], scalar=-1.0,
                    in1=aneg[:, :].unsqueeze(1).broadcast_to([P, 4, 32]), op0=ALU.mult, op1=ALU.mult), t, tdt)
                tadt = t
                OFF = {}
                n = 4
                for j in range(4):
                    for i in range(j + 1, 4):
                        OFF[(j, i)] = n
                        n += 1
                b, bw, bf = bk.take()
                first = True
                for j in range(4):
                    t = PE(lambda e, j=j, b=b, first=first: e.matmul(
                        b[:, j * 32:(j + 1) * 32], cc("nupper"), adt[:, j, :], start=first, stop=True,
                        skip_group_check=True), tadt, *(bw if first else []), inc=True)
                    first = False
                for (j, i), n in OFF.items():
                    mids = list(range(j + 1, i))
                    t = PE(lambda e, j=j, n=n, mids=mids, b=b: e.matmul(
                        b[:, n * 32:(n + 1) * 32], cc("slower"), adt[:, j, :], start=False, stop=not mids,
                        skip_group_check=True), inc=True)
                    for m_ in mids:
                        t = PE(lambda e, n=n, m_=m_, mids=mids, b=b: e.matmul(
                            b[:, n * 32:(n + 1) * 32], cc("ones"), adt[:, m_, :], start=False,
                            stop=(m_ == mids[-1]), skip_group_check=True), inc=True)
                tbias = A(lambda e, b=b: e.activation(bias[:, :, :], b[:, 0:320].rearrange("p (n h) -> p n h", h=32),
                                                 ACT.Copy), t, *t0)
                bf.append(tbias)
                b, bw, bf = bk.take()
                for j in range(4):
                    t = PE(lambda e, j=j, b=b: e.matmul(
                        b[0:32, j * P:(j + 1) * P], adt[:, j, :], cc("upper"), start=(j == 0), stop=True,
                        skip_group_check=True), tadt, *(bw if j == 0 else []), inc=(j == 3))
                tacs = A(lambda e, b=b: e.activation(acsT[:, :], b[0:32, :], ACT.Copy), t, *t0)
                bf.append(tacs)

                def conv(ch, b, t, bf, dst, wdst):
                    r, w1, f1 = tmp.take()
                    t1 = A(lambda e: e.activation(r[:, :], b[:, :], ACT.Copy), t, *w1)
                    bf.append(t1)
                    t2 = V(lambda e: e.tensor_scalar(dst, r[:, :], pc("m_cw", 3 * 32 + ch), pc("m_cb", ch),
                                                     ALU.mult, ALU.add), t1, *wdst)
                    for j in range(1, 4):
                        t2 = V(lambda e, j=j: e.scalar_tensor_tensor(
                            out=dst[:, j:T], in0=r[:, 0:T - j], scalar=pc("m_cw", (3 - j) * 32 + ch),
                            in1=dst[:, j:T], op0=ALU.mult, op1=ALU.add), t2)
                    f1.append(t2)
                    return A(lambda e: e.activation(dst, dst, ACT.Silu), t2, table="silu")

                gst = {}

                def dense_g(g):
                    gi, gw, gf = gS.take()
                    X, XT, Z = xs[gi], xt[gi], zs[gi]
                    Bt, w1, fB = bcS.take()
                    b, t, bf = group("a_w_in_2", 32 + g, 8, xin(tx), ring=bk)
                    tB = conv(16 + g, b, t, bf, Bt[:, :], w1)
                    yield
                    Ct, w2, fC = bcS.take()
                    b, t, bf = group("a_w_in_2", 40 + g, 8, xin(tx), ring=bk)
                    tC = conv(24 + g, b, t, bf, Ct[:, :], w2)
                    yield
                    tX = []
                    for i in range(2):
                        b, t, bf = group("a_w_in_2", 16 + 2 * g + i, 8, xin(tx), ring=bk)
                        tX.append(conv(2 * g + i, b, t, bf, X[:, i, :], gw))
                        if i == 0:
                            cb, w3, fcb = cbS.take()
                            tcb = []
                            pieces_ = [[(j, j, j * P) for j in range(4)],
                                       [(0, 1, 0), (0, 2, P), (0, 3, 2 * P)],
                                       [(1, 2, 0), (1, 3, P), (2, 3, 2 * P)]]
                            for pi, pcs in enumerate(pieces_):
                                bb, bw, bbf = bk.take()
                                runs = []
                                for j, i_, o in pcs:
                                    if pi and runs and runs[-1][0] == j:
                                        runs[-1][2] += 1
                                    else:
                                        runs.append([j, i_, 1, o])
                                for n, (j, i_, cnt, o) in enumerate(runs):
                                    t = PE(lambda e, j=j, i_=i_, cnt=cnt, o=o, n=n, bb=bb: e.matmul(
                                        bb[:, o:o + cnt * P], Bt[:, j * P:(j + 1) * P],
                                        Ct[:, i_ * P:(i_ + cnt) * P], start=(n == 0), stop=True,
                                        skip_group_check=True), tB, tC, *(bw if n == 0 else []),
                                        inc=(n == len(runs) - 1))
                                n0 = (0, 4, 7)[pi]
                                n1 = (4, 7, 10)[pi]
                                tc = A(lambda e, bb=bb, n0=n0, n1=n1: e.activation(
                                    cb[:, n0:n1, :], bb[:, 0:(n1 - n0) * P].rearrange("p (n c) -> p n c", c=P),
                                    ACT.Copy), t, *w3)
                                bbf.append(tc)
                                tcb.append(tc)
                            fB.append(t)
                            fC.append(t)
                        yield
                    tXT = []
                    for i in range(2):
                        bb, bw, bbf = bk.take()
                        for tb in range(4):
                            t = PE(lambda e, tb=tb, i=i, bb=bb: e.transpose(
                                bb[:, tb * P:(tb + 1) * P], X[:, i, tb * P:(tb + 1) * P], cc("ident")),
                                tX[i], *(bw if tb == 0 else []), inc=(tb == 3))
                        for hh in range(2):
                            hd = 4 * g + 2 * i + hh
                            t2 = V(lambda e, i=i, hh=hh, hd=hd, bb=bb: e.tensor_tensor(
                                XT[:, :, (2 * i + hh) * 64:(2 * i + hh + 1) * 64],
                                bb[:, :].rearrange("p (t c) -> p t c", t=4)[:, :, hh * 64:(hh + 1) * 64],
                                dtk[:, :, hd:hd + 1].broadcast_to([P, 4, 64]), ALU.mult), t, tdt, *gw)
                        bbf.append(t2)
                        tXT.append(t2)
                    tZ = []
                    for i in range(2):
                        b, t, bf = group("a_w_in_2", 2 * g + i, 8, xin(tx), ring=bk)
                        t2 = A(lambda e, i=i, b=b: e.activation(Z[:, i, :], b[:, :], ACT.Silu), t, *gw, table="silu")
                        bf.append(t2)
                        tZ.append(t2)
                        yield
                    if g == 7:
                        xuse(t)
                    gst[g] = (X, XT, Z, cb, tX, tXT, tZ, tcb, fcb, gf)

                txu = {}

                def ssd(g):
                    X, XT, Z, cb, tX, tXT, tZ, tcb, fcb, gf = gst[g]
                    us = []
                    for r in range(4):
                        hd = 4 * g + r
                        rb, rw, rf = bk.take()
                        t = PE(lambda e, rb=rb, hd=hd: e.matmul(
                            rb[:, :], con[0:32, CCOL["ident"][0] + hd:CCOL["ident"][0] + hd + 1]
                            .broadcast_to([32, P]), acsT[:, :], start=True, stop=True),
                            ld, tacs, *rw, inc=True)
                        E, ew, ef = E_.take()
                        R = rb[:, :].rearrange("p (i c) -> p i c", i=4)
                        for j in range(4):
                            V(lambda e, j=j, E=E, R=R, hd=hd: e.scalar_tensor_tensor(
                                out=E[:, j, :], in0=R[:, j, :], scalar=bias[:, j, hd:hd + 1], in1=cc("low"),
                                op0=ALU.add, op1=ALU.add), t, tbias, *ew)
                        for n0, cnt, i0 in ((4, 3, 1), (7, 2, 2), (9, 1, 3)):
                            t1 = V(lambda e, n0=n0, cnt=cnt, i0=i0, E=E, R=R, hd=hd: e.tensor_tensor(
                                E[:, n0:n0 + cnt, :], R[:, i0:i0 + cnt, :],
                                bias[:, n0:n0 + cnt, hd:hd + 1].broadcast_to([P, cnt, P]), ALU.add),
                                t, tbias, *ew)
                        rf.append(t1)
                        t2 = A(lambda e, E=E: e.activation(E[:, :, :], E[:, :, :], ACT.Exp), t1, table="log_exp")
                        t4 = V(lambda e, E=E: e.tensor_tensor(E[:, :, :], E[:, :, :], cb[:, :, :], ALU.mult),
                               t2, *tcb)
                        if r % 2 == 0:
                            yb, yw, yf = by.take()
                        ro_ = slice(64 * (r % 2), 64 * (r % 2) + 64)
                        for j in range(4):
                            for (o, cnt, n0) in ((j, 1, j), (j + 1, 3 - j, OFF.get((j, j + 1)))):
                                if cnt == 0:
                                    continue
                                t5 = PE(lambda e, j=j, o=o, cnt=cnt, n0=n0, yb=yb, E=E, r=r, ro_=ro_: e.matmul(
                                    yb[ro_, o * P:(o + cnt) * P], XT[:, j, r * 64:(r + 1) * 64],
                                    E[:, n0:n0 + cnt, :].rearrange("p n c -> p (n c)"),
                                    start=(j == 0 and o == 0), stop=(j == min(o + cnt - 1, 3)),
                                    skip_group_check=True), t4, tXT[r // 2],
                                    *(yw if j == 0 and o == 0 and r % 2 == 0 else []), inc=(j == 3))
                        ef.append(t5)
                        if r % 2:
                            i = r // 2
                            t6 = V(lambda e, i=i, yb=yb, g=g: e.scalar_tensor_tensor(
                                out=X[:, i, :], in0=X[:, i, :], scalar=pc("m_d", 2 * g + i), in1=yb[:, :],
                                op0=ALU.mult, op1=ALU.add), t5, tX[i])
                            yf.append(t6)
                            t7 = V(lambda e, i=i: e.tensor_tensor(X[:, i, :], X[:, i, :], Z[:, i, :], ALU.mult),
                                   t6, tZ[i])
                            us.append(t7)
                        yield
                    fcb.append(t4)
                    b, t, bf = square_sum([(X[:, i, :], [us[i]]) for i in range(2)], cc("ones"), ring=bk)
                    y, ty, yf = rsqrt(b, t, bf, 256, 1e-5)
                    for i in range(2):
                        t8 = V(lambda e, i=i, y=y, g=g: e.scalar_tensor_tensor(
                            out=X[:, i, :], in0=X[:, i, :], scalar=pc("m_gn", 2 * g + i), in1=y[:, :],
                            op0=ALU.mult, op1=ALU.mult), ty)
                        kslot, uw, uf = uS.take()
                        ts = split(0, X[:, i, :], [t8], uw, uh[:, kslot, :], ul[:, kslot, :])
                        gf.extend(ts)
                        txu[2 * g + i] = (uh[:, kslot, :], ul[:, kslot, :], ts, uf)
                    yf.append(t8)
                    gf.append(t5)
                    yield

                def out_half(hf):
                    for m in range(8):
                        b, t, bf = group("a_w_out_2", m, 8, lambda k: txu[8 * hf + k][:3], k0=8 * hf, ring=bk)
                        th[m] = add_h(m, b, t, bf, th)
                        yield
                    for k in range(8):
                        txu[8 * hf + k][3].append(t)

                interleave(dense_g(0))
                for g in range(8):
                    if g == 4:
                        interleave(out_half(0))
                    interleave(*([dense_g(g + 1)] if g < 7 else []), ssd(g))
                interleave(out_half(1))
                rejoin(bank, bk, by)
                return th

        def att2(th):
            ca = ExitStack()
            with ca:
                kT = sb(ca, "k2T", [P, 8, T])
                qT = sb(ca, "q2T", [P, 8, T])
                Vt = sb(ca, "V2t", [P, 4, D])
                oB = qT
                Sb = Slots([sb(ca, f"S{i}", [P, 2, T]) for i in range(2)])
                wb = Slots([sb(ca, f"w2_{i}", [P, T]) for i in range(2)])
                wT = Slots([sb(ca, f"wT{i}", [P, 10, P]) for i in range(1)])
                gS2 = Slots([sb(ca, f"gate2_{i}", [P, T]) for i in range(2)])
                small = sb(ca, "small2", [P, 16, 8])
                sml = Slots([small[:, i, :] for i in range(16)])
                lam = sb(ca, "lam", [P, 8])
                t0 = barrier()
                for s_ in (Sb, wb, wT, sml, gS2):
                    for f in s_.free:
                        f.extend(t0)

                s, sw, sf = tmp.take()
                ll = pc("lam", 0, 256).rearrange("p (a b c) -> p a b c", a=2, b=2)
                pr = s[:, 0:128].rearrange("p (a c) -> p a c", a=2)
                t = V(lambda e: e.tensor_tensor(pr, ll[:, :, 0, :], ll[:, :, 1, :], ALU.mult), ld, *sw)
                t = V(lambda e: e.tensor_reduce(lam[:, 0:2], pr, AX.X, ALU.add), t, *t0)
                sf.append(t)
                t = A(lambda e: e.activation(lam[:, 2:4], lam[:, 0:2], ACT.Exp), t, table="log_exp")
                t = V(lambda e: e.tensor_tensor(lam[:, 4:5], lam[:, 3:4], lam[:, 2:3], ALU.subtract), t)
                tlam = V(lambda e: e.tensor_scalar(lam[:, 5:6], lam[:, 4:5], -LAMBDA_INIT, None, ALU.add), t)
                tsub = V(lambda e: e.tensor_scalar(lam[:, 6:7], pc("sub_g"), 1.0 - LAMBDA_INIT, None, ALU.mult),
                         *t0, ld)

                trs = rms(1e-5, th)
                tx = normed(trs, "kv2_norm")
                tk, tq = [], []
                for m in range(8):
                    b, t, bf = group("w_kv_2", m, 8, xin(tx))
                    t1 = A(lambda e, b=b, m=m: e.activation(kT[:, m, :], b[:, :], ACT.Copy), t, *t0)
                    bf.append(t1)
                    tk.append(t1)
                tv, t = values("w_kv_2", D, tx, Vt, t0)
                xuse(t)
                tx = normed(trs, "b2_norm")
                for m in range(8):
                    b, t, bf = group("b_w_in_2", m, 8, xin(tx))
                    t1 = A(lambda e, b=b, m=m: e.activation(qT[:, m, :], b[:, :], ACT.Copy, scale=0.125), t, *t0)
                    bf.append(t1)
                    tq.append(t1)

                og = {}
                gates = {}

                def gate(hd):
                    b, t, bf = group("b_w_in_2", 8 + hd, 8, xin(tx))
                    s, sw, sf = gS2.take()
                    t4 = A(lambda e, s=s, b=b: e.activation(s[:, :], b[:, :], ACT.Silu), t, *sw, table="silu")
                    bf.append(t4)
                    gates[hd] = (s, t4, sf)
                    if hd == 7:
                        xuse(t)
                    yield

                BL = {}
                n = 0
                for j in range(4):
                    for i in range(j, 4):
                        BL[(j, i)] = n
                        n += 1

                def heads(hd):
                    slope = 2.0 ** (-(hd + 1))
                    wt, ww, wf = wT.take()
                    tT = []
                    for i in range(4):
                        nk = P * (i + 1)
                        S_, sw, sf = Sb.take()
                        for c in range(2):
                            b, bw, bf = bank.take()
                            r = slice(64 * c, 64 * c + 64)
                            t = PE(lambda e, b=b, r=r, i=i, nk=nk: e.matmul(
                                b[:, 0:nk], qT[r, hd, i * P:(i + 1) * P], kT[r, hd, 0:nk], start=True,
                                stop=True), tq[hd], tk[hd], *bw, inc=True)
                            t1 = V(lambda e, b=b, c=c, nk=nk, S_=S_: e.scalar_tensor_tensor(
                                out=S_[:, c, 0:nk], in0=cc("alibi")[:, T - nk:T], scalar=slope, in1=b[:, 0:nk],
                                op0=ALU.mult, op1=ALU.add), t, ld, *sw)
                            bf.append(t1)
                        sv, vw, vf = sml.take()
                        t1 = V(lambda e, sv=sv, S_=S_, nk=nk: e.tensor_reduce(
                            sv[:, 0:2], S_[:, :, 0:nk], AX.X, ALU.max), t1, *vw)
                        t1 = V(lambda e, sv=sv: e.tensor_scalar(sv[:, 0:2], sv[:, 0:2], -1.0, None, ALU.mult), t1)
                        for c in range(2):
                            t2 = A(lambda e, sv=sv, S_=S_, nk=nk, c=c: e.activation(
                                S_[:, c, 0:nk], S_[:, c, 0:nk], ACT.Exp, bias=sv[:, c:c + 1],
                                accum_out=sv[:, 2 + c:3 + c]), t1, table="log_exp")
                        t3 = V(lambda e, sv=sv: e.reciprocal(sv[:, 4:6], sv[:, 2:4]), t2)
                        t4 = V(lambda e, sv=sv: e.tensor_tensor(sv[:, 6:7], sv[:, 5:6], lam[:, 5:6], ALU.mult),
                               t3, tlam)
                        w_, w2, f2 = wb.take()
                        t5 = V(lambda e, sv=sv, S_=S_, nk=nk, w_=w_: e.tensor_scalar(
                            w_[:, 0:nk], S_[:, 0, 0:nk], sv[:, 4:5], None, ALU.mult), t4, *w2)
                        t6 = V(lambda e, sv=sv, S_=S_, nk=nk, w_=w_: e.scalar_tensor_tensor(
                            out=w_[:, 0:nk], in0=S_[:, 1, 0:nk], scalar=sv[:, 6:7], in1=w_[:, 0:nk],
                            op0=ALU.mult, op1=ALU.add), t5)
                        sf.append(t6)
                        vf.append(t6)
                        b, bw, bf = bank.take()
                        for j in range(i + 1):
                            t7 = PE(lambda e, b=b, j=j, w_=w_: e.transpose(
                                b[:, j * P:(j + 1) * P], w_[:, j * P:(j + 1) * P], cc("ident")),
                                t6, *(bw if j == 0 else []), inc=(j == i))
                        f2.append(t7)
                        for j in range(i + 1):
                            t8 = A(lambda e, b=b, j=j, i=i: e.activation(
                                wt[:, BL[(j, i)], :], b[:, j * P:(j + 1) * P], ACT.Copy), t7, *ww)
                        bf.append(t8)
                        tT.append(t8)
                        yield
                    ob, ow, of = bank.take()
                    for j in range(4):
                        t = PE(lambda e, j=j, ob=ob: e.matmul(
                            ob[:, j * P:T], Vt[:, j, hd * P:(hd + 1) * P],
                            wt[:, BL[(j, j)]:BL[(j, 3)] + 1, :].rearrange("p n c -> p (n c)"),
                            start=(j == 0), stop=(j == 3), skip_group_check=True),
                            *tT, *tv, *(ow if j == 0 else []), inc=(j == 3))
                    wf.append(t)
                    o = oB[:, hd, :]
                    t1 = A(lambda e, o=o, ob=ob: e.activation(o, ob[:, :], ACT.Copy), t)
                    of.append(t1)
                    b2, t2, f2 = square_sum([(o, [t1])], cc("ones"))
                    y, ty, yf = rsqrt(b2, t2, f2, 128, 1e-5)
                    t3 = V(lambda e, o=o, y=y: e.scalar_tensor_tensor(
                        out=o, in0=o, scalar=lam[:, 6:7], in1=y[:, :], op0=ALU.mult, op1=ALU.mult), ty, tsub)
                    yf.append(t3)
                    s, t4, sf = gates[hd]
                    t5 = V(lambda e, o=o, s=s: e.tensor_tensor(o, o, s[:, :], ALU.mult), t3, t4)
                    sf.append(t5)
                    og[hd] = t5
                    yield

                interleave(gate(0))
                for hd in range(8):
                    interleave(*([gate(hd + 1)] if hd < 7 else []), heads(hd))
                txo = [split(m, oB[:, m, :], [og[m]], xrel[m]) for m in range(8)]
                for m in range(8):
                    b, t, bf = group("b_w_out_2", m, 8, xin(txo))
                    th[m] = add_h(m, b, t, bf, th)
                return th

        th = [[] for _ in range(8)]
        if stages[0] != "s5":
            t = Q.put_dma("sp", lambda e: e.dma_start(h[:, :, :], d["xn"]), "ldx", [])
            th = [[t] for _ in range(8)]
        for s in stages:
            if s == "s5":
                th = s5(th)
            elif s in ("ffn0", "ffn1"):
                th = ffn(int(s[-1]), th)
            elif s == "att1":
                th = att1(th)
            elif s == "mamba":
                th = mamba(th)
            elif s == "att2":
                th = att2(th)
        for k in range(8):
            Q.dma_sem(f"out{k}")
        ov = d["out"].rearrange("(k p) t -> p k t", p=P)
        if stages[-1] == "att2":
            def store(k, s, t, f):
                f.append(Q.put_dma("sp", lambda e: e.dma_start(ov[:, k, :], s[:, :]), f"out{k}", [t]))
            normed(rms(1e-5, th), "fin", out=store)
        else:
            for k in range(8):
                Q.put_dma("sp", lambda e, k=k: e.dma_start(ov[:, k, :], h[:, k, :]), f"out{k}", th[k])
        Q.number()

        block = ctx.enter_context(nc.Block())

        @block.tensor
        def _(e):
            Q.play("pe", e)

        @block.scalar
        def _(e):
            Q.play("act", e)

        @block.vector
        def _(e):
            Q.play("dve", e)

        @block.gpsimd
        def _(e):
            Q.play("pool", e)

        @block.sync
        def _(e):
            Q.play("sp", e)
            for name in (*(f"out{k}" for k in range(8)), "ud0", "ud1", "kd", "kdz", "yd"):
                if name in Q.dma:
                    e.wait_ge(Q.dma[name][0], Q.dma[name][1])
    return units


def _pack(inputs):
    f = {n: np.asarray(a) for n, a in inputs.items()}

    def cols(v):
        return np.ascontiguousarray(np.reshape(v, (-1, P)).T)

    def rep(v):
        return np.broadcast_to(np.reshape(v, (1, -1)), (P, np.size(v)))

    pp = {
        "a_norm": cols(f["a_norm"]), "kv_norm": cols(f["kv_norm"]), "b_norm": cols(f["b_norm"]),
        "ffn_norm0": cols(f["ffn_norm"][0]), "ffn_norm1": cols(f["ffn_norm"][1]), "a_d": cols(f["a_d"]),
        "k_norm": np.tile(f["k_norm"].reshape(64, 1), (2, 1)), "q_norm": np.tile(f["b_q_norm"].reshape(64, 1), (2, 1)),
        "fcw0": cols(f["ffn_conv_w"][0]), "fcw1": cols(f["ffn_conv_w"][1]),
        "fcb0": cols(f["ffn_conv_b"][0]), "fcb1": cols(f["ffn_conv_b"][1]),
        "m_norm": cols(f["a_norm_g_2"]), "m_cw": cols(f["a_conv_w_2"]), "m_cb": cols(f["a_conv_b_2"]),
        "m_d": cols(np.repeat(f["a_d_skip_2"].reshape(-1), 64)), "m_gn": cols(f["a_gate_norm_g_2"]),
        "m_dtb": rep(f["a_dt_bias_2"]), "m_al": rep(f["a_a_log_2"]),
        "kv2_norm": cols(f["kv_norm_g_2"]), "b2_norm": cols(f["b_norm_g_2"]), "sub_g": cols(f["b_sub_g_2"]),
        "fin": cols(f["final_norm_g_2"]), "lam": rep(f["b_lambda_2"]),
        "lre": np.tile(f["a_lam_re"][0].T, (2, 1)), "lim": np.tile(f["a_lam_im"][0].T, (2, 1)),
        "ldt": rep(f["a_log_dt"]),
    }
    par = np.ascontiguousarray(np.concatenate([pp[n] for n, _ in PARAMS], axis=1), dtype=np.float32)
    b = [np.tile(np.transpose(f[n][0], (1, 0, 2)), (2, 1, 1)) for n in ("a_b_re", "a_b_im")]
    c = [np.tile(np.transpose(f[n][0], (2, 0, 1)), (2, 1, 1)) for n in ("a_c_re", "a_c_im")]
    bc5 = np.ascontiguousarray(np.stack(b + c, axis=1))
    xT = f["x"][0].T
    xn = np.ascontiguousarray(xT.reshape(8, P, T).transpose(1, 0, 2))
    xp = np.ascontiguousarray(xn.reshape(P, 8, 64, 8).transpose(0, 1, 3, 2).reshape(P, 8, T))
    return par, bc5, xn, xp


def _weights(inputs, units):
    src = {n: np.asarray(inputs[n][0]) for n in ("a_w_in", "a_w_glu", "b_w_q", "b_w_o", "a_w_in_2", "a_w_out_2",
                                                 "b_w_in_2", "b_w_out_2")}
    src["w_kv"] = np.asarray(inputs["w_kv"])
    src["w_kv_2"] = np.asarray(inputs["w_kv_2"])
    for i in range(2):
        src[f"up{i}"] = np.asarray(inputs["ffn_w_up"][i])
        src[f"down{i}"] = np.asarray(inputs["ffn_w_down"][i])
    width = {"N": 512, "N32": 32}
    flat = np.empty(sum(c for _, c in units) * P, np.float32)
    o = 0
    for (name, kind, m, k0, k1), cols in units:
        w = src[name]
        c0, cw = (m * P, P) if kind == "T" else (m, width[kind])
        blk = w[k0 * P:k1 * P, c0:c0 + cw].reshape(k1 - k0, P, cw).transpose(1, 0, 2)
        flat[o:o + P * cols] = blk.reshape(-1)
        o += P * cols
    return flat


def total_weights(stages):
    n = {"s5": 3 * D * D, "ffn0": 3 * D * F_FF, "ffn1": 3 * D * F_FF, "att1": 4 * D * D,
         "mamba": D * 6176 + 2 * D * D, "att2": 5 * D * D}
    return sum(n[s] for s in stages)


def make(nc, stages=STAGES):
    d = {}
    for name, shape in (("w", [total_weights(stages)]), ("par", [P, NPAR]), ("con", [P, NCON]),
                        ("bc5", [P, 4, G5, 16]), ("xn", [P, 8, T]), ("xp", [P, 8, T])):
        if (name in ("xp", "bc5")) != (stages[0] == "s5") and name in ("xp", "bc5", "xn"):
            if not (name == "xn" and stages[0] != "s5"):
                continue
        if name == "xn" and stages[0] == "s5":
            continue
        d[name] = nc.dram_tensor("d_" + name, shape, F32, kind="ExternalInput").ap()
    if stages[0] == "s5":
        for name, shape in (("ud", [D, T]), ("yd", [D, T]), ("kd", [16, G5, 240])):
            d[name] = nc.dram_tensor("d_" + name, shape, F32, kind="Internal").ap()
    d["out"] = nc.dram_tensor("d_out", [D, T], F32, kind="ExternalOutput").ap()
    return build_program(nc, d, stages)


def arrays_for(inputs, units, stages=STAGES):
    par, bc5, xn, xp = _pack(inputs)
    a = {"w": _weights(inputs, units), "par": par, "con": constants()}
    if stages[0] == "s5":
        a.update(bc5=bc5, xp=xp)
    else:
        a.update(xn=xn)
    return {"d_" + n: v for n, v in a.items()}


def kernel(**inputs):
    import concourse.bacc as _bacc
    from concourse.bass_utils import run_bass_kernel_spmd as _run

    nc = _bacc.Bacc("TRN2", target_bir_lowering=False, num_devices=1)
    units = make(nc)
    r = _run(nc, [arrays_for(inputs, units)], core_ids=[0])
    return np.ascontiguousarray(np.asarray(r.results[0]["d_out"]).T)[None]
```

```python
import math
from contextlib import ExitStack

import numpy as np

import concourse.bass as bass
from concourse import mybir

P = 128
T = 512
D = 1024
F_FF = 2816
NF = F_FF // P
HALF = NF // 2
G5 = 64
NQ = 8
F32 = mybir.dt.float32
R32 = mybir.dt.float32r
BF16 = mybir.dt.bfloat16
ALU = mybir.AluOpType
ACT = mybir.ActivationFunctionType
AX = mybir.AxisListType
LAMBDA_INIT = 0.8 - 0.6 * math.exp(-0.3)
STAGES = ("s5", "ffn0", "att1", "ffn1", "mamba", "att2")

PARAMS = [
    ("a_norm", 8), ("kv_norm", 8), ("b_norm", 8), ("ffn_norm0", 8), ("ffn_norm1", 8), ("a_d", 8),
    ("k_norm", 1), ("q_norm", 1), ("fcw0", 3 * NF), ("fcw1", 3 * NF), ("fcb0", NF), ("fcb1", NF),
    ("m_norm", 8), ("m_cw", 4 * 32), ("m_cb", 32), ("m_d", 16), ("m_gn", 16), ("m_dtb", 32), ("m_al", 32),
    ("kv2_norm", 8), ("b2_norm", 8), ("sub_g", 1), ("fin", 8), ("lam", 256),
    ("lre", G5), ("lim", G5), ("ldt", G5),
]
PCOL = {}
_n = 0
for _name, _w in PARAMS:
    PCOL[_name] = (_n, _w)
    _n += _w
NPAR = _n

CONSTS = [("ones", 128), ("bd64", 128), ("ident", 128), ("ntri", 128), ("nones", 128), ("upper", 128),
          ("slower", 128), ("nupper", 128), ("low", 128), ("turn", 128), ("mturn", 128), ("count", 64), ("alibi", 512)]
CCOL = {}
_n = 0
for _name, _w in CONSTS:
    CCOL[_name] = (_n, _w)
    _n += _w
NCON = _n


def constants():
    p = np.arange(P)[:, None]
    c = np.arange(P)[None, :]
    out = {
        "ones": np.ones((P, P)), "bd64": (p // 64 == c // 64), "ident": (p == c),
        "ntri": -1.0 * (p >= c), "nones": -np.ones((P, P)), "upper": (p <= c),
        "slower": (p > c), "nupper": -1.0 * (p <= c), "low": np.where(p > c, -1e30, 0.0),
    }
    turn = np.zeros((P, P))
    turn[np.arange(64) + 64, np.arange(64)] = -1.0
    turn[np.arange(64), np.arange(64) + 64] = 1.0
    out["turn"], out["mturn"] = turn, -turn
    out["count"] = np.broadcast_to(np.arange(64.0)[None, :], (P, 64))
    k = np.arange(512)[None, :] - 384
    dist = -np.abs(p - k).astype(np.float64)
    blocked = np.floor_divide(k, 64) > (p // 64)
    out["alibi"] = np.where(blocked, -1e30, dist)
    return np.concatenate([out[n].astype(np.float32) for n, _ in CONSTS], axis=1)


class Tok:

    def __init__(self, sem):
        self.sem = sem
        self.val = None


class Queues:

    ENG = ("pe", "act", "dve", "pool", "sp")

    def __init__(self, nc, ctx):
        self.nc = nc
        self.q = {e: [] for e in self.ENG}
        self.sem = {e: ctx.enter_context(nc.semaphore(f"done_{e}")) for e in self.ENG if e != "sp"}
        self.ctx = ctx
        self.last = {}
        self.names = 0
        self.dma = {}

    def put(self, eng, fn, waits, inc=True, where=None, table=None):
        tok = Tok(eng) if inc else None
        (self.q[eng] if where is None else where).append((fn, [w for w in waits if w is not None], tok, table))
        if inc:
            self.last[eng] = tok
        return tok

    def dma_sem(self, name):
        self.dma[name] = [self.ctx.enter_context(self.nc.semaphore(name)), 0]
        return name

    def put_dma(self, eng, fn, name, waits, where=None):
        self.dma[name][1] += 16
        tok = Tok(name)
        tok.val = self.dma[name][1]
        (self.q[eng] if where is None else where).append((fn, [w for w in waits if w is not None], name, None))
        return tok

    def marker(self, eng):
        m = []
        self.q[eng].append(m)
        return m

    def flat(self, eng):
        for item in self.q[eng]:
            if isinstance(item, list):
                yield from item
            else:
                yield item

    def number(self):
        for eng in self.ENG:
            n = 0
            for _, _, tok, _ in self.flat(eng):
                if isinstance(tok, Tok):
                    n += 1
                    tok.val = n

    def play(self, eng, e):
        seen = {}
        loaded = None
        for fn, waits, tok, table in self.flat(eng):
            if table == "exp":
                table = "log_exp" if loaded == "log_exp" else "tanh"
            if table is not None and table != loaded:
                loaded = table
                if table == "log_exp":
                    e.preload_act_table_set("natural_log_exp_and_others")
            need = {}
            for w in waits:
                need[w.sem] = max(need.get(w.sem, 0), w.val)
            for s, v in need.items():
                if seen.get(s, 0) < v:
                    seen[s] = v
                    e.wait_ge(self.sem[s] if s in self.sem else self.dma[s][0], v)
            ins = fn(e)
            if isinstance(tok, Tok):
                ins.then_inc(self.sem[eng], 1)
            elif tok is not None:
                ins.then_inc(self.dma[tok][0], 16)


class Slots:

    def __init__(self, bufs):
        self.bufs = bufs
        self.free = [[] for _ in bufs]
        self.n = 0

    def take(self):
        i = self.n % len(self.bufs)
        assert self.n < len(self.bufs) or self.free[i], "taken again before its release was queued"
        self.n += 1
        waits = self.free[i]
        self.free[i] = []
        return self.bufs[i], waits, self.free[i]


def parted(slots, *sizes):
    out, a = [], 0
    for n in sizes:
        r = Slots(slots.bufs[a:a + n])
        r.free = slots.free[a:a + n]
        out.append(r)
        a += n
    return out


def rejoin(slots, *parts):
    slots.free = [f for r in parts for f in r.free]
    slots.n = len(slots.bufs) if all(slots.free) else 0


def interleave(*gens):
    gens = list(gens)
    while gens:
        for g in list(gens):
            if next(g, "end") == "end":
                gens.remove(g)


def blend(*pairs):
    rest = [[g, 0, n] for g, n in pairs]
    while rest:
        p = min(rest, key=lambda x: (x[1] + 0.5) / x[2])
        p[1] += 1
        if next(p[0], "end") == "end":
            rest.remove(p)


def build_program(nc, d, stages=STAGES):
    ctx = ExitStack()
    units = []
    with ctx:
        Q = Queues(nc, ctx)

        def V(fn, *w):
            return Q.put("dve", fn, w)

        def A(fn, *w, table=None):
            return Q.put("act", fn, w, table=table)

        def G(fn, *w):
            return Q.put("pool", fn, w)

        def PE(fn, *w, inc=False):
            return Q.put("pe", fn, w, inc=inc)

        def sb(c, name, shape, dt=F32):
            return c.enter_context(nc.sbuf_tensor(name, shape, dt))

        par = sb(ctx, "par", [P, NPAR])
        con = sb(ctx, "con", [P, NCON])
        h = sb(ctx, "h", [P, 8, T])
        xh = sb(ctx, "xh", [P, 8, T], R32)
        xl = sb(ctx, "xl", [P, 8, T], R32)
        RAW, NH, LA = 5, 3, 2
        raw = [sb(ctx, f"raw{i}", [P, 1024]) for i in range(RAW)]
        wh = [sb(ctx, f"wh{i}", [P, 1024], R32) for i in range(NH)]
        wl = [sb(ctx, f"wl{i}", [P, 1024], R32) for i in range(NH)]
        tmp = Slots([sb(ctx, f"tmp{i}", [P, T]) for i in range(5)])
        bank = Slots([ctx.enter_context(nc.psum_tensor(f"bank{i}", [P, T], F32)) for i in range(8)])

        def pc(name, i=0, n=1, rows=P):
            o = PCOL[name][0]
            return par[0:rows, o + i:o + i + n]

        def cc(name):
            o, n = CCOL[name]
            return con[:, o:o + n]

        Q.dma_sem("ld")
        for i in range(4):
            Q.dma_sem(f"ldx{i}")
        if stages[0] == "s5":
            ldx = [Q.put_dma("sp" if i % 2 else "act", lambda e, i=i: e.dma_start(
                h[:, 2 * i:2 * i + 2, :], d["xp"][:, 2 * i:2 * i + 2, :]), f"ldx{i}", []) for i in range(4)]
        ld = Q.put_dma("sp", lambda e: e.dma_start(par[:, :], d["par"]), "ld", [])
        ld = Q.put_dma("sp", lambda e: e.dma_start(con[:, :], d["con"]), "ld", [])

        for i in range(RAW):
            Q.dma_sem(f"raw{i}")
        marks = [(Q.marker("act"), Q.marker("dve"), Q.marker("sp"))]
        raw_free = {}
        w_free = {}

        def weights(key, cols):
            n = len(units)
            units.append((key, cols))
            off = sum(c for _, c in units[:-1]) * P
            ri, wi = n % RAW, n % NH
            marks.append((Q.marker("act"), Q.marker("dve"), Q.marker("sp")))
            ma, md, _ = marks[max(0, n + 1 - LA)]
            ms = marks[max(0, n + 2 - RAW)][2]
            src = d["w"][off:off + P * cols].rearrange("(p c) -> p c", p=P)
            got = Q.put_dma("sp", lambda e: e.dma_start(raw[ri][:, 0:cols], src), f"raw{ri}",
                            raw_free.get(n - RAW, []), where=ms)
            free = w_free.get(n - NH, [])
            last = Q.last.get("act"), Q.last.get("dve")
            hi = Q.put("act", lambda e: e.activation(wh[wi][:, 0:cols], raw[ri][:, 0:cols], ACT.Copy),
                       [got, *free], where=ma)
            lo = Q.put("dve", lambda e: e.tensor_tensor(wl[wi][:, 0:cols], raw[ri][:, 0:cols],
                                                        wh[wi][:, 0:cols].bitcast(F32), ALU.subtract),
                       [hi, *free], where=md)
            Q.last["act"], Q.last["dve"] = last
            raw_free[n] = [hi, lo]
            w_free[n] = []
            return wh[wi], wl[wi], hi, lo, w_free[n]

        def pieces(kts):
            return [(0, kts)] if kts <= 8 else [(0, (kts + 1) // 2), ((kts + 1) // 2, kts)]

        def group(name, m, kts, x, k0=0, ring=None):
            b, bw, bf = (ring or bank).take()
            n = 0
            total = 3 * kts
            for a, z in pieces(kts):
                WH, WL, th, tl, wf = weights((name, "T", m, k0 + a, k0 + z), (z - a) * P)
                for k in range(a, z):
                    o = (k - a) * P
                    XH, XL, tx = x(k)
                    for W, X, tw in ((WH, XH, th), (WH, XL, th), (WL, XH, tl)):
                        last = n == total - 1
                        t = PE(lambda e, W=W, X=X, o=o, n=n, b=b: e.matmul(
                            b[:, :], W[:, o:o + P], X, start=(n == 0), stop=(n == total - 1)),
                            tw, *tx, *(bw if n == 0 else []), inc=last or (k == z - 1 and W is WL))
                        n += 1
                wf.append(t)
            return b, t, bf

        def xin(tx):
            return lambda k: (xh[:, k, :], xl[:, k, :], tx[k])

        def split(k, src, waits, xw, hi=None, lo=None, eng=V):
            H = xh[:, k, :] if hi is None else hi
            L = xl[:, k, :] if lo is None else lo
            a = A(lambda e: e.activation(H, src, ACT.Copy), *waits, *xw)
            v = eng(lambda e: e.tensor_tensor(L, src, H.bitcast(F32), ALU.subtract), a, *xw)
            return [a, v]

        xrel = [[] for _ in range(8)]

        def xuse(t):
            for k in range(8):
                xrel[k][:] = [t]

        def rsqrt_start(b, tb, bf, n, eps, out=None):
            v, w1, f1 = tmp.take()
            y, w2, f2 = tmp.take()
            t1 = V(lambda e: e.tensor_scalar(v[:, :], b[:, :], 1.0 / n, eps, ALU.mult, ALU.add), tb, *w1)
            bf.append(t1)
            t2 = A(lambda e: e.activation(y[:, :], v[:, :], ACT.Ln), t1, *w2, table="log_exp")
            t3 = A(lambda e: e.activation(y[:, :], y[:, :], ACT.Exp, scale=-0.5), t2, table="log_exp")

            def finish():
                s, w3, f3 = tmp.take()
                t4 = V(lambda e: e.scalar_tensor_tensor(out=s[:, :], in0=y[:, :], scalar=-0.5, in1=y[:, :],
                                                        op0=ALU.mult, op1=ALU.mult), t3, *w3)
                t5 = V(lambda e: e.tensor_tensor(s[:, :], s[:, :], v[:, :], ALU.mult), t4)
                f1.append(t5)
                o = y if out is None else out
                t6 = V(lambda e: e.scalar_tensor_tensor(out=o[:, :], in0=s[:, :], scalar=1.5, in1=y[:, :],
                                                        op0=ALU.add, op1=ALU.mult), t5)
                f3.append(t6)
                if out is not None:
                    f2.append(t6)
                return y, t6, f2
            return finish

        def rsqrt(b, tb, bf, n, eps):
            return rsqrt_start(b, tb, bf, n, eps)()

        def square_sum(srcs, lhs, ring=None):
            b, bw, bf = (ring or bank).take()
            for i, (src, ts) in enumerate(srcs):
                q, w, f = tmp.take()
                ta = A(lambda e, q=q, src=src: e.activation(q[:, :], src, ACT.Square), *ts, *w)
                t = PE(lambda e, q=q, i=i: e.matmul(b[:, :], lhs, q[:, :], start=(i == 0),
                                                    stop=(i == len(srcs) - 1)),
                       ta, ld, *(bw if i == 0 else []), inc=True)
                f.append(t)
            return b, t, bf

        rs_keep = sb(ctx, "rs_keep", [P, T])
        rs_free = []
        squares = []

        def note(src, t):
            if not squares:
                squares.append(A(lambda e: e.activation(rs_keep[:, :], src, ACT.Square), t, *rs_free))
                rs_free.clear()
                return
            q, w, f = tmp.take()
            ta = A(lambda e: e.activation(q[:, :], src, ACT.Square), t, *w)
            tp = G(lambda e: e.tensor_tensor(rs_keep[:, :], rs_keep[:, :], q[:, :], ALU.add), ta, squares[-1])
            f.append(tp)
            squares.append(tp)

        def rms(eps):
            assert len(squares) == 8
            b, bw, bf = bank.take()
            t = PE(lambda e: e.matmul(b[:, :], cc("ones"), rs_keep[:, :], start=True, stop=True),
                   squares[-1], ld, *bw, inc=True)
            squares.clear()
            _, t, _ = rsqrt_start(b, t, bf, D, eps, rs_keep)()
            return t

        def normed(trs, gname, src=None, out=None):
            src = h if src is None else src
            tx = []
            for k in range(8):
                s, w, f = tmp.take()
                t = V(lambda e, k=k, s=s: e.scalar_tensor_tensor(
                    out=s[:, :], in0=src[:, k, :], scalar=pc(gname, k), in1=rs_keep[:, :],
                    op0=ALU.mult, op1=ALU.mult), trs, *w)
                rs_free.append(t)
                if out is None:
                    ts = split(k, s[:, :], [t], xrel[k], eng=G if k % 2 else V)
                    f.extend(ts)
                    tx.append(ts)
                else:
                    out(k, s, t, f)
            return tx

        def add_h(m, b, t, bf, th, final=True):
            t2 = V(lambda e: e.tensor_tensor(h[:, m, :], h[:, m, :], b[:, :], ALU.add), t, *th[m])
            bf.append(t2)
            if final:
                note(h[:, m, :], t2)
            return [t2]

        def barrier():
            return [Q.last[e] for e in ("pe", "act", "dve", "pool") if e in Q.last]

        def s5(th_in):
            c5 = ExitStack()
            with c5:
                NC, W = 64, NQ
                w = G5
                xp = h
                sm = sb(c5, "s5small", [P, 14, w])
                pw = sb(c5, "pw", [P, 2, w, 9])
                cb_ = sb(c5, "coefb", [P, 2, w, 8])
                kk = sb(c5, "kk", [P, 2, 2, W, 9])
                tau = sb(c5, "tau", [P, w])
                Bp = sb(c5, "Bp", [P, W, P])
                Bs = sb(c5, "Bs", [P, W, 9 * 16])
                ksb = sb(c5, "ksb", [16, W, P])
                rho = sb(c5, "rho", [P, W, NC])
                t0 = barrier()

                def ring(name, shape, n):
                    r = Slots([sb(c5, f"{name}{i}", shape) for i in range(n)])
                    for f in r.free:
                        f.extend(t0)
                    return r

                BTs = ring("BT", [P, W, P], 2)
                CAs = ring("CA", [P, W, 9 * 16], 3)
                Mts = ring("Mt", [P, W, P], 2)
                bcs = ring("bc", [P, 4, W, 16], 2)
                Us = ring("U", [P, W, NC], 3)
                rots = ring("rot", [P, 2, W, NC], 2)
                wk = ring("wk", [P, W, NC], 4)
                Vring = ring("V", [P, W, NC], 2)
                ust = ring("ust", [P, T], 2)
                for n in ("bc0", "bc1", "kd0", "kd1", "kdz", "mt0", "mt1", "ud0", "ud1", "ul0", "ul1", "ul2", "yd0", "yd1",
                          "ur0", "ur1", *(f"yl{m}" for m in range(8))):
                    Q.dma_sem(n)
                S = lambda i: sm[:, i, :]
                st = {}
                last = [ld]

                def v(fn, *ws):
                    last[0] = V(fn, last[0], *ws)
                    return last[0]

                def a(fn, *ws, table=None):
                    last[0] = A(fn, last[0], *ws, table=table)
                    return last[0]

                def tt(o, x, y, op):
                    return v(lambda e: e.tensor_tensor(o, x, y, op))

                def cmul(o, x, y, t1, t2):
                    tt(o[0], x[0], y[0], ALU.mult)
                    tt(t1, x[1], y[1], ALU.mult)
                    tt(o[1], x[0], y[1], ALU.mult)
                    tt(t2, x[1], y[0], ALU.mult)
                    tt(o[0], o[0], t1, ALU.subtract)
                    tt(o[1], o[1], t2, ALU.add)

                zt_ = V(lambda e: e.memset(Bs[0:16, :, :], 0.0), *t0)
                for q in range(G5 // W):
                    tz = Q.put_dma("pool", lambda e, q=q: e.dma_start(
                        d["kd"][:, q * W:(q + 1) * W, 0:112], Bs[0:16, :, 0:112]), "kdz", [zt_])

                MAGIC = 12582912.0
                TP = 2.0 * math.pi
                TP1 = 6.28125
                TP2 = float(np.float32(TP - TP1))
                TP3 = TP - TP1 - TP2

                def prep():
                    lre, lim, ldt = pc("lre", 0, w), pc("lim", 0, w), pc("ldt", 0, w)
                    last[0] = A(lambda e: e.activation(S(0), ldt, ACT.Exp), ld, *t0, table="log_exp")
                    tt(S(1), lre, S(0), ALU.mult)
                    tt(S(2), lim, S(0), ALU.mult)
                    a(lambda e: e.activation(S(3), S(1), ACT.Exp), table="log_exp")
                    a(lambda e: e.activation(S(6), S(1), ACT.Exp, scale=8.0), table="log_exp")
                    v(lambda e: e.tensor_scalar(S(10), S(2), 1.0 / TP, None, ALU.mult))
                    v(lambda e: e.tensor_scalar(S(10), S(10), MAGIC, -MAGIC, ALU.add, ALU.add))
                    for c, src in ((TP1, S(2)), (TP2, S(9)), (TP3, S(9))):
                        v(lambda e, c=c, src=src: e.scalar_tensor_tensor(
                            out=S(9), in0=S(10), scalar=-c, in1=src, op0=ALU.mult, op1=ALU.add))
                    v(lambda e: e.tensor_scalar(S(9), S(9), 3.1415925, -3.1415925, ALU.min, ALU.max))
                    a(lambda e: e.activation(S(4), S(9), ACT.Sin), table="sin")
                    a(lambda e: e.activation(S(10), S(9), ACT.Abs))
                    v(lambda e: e.tensor_scalar(S(10), S(10), -1.0, math.pi / 2, ALU.mult, ALU.add))
                    a(lambda e: e.activation(S(5), S(10), ACT.Sin), table="sin")
                    v(lambda e: e.tensor_scalar(S(10), S(9), 8.0 / TP, None, ALU.mult))
                    v(lambda e: e.tensor_scalar(S(11), S(10), MAGIC, -MAGIC, ALU.add, ALU.add))
                    st["tau"] = tt(tau[:, :], S(10), S(11), ALU.subtract)
                    yield
                    v(lambda e: e.memset(pw[:, 0, :, 0], 1.0))
                    v(lambda e: e.memset(pw[:, 1, :, 0], 0.0))
                    tt(pw[:, 0, :, 1], S(3), S(5), ALU.mult)
                    tt(pw[:, 1, :, 1], S(3), S(4), ALU.mult)
                    for k in (1, 2, 4):
                        def view(z, i, n):
                            return pw[:, z, :, i:i + n]
                        def bc(z, i, n):
                            return pw[:, z, :, i:i + 1].broadcast_to([P, w, n])
                        cmul((view(0, k + 1, k), view(1, k + 1, k)), (view(0, 1, k), view(1, 1, k)),
                             (bc(0, k, k), bc(1, k, k)), cb_[:, 0, :, 0:k], cb_[:, 1, :, 0:k])
                    yield
                    tt(S(7), lre, lre, ALU.mult)
                    tt(S(8), lim, lim, ALU.mult)
                    tt(S(7), S(7), S(8), ALU.add)
                    v(lambda e: e.reciprocal(S(7), S(7)))
                    v(lambda e: e.tensor_scalar(S(8), pw[:, 0, :, 1], -1.0, None, ALU.add))
                    tt(S(11), S(8), lre, ALU.mult)
                    tt(S(12), pw[:, 1, :, 1], lim, ALU.mult)
                    tt(S(11), S(11), S(12), ALU.add)
                    tt(S(12), pw[:, 1, :, 1], lre, ALU.mult)
                    tt(S(13), S(8), lim, ALU.mult)
                    tt(S(12), S(12), S(13), ALU.subtract)
                    tt(S(11), S(11), S(7), ALU.mult)
                    tt(S(12), S(12), S(7), ALU.mult)
                    yield
                    t1, t2 = (Bp[:, 4 * i:4 * i + 4, :].rearrange("p a b -> p (a b)")
                              .rearrange("p (g k) -> p g k", k=8) for i in range(2))
                    b8 = lambda i: S(i).unsqueeze(2).broadcast_to([P, w, 8])
                    cmul((cb_[:, 0], cb_[:, 1]), (pw[:, 0, :, 0:8], pw[:, 1, :, 0:8]), (b8(11), b8(12)), t1, t2)
                    st["prep"] = last[0]
                    yield

                def dense_u():
                    for k in range(8):
                        note(xp[:, k, :], ldx[k // 2])
                    marks[0] = Q.marker("act"), Q.marker("dve"), marks[0][2]
                    trs = rms(1e-6)
                    tx = normed(trs, "a_norm", xp)
                    for m in range(8):
                        b, t, bf = group("a_w_in", m, 8, xin(tx))
                        s, sw, sf = ust.take()
                        t2 = A(lambda e, b=b, s=s: e.activation(s[:, :], b[:, :], ACT.Copy), t, *sw)
                        bf.append(t2)
                        tw = Q.put_dma("sp", lambda e, m=m, s=s: e.dma_start(
                            d["ud"][m * P:(m + 1) * P, :], s[:, :]), f"ud{m % 2}", [t2])
                        sf.append(tw)
                        st[("ud", m)] = tw
                        yield
                    xuse(t)

                def mats(q):
                    gs = slice(q * W, (q + 1) * W)
                    bcin, w1, f1 = bcs.take()
                    tb = Q.put_dma("sp", lambda e: e.dma_start(bcin[:, :, :, :], d["bc5"][:, :, gs, :]),
                                   f"bc{q % 2}", w1)
                    K = kk[:, q % 2]
                    l = [st["prep"]]

                    def vv(fn, *ws):
                        l[0] = V(fn, l[0], *ws)
                        return l[0]

                    def stack(dst, top, bot):
                        vv(lambda e: e.tensor_scalar(dst[0:64], top[0][0:64], top[1], None, ALU.mult))
                        vv(lambda e: e.tensor_scalar(dst[64:128], bot[0][64:128], bot[1], None, ALU.mult))

                    def combine(out, n, i1, i2, *ws):
                        sh = [P, W, n, 16]
                        scr = hv(Bs, n)
                        vv(lambda e: e.tensor_tensor(out, K[:, 0, :, 0:n].unsqueeze(3).broadcast_to(sh),
                                                     bcin[:, i1].unsqueeze(2).broadcast_to(sh), ALU.mult), tb, *ws)
                        vv(lambda e: e.tensor_tensor(scr, K[:, 1, :, 0:n].unsqueeze(3).broadcast_to(sh),
                                                     bcin[:, i2].unsqueeze(2).broadcast_to(sh), ALU.mult),
                           tz)
                        vv(lambda e: e.tensor_tensor(out, out, scr, ALU.add))

                    def hv(t, n):
                        return t[:, :, 0:n * 16].rearrange("p g (k h) -> p g k h", h=16)

                    cr, ci = cb_[:, 0, gs, :], cb_[:, 1, gs, :]
                    stack(K[:, 0, :, 0:8], (cr, 1.0), (ci, 1.0))
                    stack(K[:, 1, :, 0:8], (ci, -1.0), (cr, 1.0))
                    combine(hv(Bp, 8), 8, 0, 1, *st.get("Bp", []))
                    tBp = l[0]
                    yield
                    BT, w2, fBT = BTs.take()
                    tBT = []
                    for j in range(W // 4):
                        b, bw, bf = bank.take()
                        for i in range(4):
                            g = 4 * j + i
                            t = PE(lambda e, g=g, i=i, b=b: e.transpose(
                                b[:, i * P:(i + 1) * P], Bp[:, g, :], cc("ident")),
                                tBp, *(bw if i == 0 else []), inc=(i == 3))
                        t2 = A(lambda e, j=j, b=b: e.activation(
                            BT[:, 4 * j:4 * j + 4, :], b[:, :].rearrange("p (g c) -> p g c", g=4), ACT.Copy),
                            t, *w2)
                        bf.append(t2)
                        tBT.append(t2)
                    yield
                    ar, ai = pw[:, 0, gs, :], pw[:, 1, gs, :]
                    stack(K[:, 0, :, :], (ar, 1.0), (ai, -1.0))
                    stack(K[:, 1, :, :], (ai, -1.0), (ar, -1.0))
                    CA, w3, fCA = CAs.take()
                    combine(hv(CA, 9), 9, 2, 3, *w3)
                    tCA = l[0]
                    f1.append(tCA)
                    yield
                    for j in range(W // 4):
                        b, bw, bf = bank.take()
                        for i in range(4):
                            g = 4 * j + i
                            t = PE(lambda e, g=g, i=i, b=b: e.matmul(
                                b[0:16, i * P:(i + 1) * P], Bp[:, g, 0:16], CA[:, g, 0:P],
                                start=(i == 0), stop=True, skip_group_check=True),
                                tCA, *(bw if i == 0 else []), inc=(i == 3))
                        t2 = A(lambda e, j=j, b=b: e.activation(
                            ksb[:, 4 * j:4 * j + 4, :], b[0:16, :].rearrange("p (g c) -> p g c", g=4), ACT.Copy),
                            t, *st.get("kd", []))
                        bf.append(t2)
                    st["Bp"] = [t]
                    tk = Q.put_dma("pool", lambda e: e.dma_start(d["kd"][:, gs, 112:240], ksb[:, :, :]),
                                   f"kd{q % 2}", [t2])
                    st["kd"] = [tk]
                    Mt, w4, fM = Mts.take()
                    for s in range(8):
                        tm = Q.put_dma("pool", lambda e, s=s: e.dma_start(
                            Mt[s * 16:(s + 1) * 16, :, :], d["kd"][:, gs, s * 16:s * 16 + P]),
                            f"mt{q % 2}", [tk, tz, *w4])
                    st[("m", q)] = (BT, tBT, fBT, CA, tCA, fCA, Mt, tm, fM)
                    yield

                def load_u(q):
                    U, w1, fU = Us.take()
                    src = d["ud"][q * P:(q + 1) * P, :].rearrange("(g h) (s c) -> s h g c", h=16, s=8)
                    for s in range(8):
                        tu = Q.put_dma("sp", lambda e, s=s: e.dma_start(
                            U[s * 16:(s + 1) * 16, :, :], src[7 - s]), f"ul{q % 3}", [st[("ud", q)], *w1])
                    st[("U", q)] = U, tu, fU

                def scan(q):
                    gs = slice(q * W, (q + 1) * W)
                    BT, tBT, fBT, CA, tCA, fCA, Mt, tm, fM = st[("m", q)]
                    U, tu, fU = st[("U", q)]
                    ro, w2, fro = rots.take()
                    rs_, rc_ = ro[:, 1], ro[:, 0]
                    l = [st["tau"]]

                    def vv(fn, *ws):
                        l[0] = V(fn, l[0], *ws)
                        return l[0]
                    rsc, w9, f9 = wk.take()
                    vv(lambda e: e.tensor_tensor(rsc[:, :, :], tau[:, gs].unsqueeze(2).broadcast_to([P, W, NC]),
                                                 cc("count")[:, 0:NC].unsqueeze(1).broadcast_to([P, W, NC]),
                                                 ALU.mult), *w9)
                    vv(lambda e: e.tensor_scalar(rc_, rsc[:, :, :], MAGIC, -MAGIC, ALU.add, ALU.add), *w2)
                    vv(lambda e: e.tensor_tensor(rsc[:, :, :], rsc[:, :, :], rc_, ALU.subtract))
                    t1 = A(lambda e: e.activation(rs_, rsc[:, :, :], ACT.Sin, scale=6.283185), l[0], table="sin")
                    t2 = A(lambda e: e.activation(rc_, rsc[:, :, :], ACT.Abs, scale=6.283185), l[0])
                    vv(lambda e: e.tensor_scalar(rc_, rc_, -1.0, math.pi / 2, ALU.mult, ALU.add), t2)
                    t3 = A(lambda e: e.activation(rc_, rc_, ACT.Sin), l[0], table="sin")
                    f9.append(t2)
                    b, bw, bf = bank.take()
                    for i in range(8):
                        t = PE(lambda e, i=i, b=b: e.matmul(
                            b[:, i * NC:(i + 1) * NC], BT[:, i, :], U[:, i, :], start=(i == 0), stop=True,
                            skip_group_check=True), *tBT, tu, *(bw if i == 0 else []), inc=(i == 7))
                    fBT.append(t)
                    Vs, wv, fv = Vring.take()
                    fl = lambda x: x[:, :, :].rearrange("p g c -> p (g c)")
                    t4 = A(lambda e, b=b: e.activation(fl(Vs), b[:, :], ACT.Copy), t, *wv)
                    bf.append(t4)
                    yield
                    b2, bw, bf = bank.take()
                    t = PE(lambda e: e.matmul(b2[:, :], cc("mturn"), fl(Vs), start=True, stop=True), t4, *bw,
                           inc=True)
                    vr, w3, f3 = wk.take()
                    bv = b2[:, :].rearrange("p (g c) -> p g c", g=W)
                    vv(lambda e: e.tensor_tensor(vr[:, :, :], bv, rs_, ALU.mult), t, t1, *w3)
                    bf.append(l[0])
                    vv(lambda e: e.tensor_tensor(Vs[:, :, :], Vs[:, :, :], rc_, ALU.mult), t3)
                    vv(lambda e: e.tensor_tensor(vr[:, :, :], vr[:, :, :], Vs[:, :, :], ALU.add))
                    fv.append(l[0])
                    Ss, w5, f5 = wk.take()
                    vv(lambda e: e.tensor_copy(rho[:, :, :], S(6)[:, gs].unsqueeze(2).broadcast_to([P, W, NC])),
                       *st.get("rho", []))
                    vv(lambda e: e.memset(rho[:, :, 0:1], 0.0))
                    vv(lambda e: e.tensor_tensor_scan(fl(Ss), fl(rho), fl(vr), 0.0, ALU.mult, ALU.add), *w5)
                    st["rho"] = [l[0]]
                    f3.append(l[0])
                    tS = l[0]
                    yield
                    b3, bw, bf = bank.take()
                    t = PE(lambda e: e.matmul(b3[:, :], cc("turn"), fl(Ss), start=True, stop=True), tS, *bw,
                           inc=True)
                    H, w6, f6 = wk.take()
                    bv3 = b3[:, :].rearrange("p (g c) -> p g c", g=W)
                    vv(lambda e: e.memset(H[:, :, 0:1], 0.0), *w6)
                    vv(lambda e: e.tensor_tensor(H[:, :, 1:NC], bv3[:, :, 0:NC - 1], rs_[:, :, 0:NC - 1],
                                                 ALU.mult), t)
                    bf.append(l[0])
                    vv(lambda e: e.tensor_tensor(Ss[:, :, 0:NC - 1], Ss[:, :, 0:NC - 1], rc_[:, :, 0:NC - 1],
                                                 ALU.mult), t)
                    fro.append(l[0])
                    vv(lambda e: e.tensor_tensor(H[:, :, 1:NC], H[:, :, 1:NC], Ss[:, :, 0:NC - 1], ALU.add))
                    f5.append(l[0])
                    yield
                    b4, bw, bf = bank.take()
                    for i in range(8):
                        for n, (L, R_) in enumerate(((Mt[:, i, :], U[:, i, :]), (CA[:, i, 16:144], H[:, i, :]))):
                            t = PE(lambda e, i=i, L=L, R_=R_, n=n: e.matmul(
                                b4[:, i * NC:(i + 1) * NC], L, R_, start=(i == 0 and n == 0), stop=(n == 1),
                                skip_group_check=True),
                                l[0], tm, *(bw if i == 0 and n == 0 else []), inc=(i == 7 and n == 1))
                    for f in (fU, fM, fCA, f6):
                        f.append(t)
                    Y, w7, f7 = wk.take()
                    t2 = A(lambda e: e.activation(fl(Y), b4[:, :], ACT.Copy), t, *w7)
                    bf.append(t2)
                    yv = d["yd"][q * P:(q + 1) * P, :].rearrange("(g h) (t c) -> t h g c", h=16, t=8)
                    for s in range(8):
                        tY = Q.put_dma("sp", lambda e, s=s: e.dma_start(yv[s], Y[s * 16:(s + 1) * 16, :, :]),
                                       f"yd{q % 2}", [t2])
                    f7.append(tY)
                    st[("yd", q)] = tY
                    yield

                txy = []

                def post(m):
                    y, w1, f1 = tmp.take()
                    u, w2, f2 = ust.take()
                    ty = Q.put_dma("pool", lambda e: e.dma_start(y[:, :], d["yd"][m * P:(m + 1) * P, :]),
                                   f"yl{m}", [st[("yd", m)], *w1])
                    tu = Q.put_dma("pool", lambda e: e.dma_start(u[:, :], d["ud"][m * P:(m + 1) * P, :]),
                                   f"ur{m % 2}", w2)
                    yield
                    t = V(lambda e: e.scalar_tensor_tensor(out=y[:, :], in0=u[:, :], scalar=pc("a_d", m),
                                                           in1=y[:, :], op0=ALU.mult, op1=ALU.add), ty, tu)
                    f2.append(t)
                    t = A(lambda e: e.activation(y[:, :], y[:, :], ACT.Gelu_apprx_tanh), t, table="gelu")
                    ts = split(m, y[:, :], [t], xrel[m])
                    f1.extend(ts)
                    txy.append(ts)
                    yield

                def ahead():
                    yield from prep()
                    yield from mats(0)
                    yield from mats(1)

                interleave(dense_u(), ahead())
                posts = [post(m) for m in range(8)]
                at = {2: (0, 1), 3: (0, 1), 4: (2, 3), 5: (2, 3), 6: (4, 5), 7: (4, 5, 6, 7, 6, 7)}
                scans = [scan(q) for q in range(8)]
                load_u(0)
                load_u(1)
                next(scans[0])
                for q in range(8):
                    ma = mats(q + 2) if q < 6 else iter(())
                    if q < 6:
                        load_u(q + 2)
                    if q < 7:
                        next(scans[q + 1])
                    next(scans[q])
                    next(ma, None)
                    next(scans[q])
                    next(ma, None)
                    next(ma, None)
                    next(scans[q])
                    next(ma, None)
                    for m in at.get(q, ()):
                        next(posts[m])
                th = []
                for m in range(8):
                    bv_, tv, fv = group("a_w_glu", m, 8, xin(txy))
                    bg, tg, fg = group("a_w_glu", 8 + m, 8, xin(txy))
                    s, sw, sf = tmp.take()
                    ta = A(lambda e, s=s, bg=bg: e.activation(s[:, :], bg[:, :], ACT.Sigmoid), tg, *sw,
                           table="sigmoid")
                    fg.append(ta)
                    t1 = V(lambda e, s=s, bv_=bv_: e.tensor_tensor(s[:, :], s[:, :], bv_[:, :], ALU.mult), ta, tv)
                    fv.append(t1)
                    t1 = V(lambda e, s=s, m=m: e.tensor_tensor(s[:, :], s[:, :], xp[:, m, :], ALU.add), t1)
                    t2 = V(lambda e, s=s, m=m: e.tensor_copy(
                        h[:, m, :].rearrange("p (c s) -> p s c", s=8),
                        s[:, :].rearrange("p (s c) -> p s c", s=8)), t1)
                    sf.append(t2)
                    note(h[:, m, :], t2)
                    th.append([t2])
                xuse(tg)
                return th

        def ffn(layer, th):
            cf = ExitStack()
            with cf:
                hi = sb(cf, f"fh{layer}", [P, 13, T], R32)
                lo = sb(cf, f"fl{layer}", [P, 13, T], R32)
                gts = [sb(cf, f"fg{layer}_{i}", [P, T]) for i in range(3)]
                t0 = barrier()
                act = Slots([(hi[:, i, :], lo[:, i, :]) for i in range(13)])
                gt = Slots(gts)
                for f in act.free:
                    f.extend(t0)
                for f in gt.free:
                    f.extend(t0)
                tx = normed(rms(1e-6), f"ffn_norm{layer}")
                cw, cbn = f"fcw{layer}", f"fcb{layer}"

                for half in range(2):
                    xa = []
                    for f in range(half * HALF, (half + 1) * HALF):
                        bg, tg, fg = group(f"up{layer}", NF + f, 8, xin(tx))
                        raw_, w1, f1 = gt.take()
                        t1 = A(lambda e, r=raw_, b=bg: e.activation(r[:, :], b[:, :], ACT.Copy), tg, *w1)
                        fg.append(t1)
                        bv_, tv, fv = group(f"up{layer}", f, 8, xin(tx))
                        g, w2, f2 = tmp.take()
                        t2 = V(lambda e, g=g, r=raw_, f=f: e.tensor_scalar(
                            g[:, :], r[:, :], pc(cw, 2 * NF + f), pc(cbn, f), ALU.mult, ALU.add), t1, ld, *w2)
                        t3 = V(lambda e, g=g, r=raw_, f=f: e.scalar_tensor_tensor(
                            out=g[:, 1:T], in0=r[:, 0:T - 1], scalar=pc(cw, NF + f), in1=g[:, 1:T],
                            op0=ALU.mult, op1=ALU.add), t2)
                        t4 = V(lambda e, g=g, r=raw_, f=f: e.scalar_tensor_tensor(
                            out=g[:, 2:T], in0=r[:, 0:T - 2], scalar=pc(cw, f), in1=g[:, 2:T],
                            op0=ALU.mult, op1=ALU.add), t3)
                        f1.append(t4)
                        t5 = A(lambda e, g=g: e.activation(g[:, :], g[:, :], ACT.Silu), t4, table="silu")
                        t6 = V(lambda e, g=g, b=bv_: e.tensor_tensor(g[:, :], g[:, :], b[:, :], ALU.mult), t5, tv)
                        fv.append(t6)
                        (H, L), w3, f3 = act.take()
                        ts = split(0, g[:, :], [t6], w3, H, L)
                        f2.extend(ts)
                        xa.append((H, L, ts, f3))
                    for m in range(8):
                        b, t, bf = group(f"down{layer}", m, HALF, lambda k: xa[k][:3], k0=half * HALF)
                        th[m] = add_h(m, b, t, bf, th, half == 1)
                    for x in xa:
                        x[3].append(t)
                xuse(t)
                return th

        def values(name, c0, tx, Vt, tv_w):
            out = []
            for half in range(2):
                bs = [bank.take() for _ in range(4)]
                for u in range(4):
                    WH, WL, t1, t2, wf = weights((name, "N", c0 + half * 512, 2 * u, 2 * u + 2), 1024)
                    for kk_ in range(2):
                        k = 2 * u + kk_
                        for tt_ in range(4):
                            b, bw, bf = bs[tt_]
                            for n, (X, W) in enumerate(((xh, WH), (xl, WH), (xh, WL))):
                                last = k == 7 and n == 2
                                t = PE(lambda e, b=b, X=X, W=W, k=k, kk_=kk_, tt_=tt_, n=n: e.matmul(
                                    b[:, :], X[:, k, tt_ * P:(tt_ + 1) * P], W[:, kk_ * 512:(kk_ + 1) * 512],
                                    start=(k == 0 and n == 0), stop=(k == 7 and n == 2)),
                                    t1, t2, *tx[k], *(bw if k == 0 and n == 0 else []),
                                    inc=last or (kk_ == 1 and tt_ == 3 and n == 2))
                            if last:
                                bs[tt_] = (b, t, bf)
                    wf.append(t)
                for tt_ in range(4):
                    b, t, bf = bs[tt_]
                    t2 = A(lambda e, b=b, tt_=tt_, half=half: e.activation(
                        Vt[:, tt_, half * 512:(half + 1) * 512], b[:, :], ACT.Copy), t, *tv_w)
                    bf.append(t2)
                    out.append(t2)
            return out, t

        def att1(th):
            ca = ExitStack()
            with ca:
                kT = sb(ca, "kT", [P, 8, T])
                qT = sb(ca, "qT", [P, 8, T])
                Vt = sb(ca, "Vt", [P, 4, D])
                spb = [sb(ca, f"sp{i}", [P, 1280]) for i in range(2)]
                wwb = [sb(ca, f"ww{i}", [P, 1280]) for i in range(2)]
                idb = sb(ca, "idb", [P, P], BF16)
                mkb = sb(ca, "mkb", [P, P], BF16)
                t0 = barrier()
                V(lambda e: e.tensor_copy(idb[:, :], cc("ident")), ld, *t0)
                tmk = V(lambda e: e.tensor_scalar(mkb[:, :], cc("ntri"), 1e30, None, ALU.mult), ld)

                def head_norm(dst, m, b, t, bf, gname, scale):
                    t1 = A(lambda e: e.activation(dst[:, m, :], b[:, :], ACT.Copy), t, *t0)
                    bf.append(t1)
                    b2, t2, f2 = square_sum([(dst[:, m, :], [t1])], cc("bd64"))
                    y, t3, yf = rsqrt(b2, t2, f2, 64, 1e-6)
                    t4 = V(lambda e: e.scalar_tensor_tensor(out=dst[:, m, :], in0=dst[:, m, :],
                                                            scalar=pc(gname), in1=y[:, :],
                                                            op0=ALU.mult, op1=ALU.mult), t3)
                    yf.append(t4)
                    if scale:
                        t4 = V(lambda e: e.tensor_scalar(dst[:, m, :], dst[:, m, :], scale, None, ALU.mult), t4)
                    return t4

                trs = rms(1e-6)
                tx = normed(trs, "kv_norm")
                tk = []
                for m in range(8):
                    b, t, bf = group("w_kv", m, 8, xin(tx))
                    tk.append(head_norm(kT, m, b, t, bf, "k_norm", None))
                tv, t = values("w_kv", D, tx, Vt, t0)
                xuse(t)
                tx = normed(trs, "b_norm")
                tq = []
                for m in range(8):
                    b, t, bf = group("b_w_q", m, 8, xin(tx))
                    tq.append(head_norm(qT, m, b, t, bf, "q_norm", 0.125))
                xuse(t)

                PL = {0: (0, 0), 1: (1, 0), 3: (1, 384), 2: (2, 0)}
                OF = {0: 0, 1: 512, 3: 896, 2: 1024}
                N = {j: T - P * j for j in range(4)}
                sps, wws = Slots(spb), Slots(wwb)
                for s_ in (sps, wws):
                    for f in s_.free:
                        f.extend(t0)
                txo = []
                st = {}

                def scores(hd):
                    r = slice(64 * (hd % 2), 64 * (hd % 2) + 64)
                    m = hd // 2
                    bs = [bank.take() for _ in range(3)]
                    for j in (0, 1, 3, 2):
                        bi, o = PL[j]
                        b, bw, bf = bs[bi]
                        t = PE(lambda e, b=b, o=o, j=j, r=r, m=m: e.matmul(
                            b[:, o:o + N[j]], kT[r, m, j * P:(j + 1) * P], qT[r, m, j * P:T],
                            start=(o == 0), stop=False, skip_group_check=True),
                            tk[m], tq[m], *(bw if o == 0 else []))
                        t = PE(lambda e, b=b, o=o: e.matmul(
                            b[:, o:o + P], idb[:, :], mkb[:, :], start=False, stop=False, skip_group_check=True),
                            tmk, inc=True)
                    sp, w, f = sps.take()
                    tg = []
                    for bi, (o, n) in enumerate(((0, 512), (512, 512), (1024, 256))):
                        b = bs[bi][0]
                        sv = sp[:, o:o + n]
                        s, sw, sf = tmp.take()
                        t1 = A(lambda e, s=s, b=b, n=n: e.activation(s[:, 0:n], b[:, 0:n], ACT.Abs), t, *sw)
                        t2 = A(lambda e, s=s, n=n: e.activation(s[:, 0:n], s[:, 0:n], ACT.Exp, scale=-1.0), t1, table="log_exp")
                        t3 = A(lambda e, s=s, n=n: e.activation(s[:, 0:n], s[:, 0:n], ACT.Ln, bias=1.0), t2, table="log_exp")
                        t4 = V(lambda e, s=s, n=n, b=b, sv=sv: e.scalar_tensor_tensor(
                            out=sv, in0=b[:, 0:n], scalar=0.0, in1=s[:, 0:n], op0=ALU.max, op1=ALU.add),
                            t3, *w)
                        sf.append(t4)
                    st[hd] = (bs, sp, f, [t4])

                def sums(hd):
                    bs, sp, f, tg = st[hd]
                    for i in range(4):
                        bi, o = PL[i]
                        b = bs[bi][0]
                        for j in range(i, 4):
                            L = cc("ntri") if j == i else cc("nones")
                            oo = o + P * (j - i)
                            t = PE(lambda e, b=b, oo=oo, j=j, L=L, i=i: e.matmul(
                                b[:, oo:oo + N[j]], L, sp[:, OF[j]:OF[j] + N[j]], start=False,
                                stop=(j == 3), skip_group_check=True), *tg, inc=True)
                    f.append(t)
                    ww, w, f2 = wws.take()
                    tg = []
                    for bi, (o, n) in enumerate(((0, 512), (512, 512), (1024, 256))):
                        b, _, bf = bs[bi]
                        t1 = A(lambda e, b=b, n=n, o=o: e.activation(ww[:, o:o + n], b[:, 0:n], ACT.Exp), t, *w, table="log_exp")
                        bf.append(t1)
                    st[hd] = (ww, f2, [t1])

                def mix(hd):
                    ww, f, tg = st[hd]
                    r = slice(64 * (hd % 2), 64 * (hd % 2) + 64)
                    if hd % 2 == 0:
                        st["o"] = bank.take()
                    b, bw, bf = st["o"]
                    for j in range(4):
                        t = PE(lambda e, j=j, b=b, r=r, hd=hd: e.matmul(
                            b[r, j * P:T], Vt[:, j, hd * 64:(hd + 1) * 64], ww[:, OF[j]:OF[j] + N[j]],
                            start=(j == 0), stop=(j == 3), skip_group_check=True),
                            *tg, *tv, *(bw if j == 0 and hd % 2 == 0 else []), inc=(j == 3))
                    f.append(t)
                    if hd % 2:
                        m = hd // 2
                        a = A(lambda e: e.activation(xh[:, m, :], b[:, :], ACT.Copy), t, *xrel[m])
                        v = V(lambda e: e.tensor_tensor(xl[:, m, :], b[:, :], xh[:, m, :].bitcast(F32),
                                                        ALU.subtract), a, *xrel[m])
                        bf.append(v)
                        txo.append([a, v])

                for s in range(18):
                    if s < 16:
                        scores(s)
                    if 1 <= s < 17:
                        sums(s - 1)
                    if s >= 2:
                        mix(s - 2)
                for m in range(8):
                    b, t, bf = group("b_w_o", m, 8, xin(txo))
                    th[m] = add_h(m, b, t, bf, th)
                xuse(t)
                return th

        def mamba(th):
            cm = ExitStack()
            with cm:
                xs = [sb(cm, f"mx{i}", [P, 2, T]) for i in range(2)]
                xt = [sb(cm, f"mxt{i}", [P, 4, 256]) for i in range(2)]
                zs = [sb(cm, f"mz{i}", [P, 2, T]) for i in range(2)]
                cbs = [sb(cm, f"mcb{i}", [P, 10, P]) for i in range(2)]
                Eb = [sb(cm, f"mE{i}", [P, 10, P]) for i in range(3)]
                bcT = [sb(cm, f"mbc{i}", [P, T]) for i in range(2)]
                uh = sb(cm, "muh", [P, 8, T], R32)
                ul = sb(cm, "mul", [P, 8, T], R32)
                dtk = sb(cm, "dtk", [P, 4, 32])
                adt = sb(cm, "adt", [P, 4, 32])
                aneg = sb(cm, "aneg", [P, 32])
                bias = sb(cm, "mbias", [P, 10, 32])
                acsT = sb(cm, "acsT", [32, T])
                t0 = barrier()
                E_, cbS, bcS, uS = Slots(Eb), Slots(cbs), Slots(bcT), Slots(list(range(8)))
                for s_ in (E_, cbS, bcS, uS):
                    for f in s_.free:
                        f.extend(t0)
                gS = Slots([0, 1])
                for f in gS.free:
                    f.extend(t0)
                half = par[:, PCOL["m_cw"][0]:PCOL["m_cb"][0] + 32]
                tcw = V(lambda e: e.tensor_scalar(half, half, 0.5, None, ALU.mult), ld)
                tx = normed(rms(1e-5), "m_norm")

                bk, bm, br, by = parted(bank, 3, 2, 1, 2)

                WH, WL, w1, w2, wf = weights(("a_w_in_2", "N32", 6144, 0, 8), 256)
                b, bw, bf = bk.take()
                for tb in range(4):
                    for k in range(8):
                        for n, (X, W) in enumerate(((xh, WH), (xl, WH), (xh, WL))):
                            t = PE(lambda e, tb=tb, k=k, n=n, X=X, W=W, b=b: e.matmul(
                                b[:, tb * 32:(tb + 1) * 32], X[:, k, tb * P:(tb + 1) * P],
                                W[:, k * 32:(k + 1) * 32], start=(tb == 0 and k == 0 and n == 0),
                                stop=(k == 7 and n == 2), skip_group_check=True),
                                w1, w2, *tx[k], *(bw if tb == 0 and k == 0 and n == 0 else []),
                                inc=(k == 7 and n == 2))
                wf.append(t)
                s, sw, sf = tmp.take()
                xb = s[:, 0:128].rearrange("p (t h) -> p t h", t=4)
                xe = s[:, 128:256].rearrange("p (t h) -> p t h", t=4)
                t = V(lambda e, b=b: e.tensor_tensor(xb, b[:, 0:128].rearrange("p (t h) -> p t h", t=4),
                                                pc("m_dtb", 0, 32).unsqueeze(1).broadcast_to([P, 4, 32]),
                                                ALU.add), t, ld, *sw)
                bf.append(t)
                t = A(lambda e: e.activation(xe, xb, ACT.Abs), t)
                t = A(lambda e: e.activation(xe, xe, ACT.Exp, scale=-1.0), t, table="log_exp")
                t = A(lambda e: e.activation(xe, xe, ACT.Ln, bias=1.0), t, table="log_exp")
                t = V(lambda e: e.scalar_tensor_tensor(out=dtk[:, :, :], in0=xb, scalar=0.0, in1=xe,
                                                       op0=ALU.max, op1=ALU.add), t, *t0)
                sf.append(t)
                tdt = t
                t = A(lambda e: e.activation(aneg[:, :], pc("m_al", 0, 32), ACT.Exp), ld, *t0, table="log_exp")
                t = V(lambda e: e.scalar_tensor_tensor(
                    out=adt[:, :, :], in0=dtk[:, :, :], scalar=-1.0,
                    in1=aneg[:, :].unsqueeze(1).broadcast_to([P, 4, 32]), op0=ALU.mult, op1=ALU.mult), t, tdt)
                tadt = t
                OFF = {}
                n = 4
                for j in range(4):
                    for i in range(j + 1, 4):
                        OFF[(j, i)] = n
                        n += 1
                b, bw, bf = bk.take()
                first = True
                for j in range(4):
                    t = PE(lambda e, j=j, b=b, first=first: e.matmul(
                        b[:, j * 32:(j + 1) * 32], cc("nupper"), adt[:, j, :], start=first, stop=True,
                        skip_group_check=True), tadt, *(bw if first else []), inc=True)
                    first = False
                for (j, i), n in OFF.items():
                    mids = list(range(j + 1, i))
                    t = PE(lambda e, j=j, n=n, mids=mids, b=b: e.matmul(
                        b[:, n * 32:(n + 1) * 32], cc("slower"), adt[:, j, :], start=False, stop=not mids,
                        skip_group_check=True), inc=True)
                    for m_ in mids:
                        t = PE(lambda e, n=n, m_=m_, mids=mids, b=b: e.matmul(
                            b[:, n * 32:(n + 1) * 32], cc("ones"), adt[:, m_, :], start=False,
                            stop=(m_ == mids[-1]), skip_group_check=True), inc=True)
                tbias = A(lambda e, b=b: e.activation(bias[:, :, :], b[:, 0:320].rearrange("p (n h) -> p n h", h=32),
                                                 ACT.Copy), t, *t0)
                bf.append(tbias)
                b, bw, bf = bk.take()
                for j in range(4):
                    t = PE(lambda e, j=j, b=b: e.matmul(
                        b[0:32, j * P:(j + 1) * P], adt[:, j, :], cc("upper"), start=(j == 0), stop=True,
                        skip_group_check=True), tadt, *(bw if j == 0 else []), inc=(j == 3))
                tacs = A(lambda e, b=b: e.activation(acsT[:, :], b[0:32, :], ACT.Copy), t, *t0)
                bf.append(tacs)

                def conv(ch, b, t, bf, dst, wdst):
                    t2 = A(lambda e: e.activation(dst, b[:, :], ACT.Identity, scale=pc("m_cw", 3 * 32 + ch),
                                                  bias=pc("m_cb", ch)), t, tcw, *wdst)
                    for j in range(1, 4):
                        t2 = V(lambda e, j=j: e.scalar_tensor_tensor(
                            out=dst[:, j:T], in0=b[:, 0:T - j], scalar=pc("m_cw", (3 - j) * 32 + ch),
                            in1=dst[:, j:T], op0=ALU.mult, op1=ALU.add), t2)
                    bf.append(t2)

                    def finish():
                        r, w1, f1 = tmp.take()
                        ta = A(lambda e: e.activation(r[:, :], dst, ACT.Tanh), t2, *w1, table="tanh")
                        tb = V(lambda e: e.scalar_tensor_tensor(out=dst, in0=r[:, :], scalar=1.0, in1=dst,
                                                                op0=ALU.add, op1=ALU.mult), ta)
                        f1.append(tb)
                        return tb
                    return finish

                gst = {}

                def dense_g(g):
                    def conv_later(tile, ch, dst, wdst):
                        b, t, bf = group("a_w_in_2", tile, 8, xin(tx), ring=bk)
                        return lambda: conv(ch, b, t, bf, dst, wdst)
                    Bt, w1, fB = bcS.take()
                    cB = conv_later(32 + g, 16 + g, Bt[:, :], w1)
                    yield
                    Ct, w2, fC = bcS.take()
                    fin_b = cB()
                    cC = conv_later(40 + g, 24 + g, Ct[:, :], w2)
                    yield
                    gi, gw, gf = gS.take()
                    X, XT, Z = xs[gi], xt[gi], zs[gi]
                    tX = []
                    tB = fin_b()
                    fin_c = cC()
                    c0 = conv_later(16 + 2 * g, 2 * g, X[:, 0, :], gw)
                    yield
                    tC = fin_c()
                    fin_0 = c0()
                    c1 = conv_later(17 + 2 * g, 2 * g + 1, X[:, 1, :], gw)
                    yield
                    tX.append(fin_0())
                    fin_1 = c1()
                    zb = [group("a_w_in_2", 2 * g, 8, xin(tx), ring=bk)]
                    cb, w3, fcb = cbS.take()
                    tcb = []
                    pieces_ = [[(j, j, j * P) for j in range(4)],
                               [(0, 1, 0), (0, 2, P), (0, 3, 2 * P)],
                               [(1, 2, 0), (1, 3, P), (2, 3, 2 * P)]]
                    for pi, pcs in enumerate(pieces_):
                        bb, bw, bbf = bm.take()
                        runs = []
                        for j, i_, o in pcs:
                            if pi and runs and runs[-1][0] == j:
                                runs[-1][2] += 1
                            else:
                                runs.append([j, i_, 1, o])
                        for n, (j, i_, cnt, o) in enumerate(runs):
                            t = PE(lambda e, j=j, i_=i_, cnt=cnt, o=o, n=n, bb=bb: e.matmul(
                                bb[:, o:o + cnt * P], Bt[:, j * P:(j + 1) * P],
                                Ct[:, i_ * P:(i_ + cnt) * P], start=(n == 0), stop=True,
                                skip_group_check=True), tB, tC, *(bw if n == 0 else []),
                                inc=(n == len(runs) - 1))
                        n0 = (0, 4, 7)[pi]
                        n1 = (4, 7, 10)[pi]
                        tc = A(lambda e, bb=bb, n0=n0, n1=n1: e.activation(
                            cb[:, n0:n1, :], bb[:, 0:(n1 - n0) * P].rearrange("p (n c) -> p n c", c=P),
                            ACT.Copy), t, *w3)
                        bbf.append(tc)
                        tcb.append(tc)
                    fB.append(t)
                    fC.append(t)
                    yield
                    tXT = []
                    tZ = []

                    def token_major(i):
                        bb, bw, bbf = bm.take()
                        for tb in range(4):
                            tp = PE(lambda e, tb=tb: e.transpose(
                                bb[:, tb * P:(tb + 1) * P], X[:, i, tb * P:(tb + 1) * P], cc("ident")),
                                tX[i], *(bw if tb == 0 else []), inc=(tb == 3))

                        def scaled():
                            for hh in range(2):
                                hd = 4 * g + 2 * i + hh
                                t2 = V(lambda e, hh=hh, hd=hd: e.tensor_tensor(
                                    XT[:, :, (2 * i + hh) * 64:(2 * i + hh + 1) * 64],
                                    bb[:, :].rearrange("p (t c) -> p t c", t=4)[:, :, hh * 64:(hh + 1) * 64],
                                    dtk[:, :, hd:hd + 1].broadcast_to([P, 4, 64]), ALU.mult), tp, tdt, *gw)
                            bbf.append(t2)
                            tXT.append(t2)
                        return scaled

                    def gate(i):
                        b, t, bf = zb[i]
                        r, w1, f1 = tmp.take()
                        t1 = A(lambda e: e.activation(r[:, :], b[:, :], ACT.Tanh, scale=0.5), t, *w1,
                               table="tanh")
                        t2 = V(lambda e: e.scalar_tensor_tensor(
                            out=Z[:, i, :], in0=r[:, :], scalar=1.0, in1=b[:, :], op0=ALU.add, op1=ALU.mult),
                            t1, *gw)
                        bf.append(t2)
                        f1.append(t2)
                        tZ.append(t2)
                    gate(0)
                    tX.append(fin_1())
                    zb.append(group("a_w_in_2", 2 * g + 1, 8, xin(tx), ring=bk))
                    if g == 7:
                        xuse(zb[1][1])
                    sc0 = token_major(0)
                    yield
                    sc0()
                    token_major(1)()
                    gate(1)
                    gst[g] = (X, XT, Z, cb, tX, tXT, tZ, tcb, fcb, gf)
                    yield

                txu = {}
                est = {}

                def spread(hd):
                    rb, rw, rf = br.take()
                    t = PE(lambda e: e.matmul(
                        rb[:, :], con[0:32, CCOL["ident"][0] + hd:CCOL["ident"][0] + hd + 1]
                        .broadcast_to([32, P]), acsT[:, :], start=True, stop=True),
                        ld, tacs, *rw, inc=True)
                    est[hd] = rb, t, rf

                def decay(hd):
                    rb, t, rf = est[hd]
                    E, ew, ef = E_.take()
                    R = rb[:, :].rearrange("p (i c) -> p i c", i=4)
                    for j in range(4):
                        t1 = V(lambda e, j=j: e.scalar_tensor_tensor(
                            out=E[:, j, :], in0=R[:, j, :], scalar=bias[:, j, hd:hd + 1], in1=cc("low"),
                            op0=ALU.add, op1=ALU.add), t, tbias, *ew)
                    for n0, cnt, i0 in ((4, 3, 1), (7, 2, 2), (9, 1, 3)):
                        for i in range(cnt):
                            ta = A(lambda e, n=n0 + i, i=i0 + i: e.activation(
                                E[:, n, :], R[:, i, :], ACT.Exp, bias=bias[:, n, hd:hd + 1]),
                                t1, tbias, *ew, table="exp")
                    rf.append(ta)
                    ta = A(lambda e: e.activation(E[:, 0:4, :], E[:, 0:4, :], ACT.Exp), t1, table="exp")
                    est[hd] = (E, [ta], ef)

                def ssd(g):
                    X, XT, Z, cb, tX, tXT, tZ, tcb, fcb, gf = gst[g]
                    us, ybs, ty = [], {}, {}

                    def update(i):
                        yb, yf = ybs[i]
                        t6 = V(lambda e: e.scalar_tensor_tensor(
                            out=X[:, i, :], in0=X[:, i, :], scalar=pc("m_d", 2 * g + i), in1=yb[:, :],
                            op0=ALU.mult, op1=ALU.add), ty[i], tX[i])
                        yf.append(t6)
                        us.append(V(lambda e: e.scalar_tensor_tensor(
                            out=X[:, i, :], in0=X[:, i, :], scalar=0.5, in1=Z[:, i, :], op0=ALU.mult,
                            op1=ALU.mult), t6, tZ[i]))

                    for r in range(4):
                        hd = 4 * g + r
                        if hd < 31:
                            decay(hd + 1)
                        if r == 2:
                            update(0)
                        yield
                        E, t2, ef = est[hd]
                        t4 = V(lambda e, E=E: e.tensor_tensor(E[:, :, :], E[:, :, :], cb[:, :, :], ALU.mult),
                               *t2, *tcb)
                        if hd < 30:
                            spread(hd + 2)
                        if r % 2 == 0:
                            yb, yw, yf = by.take()
                        ybs[r // 2] = yb, yf
                        ro_ = slice(64 * (r % 2), 64 * (r % 2) + 64)
                        for j in range(4):
                            for (o, cnt, n0) in ((j, 1, j), (j + 1, 3 - j, OFF.get((j, j + 1)))):
                                if cnt == 0:
                                    continue
                                t5 = PE(lambda e, j=j, o=o, cnt=cnt, n0=n0, yb=yb, E=E, r=r, ro_=ro_: e.matmul(
                                    yb[ro_, o * P:(o + cnt) * P], XT[:, j, r * 64:(r + 1) * 64],
                                    E[:, n0:n0 + cnt, :].rearrange("p n c -> p (n c)"),
                                    start=(j == 0 and o == 0), stop=(j == min(o + cnt - 1, 3)),
                                    skip_group_check=True), t4, tXT[r // 2],
                                    *(yw if j == 0 and o == 0 and r % 2 == 0 else []), inc=(j == 3))
                        ef.append(t5)
                        ty[r // 2] = t5
                        yield
                    update(1)
                    fcb.append(t4)
                    sq, w1, f1 = tmp.take()
                    sq2, w2, f2 = tmp.take()
                    t = V(lambda e: e.tensor_tensor(sq[:, :], X[:, 0, :], X[:, 0, :], ALU.mult), us[0], *w1)
                    ta = A(lambda e: e.activation(sq2[:, :], X[:, 1, :], ACT.Square), us[1], *w2)
                    t = V(lambda e: e.tensor_tensor(sq[:, :], sq[:, :], sq2[:, :], ALU.add), t, ta)
                    f2.append(t)
                    yield
                    b, bw, bf = by.take()
                    t = PE(lambda e: e.matmul(b[:, :], cc("ones"), sq[:, :], start=True, stop=True), t, ld, *bw,
                           inc=True)
                    f1.append(t)
                    yield
                    newton = rsqrt_start(b, t, bf, 256, 1e-5)
                    yield
                    y, ty, yf = newton()
                    for i in range(2):
                        t8 = V(lambda e, i=i, y=y, g=g: e.scalar_tensor_tensor(
                            out=X[:, i, :], in0=X[:, i, :], scalar=pc("m_gn", 2 * g + i), in1=y[:, :],
                            op0=ALU.mult, op1=ALU.mult), ty)
                        kslot, uw, uf = uS.take()
                        ts = split(0, X[:, i, :], [t8], uw, uh[:, kslot, :], ul[:, kslot, :])
                        gf.extend(ts)
                        txu[2 * g + i] = (uh[:, kslot, :], ul[:, kslot, :], ts, uf)
                    yf.append(t8)
                    gf.append(t5)
                    yield

                def out_part(q, ms):
                    late = None
                    for m in ms:
                        if late:
                            th[late[0]] = add_h(*late, th, q == 3)
                        b, t, bf = group("a_w_out_2", m, 4, lambda k: txu[4 * q + k][:3], k0=4 * q, ring=bk)
                        if m == 7:
                            for k in range(4):
                                txu[4 * q + k][3].append(t)
                        late = m, b, t, bf
                        yield
                    th[late[0]] = add_h(*late, th, q == 3)
                    yield

                interleave(dense_g(0))
                spread(0)
                decay(0)
                spread(1)
                for g in range(8):
                    q = g // 2 - 1
                    blend((ssd(g), 13), *([(dense_g(g + 1), 7)] if g < 7 else []),
                          *([(out_part(q, range(4 * (g % 2), 4 * (g % 2) + 4)), 5)] if q >= 0 else []))
                interleave(out_part(3, range(8)))
                rejoin(bank, bk, bm, br, by)
                return th

        def att2(th):
            ca = ExitStack()
            with ca:
                kT = sb(ca, "k2T", [P, 8, T])
                qT = sb(ca, "q2T", [P, 8, T])
                Vt = sb(ca, "V2t", [P, 4, D])
                oB = qT
                Sb = Slots([sb(ca, f"S{i}", [P, 2, T]) for i in range(2)])
                wb = Slots([sb(ca, f"w2_{i}", [P, T]) for i in range(2)])
                wT = Slots([sb(ca, f"wT{i}", [P, 10, P]) for i in range(1)])
                gS2 = Slots([sb(ca, f"gate2_{i}", [P, T]) for i in range(2)])
                small = sb(ca, "small2", [P, 16, 8])
                sml = Slots([small[:, i, :] for i in range(16)])
                lam = sb(ca, "lam", [P, 8])
                t0 = barrier()
                for s_ in (Sb, wb, wT, sml, gS2):
                    for f in s_.free:
                        f.extend(t0)

                s, sw, sf = tmp.take()
                ll = pc("lam", 0, 256).rearrange("p (a b c) -> p a b c", a=2, b=2)
                pr = s[:, 0:128].rearrange("p (a c) -> p a c", a=2)
                t = V(lambda e: e.tensor_tensor(pr, ll[:, :, 0, :], ll[:, :, 1, :], ALU.mult), ld, *sw)
                t = V(lambda e: e.tensor_reduce(lam[:, 0:2], pr, AX.X, ALU.add), t, *t0)
                sf.append(t)
                t = A(lambda e: e.activation(lam[:, 2:4], lam[:, 0:2], ACT.Exp), t, table="log_exp")
                t = V(lambda e: e.tensor_tensor(lam[:, 4:5], lam[:, 3:4], lam[:, 2:3], ALU.subtract), t)
                tlam = V(lambda e: e.tensor_scalar(lam[:, 5:6], lam[:, 4:5], -LAMBDA_INIT, None, ALU.add), t)
                tsub = V(lambda e: e.tensor_scalar(lam[:, 6:7], pc("sub_g"), 1.0 - LAMBDA_INIT, None, ALU.mult),
                         *t0, ld)

                trs = rms(1e-5)
                tx = normed(trs, "kv2_norm")
                tk, tq = [], []
                for m in range(8):
                    b, t, bf = group("w_kv_2", m, 8, xin(tx))
                    t1 = A(lambda e, b=b, m=m: e.activation(kT[:, m, :], b[:, :], ACT.Copy), t, *t0)
                    bf.append(t1)
                    tk.append(t1)
                tv, t = values("w_kv_2", D, tx, Vt, t0)
                xuse(t)
                tx = normed(trs, "b2_norm")
                for m in range(8):
                    b, t, bf = group("b_w_in_2", m, 8, xin(tx))
                    t1 = A(lambda e, b=b, m=m: e.activation(qT[:, m, :], b[:, :], ACT.Copy, scale=0.125), t, *t0)
                    bf.append(t1)
                    tq.append(t1)

                og = {}
                gates = {}

                def gate(hd):
                    b, t, bf = group("b_w_in_2", 8 + hd, 8, xin(tx))
                    s, sw, sf = gS2.take()
                    t4 = A(lambda e, s=s, b=b: e.activation(s[:, :], b[:, :], ACT.Silu), t, *sw, table="silu")
                    bf.append(t4)
                    gates[hd] = (s, t4, sf)
                    if hd == 7:
                        xuse(t)
                    yield

                BL = {}
                n = 0
                for j in range(4):
                    for i in range(j, 4):
                        BL[(j, i)] = n
                        n += 1

                def heads(hd):
                    slope = 2.0 ** (-(hd + 1))
                    wt, ww, wf = wT.take()
                    tT = []
                    for i in range(4):
                        nk = P * (i + 1)
                        S_, sw, sf = Sb.take()
                        for c in range(2):
                            b, bw, bf = bank.take()
                            r = slice(64 * c, 64 * c + 64)
                            t = PE(lambda e, b=b, r=r, i=i, nk=nk: e.matmul(
                                b[:, 0:nk], qT[r, hd, i * P:(i + 1) * P], kT[r, hd, 0:nk], start=True,
                                stop=True), tq[hd], tk[hd], *bw, inc=True)
                            t1 = V(lambda e, b=b, c=c, nk=nk, S_=S_: e.scalar_tensor_tensor(
                                out=S_[:, c, 0:nk], in0=cc("alibi")[:, T - nk:T], scalar=slope, in1=b[:, 0:nk],
                                op0=ALU.mult, op1=ALU.add), t, ld, *sw)
                            bf.append(t1)
                        sv, vw, vf = sml.take()
                        t1 = V(lambda e, sv=sv, S_=S_, nk=nk: e.tensor_reduce(
                            sv[:, 0:2], S_[:, :, 0:nk], AX.X, ALU.max), t1, *vw)
                        t1 = V(lambda e, sv=sv: e.tensor_scalar(sv[:, 0:2], sv[:, 0:2], -1.0, None, ALU.mult), t1)
                        for c in range(2):
                            t2 = A(lambda e, sv=sv, S_=S_, nk=nk, c=c: e.activation(
                                S_[:, c, 0:nk], S_[:, c, 0:nk], ACT.Exp, bias=sv[:, c:c + 1],
                                accum_out=sv[:, 2 + c:3 + c]), t1, table="log_exp")
                        t3 = V(lambda e, sv=sv: e.reciprocal(sv[:, 4:6], sv[:, 2:4]), t2)
                        t4 = V(lambda e, sv=sv: e.tensor_tensor(sv[:, 6:7], sv[:, 5:6], lam[:, 5:6], ALU.mult),
                               t3, tlam)
                        w_, w2, f2 = wb.take()
                        t5 = V(lambda e, sv=sv, S_=S_, nk=nk, w_=w_: e.tensor_scalar(
                            w_[:, 0:nk], S_[:, 0, 0:nk], sv[:, 4:5], None, ALU.mult), t4, *w2)
                        t6 = V(lambda e, sv=sv, S_=S_, nk=nk, w_=w_: e.scalar_tensor_tensor(
                            out=w_[:, 0:nk], in0=S_[:, 1, 0:nk], scalar=sv[:, 6:7], in1=w_[:, 0:nk],
                            op0=ALU.mult, op1=ALU.add), t5)
                        sf.append(t6)
                        vf.append(t6)
                        b, bw, bf = bank.take()
                        for j in range(i + 1):
                            t7 = PE(lambda e, b=b, j=j, w_=w_: e.transpose(
                                b[:, j * P:(j + 1) * P], w_[:, j * P:(j + 1) * P], cc("ident")),
                                t6, *(bw if j == 0 else []), inc=(j == i))
                        f2.append(t7)
                        for j in range(i + 1):
                            t8 = A(lambda e, b=b, j=j, i=i: e.activation(
                                wt[:, BL[(j, i)], :], b[:, j * P:(j + 1) * P], ACT.Copy), t7, *ww)
                        bf.append(t8)
                        tT.append(t8)
                        yield
                    ob, ow, of = bank.take()
                    for j in range(4):
                        t = PE(lambda e, j=j, ob=ob: e.matmul(
                            ob[:, j * P:T], Vt[:, j, hd * P:(hd + 1) * P],
                            wt[:, BL[(j, j)]:BL[(j, 3)] + 1, :].rearrange("p n c -> p (n c)"),
                            start=(j == 0), stop=(j == 3), skip_group_check=True),
                            *tT, *tv, *(ow if j == 0 else []), inc=(j == 3))
                    wf.append(t)
                    o = oB[:, hd, :]
                    t1 = A(lambda e, o=o, ob=ob: e.activation(o, ob[:, :], ACT.Copy), t)
                    of.append(t1)
                    b2, t2, f2 = square_sum([(o, [t1])], cc("ones"))
                    y, ty, yf = rsqrt(b2, t2, f2, 128, 1e-5)
                    t3 = V(lambda e, o=o, y=y: e.scalar_tensor_tensor(
                        out=o, in0=o, scalar=lam[:, 6:7], in1=y[:, :], op0=ALU.mult, op1=ALU.mult), ty, tsub)
                    yf.append(t3)
                    s, t4, sf = gates[hd]
                    t5 = V(lambda e, o=o, s=s: e.tensor_tensor(o, o, s[:, :], ALU.mult), t3, t4)
                    sf.append(t5)
                    og[hd] = t5
                    yield

                interleave(gate(0))
                for hd in range(8):
                    interleave(*([gate(hd + 1)] if hd < 7 else []), heads(hd))
                txo = [split(m, oB[:, m, :], [og[m]], xrel[m]) for m in range(8)]
                for m in range(8):
                    b, t, bf = group("b_w_out_2", m, 8, xin(txo))
                    th[m] = add_h(m, b, t, bf, th)
                return th

        th = [[] for _ in range(8)]
        if stages[0] != "s5":
            t = Q.put_dma("sp", lambda e: e.dma_start(h[:, :, :], d["xn"]), "ldx0", [])
            th = [[t] for _ in range(8)]
            for k in range(8):
                note(h[:, k, :], t)
        for s in stages:
            if s == "s5":
                th = s5(th)
            elif s in ("ffn0", "ffn1"):
                th = ffn(int(s[-1]), th)
            elif s == "att1":
                th = att1(th)
            elif s == "mamba":
                th = mamba(th)
            elif s == "att2":
                th = att2(th)
        for k in range(8):
            Q.dma_sem(f"out{k}")
        ov = d["out"].rearrange("(k p) t -> p k t", p=P)
        if stages[-1] == "att2":
            def store(k, s, t, f):
                f.append(Q.put_dma("sp", lambda e: e.dma_start(ov[:, k, :], s[:, :]), f"out{k}", [t]))
            normed(rms(1e-5), "fin", out=store)
        else:
            for k in range(8):
                Q.put_dma("sp", lambda e, k=k: e.dma_start(ov[:, k, :], h[:, k, :]), f"out{k}", th[k])
        Q.number()

        block = ctx.enter_context(nc.Block())

        @block.tensor
        def _(e):
            Q.play("pe", e)

        @block.scalar
        def _(e):
            Q.play("act", e)

        @block.vector
        def _(e):
            Q.play("dve", e)

        @block.gpsimd
        def _(e):
            Q.play("pool", e)

        @block.sync
        def _(e):
            Q.play("sp", e)
            for name in (*(f"out{k}" for k in range(8)), "ud0", "ud1", "kd0", "kd1", "kdz", "yd0", "yd1"):
                if name in Q.dma:
                    e.wait_ge(Q.dma[name][0], Q.dma[name][1])
    return units


def _pack(inputs):
    f = {n: np.asarray(a) for n, a in inputs.items()}

    def cols(v):
        return np.ascontiguousarray(np.reshape(v, (-1, P)).T)

    def rep(v):
        return np.broadcast_to(np.reshape(v, (1, -1)), (P, np.size(v)))

    pp = {
        "a_norm": cols(f["a_norm"]), "kv_norm": cols(f["kv_norm"]), "b_norm": cols(f["b_norm"]),
        "ffn_norm0": cols(f["ffn_norm"][0]), "ffn_norm1": cols(f["ffn_norm"][1]), "a_d": cols(f["a_d"]),
        "k_norm": np.tile(f["k_norm"].reshape(64, 1), (2, 1)), "q_norm": np.tile(f["b_q_norm"].reshape(64, 1), (2, 1)),
        "fcw0": cols(f["ffn_conv_w"][0]), "fcw1": cols(f["ffn_conv_w"][1]),
        "fcb0": cols(f["ffn_conv_b"][0]), "fcb1": cols(f["ffn_conv_b"][1]),
        "m_norm": cols(f["a_norm_g_2"]), "m_cw": cols(f["a_conv_w_2"]), "m_cb": cols(f["a_conv_b_2"]),
        "m_d": cols(np.repeat(f["a_d_skip_2"].reshape(-1), 64)), "m_gn": cols(f["a_gate_norm_g_2"]),
        "m_dtb": rep(f["a_dt_bias_2"]), "m_al": rep(f["a_a_log_2"]),
        "kv2_norm": cols(f["kv_norm_g_2"]), "b2_norm": cols(f["b_norm_g_2"]), "sub_g": cols(f["b_sub_g_2"]),
        "fin": cols(f["final_norm_g_2"]), "lam": rep(f["b_lambda_2"]),
        "lre": np.tile(f["a_lam_re"][0].T, (2, 1)), "lim": np.tile(f["a_lam_im"][0].T, (2, 1)),
        "ldt": rep(f["a_log_dt"]),
    }
    par = np.ascontiguousarray(np.concatenate([pp[n] for n, _ in PARAMS], axis=1), dtype=np.float32)
    b = [np.tile(np.transpose(f[n][0], (1, 0, 2)), (2, 1, 1)) for n in ("a_b_re", "a_b_im")]
    c = [np.tile(np.transpose(f[n][0], (2, 0, 1)), (2, 1, 1)) for n in ("a_c_re", "a_c_im")]
    bc5 = np.ascontiguousarray(np.stack(b + c, axis=1))
    xT = f["x"][0].T
    xn = np.ascontiguousarray(xT.reshape(8, P, T).transpose(1, 0, 2))
    xp = np.ascontiguousarray(xn.reshape(P, 8, 64, 8).transpose(0, 1, 3, 2).reshape(P, 8, T))
    return par, bc5, xn, xp


def _weights(inputs, units):
    src = {n: np.asarray(inputs[n][0]) for n in ("a_w_in", "a_w_glu", "b_w_q", "b_w_o", "a_w_in_2", "a_w_out_2",
                                                 "b_w_in_2", "b_w_out_2")}
    src["w_kv"] = np.asarray(inputs["w_kv"])
    src["w_kv_2"] = np.asarray(inputs["w_kv_2"])
    for i in range(2):
        src[f"up{i}"] = np.asarray(inputs["ffn_w_up"][i])
        src[f"down{i}"] = np.asarray(inputs["ffn_w_down"][i])
    width = {"N": 512, "N32": 32}
    flat = np.empty(sum(c for _, c in units) * P, np.float32)
    o = 0
    for (name, kind, m, k0, k1), cols in units:
        w = src[name]
        c0, cw = (m * P, P) if kind == "T" else (m, width[kind])
        blk = w[k0 * P:k1 * P, c0:c0 + cw].reshape(k1 - k0, P, cw).transpose(1, 0, 2)
        flat[o:o + P * cols] = blk.reshape(-1)
        o += P * cols
    return flat


def total_weights(stages):
    n = {"s5": 3 * D * D, "ffn0": 3 * D * F_FF, "ffn1": 3 * D * F_FF, "att1": 4 * D * D,
         "mamba": D * 6176 + 2 * D * D, "att2": 5 * D * D}
    return sum(n[s] for s in stages)


def make(nc, stages=STAGES):
    d = {}
    for name, shape in (("w", [total_weights(stages)]), ("par", [P, NPAR]), ("con", [P, NCON]),
                        ("bc5", [P, 4, G5, 16]), ("xn", [P, 8, T]), ("xp", [P, 8, T])):
        if (name in ("xp", "bc5")) != (stages[0] == "s5") and name in ("xp", "bc5", "xn"):
            if not (name == "xn" and stages[0] != "s5"):
                continue
        if name == "xn" and stages[0] == "s5":
            continue
        d[name] = nc.dram_tensor("d_" + name, shape, F32, kind="ExternalInput").ap()
    if stages[0] == "s5":
        for name, shape in (("ud", [D, T]), ("yd", [D, T]), ("kd", [16, G5, 240])):
            d[name] = nc.dram_tensor("d_" + name, shape, F32, kind="Internal").ap()
    d["out"] = nc.dram_tensor("d_out", [D, T], F32, kind="ExternalOutput").ap()
    return build_program(nc, d, stages)


def arrays_for(inputs, units, stages=STAGES):
    par, bc5, xn, xp = _pack(inputs)
    a = {"w": _weights(inputs, units), "par": par, "con": constants()}
    if stages[0] == "s5":
        a.update(bc5=bc5, xp=xp)
    else:
        a.update(xn=xn)
    return {"d_" + n: v for n, v in a.items()}


def kernel(**inputs):
    import concourse.bacc as _bacc
    from concourse.bass_utils import run_bass_kernel_spmd as _run

    nc = _bacc.Bacc("TRN2", target_bir_lowering=False, num_devices=1)
    units = make(nc)
    r = _run(nc, [arrays_for(inputs, units)], core_ids=[0])
    return np.ascontiguousarray(np.asarray(r.results[0]["d_out"]).T)[None]
```

```python
import math
from contextlib import ExitStack

import numpy as np

import concourse.bass as bass
from concourse import mybir

P = 128
T = 512
D = 1024
F_FF = 2816
NF = F_FF // P
HALF = NF // 2
G5 = 64
NQ = 8
F32 = mybir.dt.float32
R32 = mybir.dt.float32r
BF16 = mybir.dt.bfloat16
ALU = mybir.AluOpType
ACT = mybir.ActivationFunctionType
AX = mybir.AxisListType
LAMBDA_INIT = 0.8 - 0.6 * math.exp(-0.3)
STAGES = ("s5", "ffn0", "att1", "ffn1", "mamba", "att2")

PARAMS = [
    ("a_norm", 8), ("kv_norm", 8), ("b_norm", 8), ("ffn_norm0", 8), ("ffn_norm1", 8), ("a_d", 8),
    ("k_norm", 1), ("q_norm", 1), ("fcw0", 3 * NF), ("fcw1", 3 * NF), ("fcb0", NF), ("fcb1", NF),
    ("m_norm", 8), ("m_cw", 4 * 32), ("m_cb", 32), ("m_d", 16), ("m_gn", 16), ("m_dtb", 32), ("m_al", 32),
    ("kv2_norm", 8), ("b2_norm", 8), ("sub_g", 1), ("fin", 8), ("lam", 256),
    ("lre", G5), ("lim", G5), ("ldt", G5),
]
PCOL = {}
_n = 0
for _name, _w in PARAMS:
    PCOL[_name] = (_n, _w)
    _n += _w
NPAR = _n

CONSTS = [("ones", 128), ("bd64", 128), ("ident", 128), ("ntri", 128), ("nones", 128), ("upper", 128),
          ("slower", 128), ("nupper", 128), ("low", 128), ("turn", 128), ("mturn", 128), ("count", 64), ("alibi", 512)]
CCOL = {}
_n = 0
for _name, _w in CONSTS:
    CCOL[_name] = (_n, _w)
    _n += _w
NCON = _n


def constants():
    p = np.arange(P)[:, None]
    c = np.arange(P)[None, :]
    out = {
        "ones": np.ones((P, P)), "bd64": (p // 64 == c // 64), "ident": (p == c),
        "ntri": -1.0 * (p >= c), "nones": -np.ones((P, P)), "upper": (p <= c),
        "slower": (p > c), "nupper": -1.0 * (p <= c), "low": np.where(p > c, -1e30, 0.0),
    }
    turn = np.zeros((P, P))
    turn[np.arange(64) + 64, np.arange(64)] = -1.0
    turn[np.arange(64), np.arange(64) + 64] = 1.0
    out["turn"], out["mturn"] = turn, -turn
    out["count"] = np.broadcast_to(np.arange(64.0)[None, :], (P, 64))
    k = np.arange(512)[None, :] - 384
    dist = -np.abs(p - k).astype(np.float64)
    blocked = np.floor_divide(k, 64) > (p // 64)
    out["alibi"] = np.where(blocked, -1e30, dist)
    return np.concatenate([out[n].astype(np.float32) for n, _ in CONSTS], axis=1)


class Tok:

    def __init__(self, sem):
        self.sem = sem
        self.val = None


class Queues:

    ENG = ("pe", "act", "dve", "pool", "sp")

    def __init__(self, nc, ctx):
        self.nc = nc
        self.q = {e: [] for e in self.ENG}
        self.sem = {e: ctx.enter_context(nc.semaphore(f"done_{e}")) for e in self.ENG if e != "sp"}
        self.ctx = ctx
        self.last = {}
        self.names = 0
        self.dma = {}

    def put(self, eng, fn, waits, inc=True, where=None, table=None):
        tok = Tok(eng) if inc else None
        (self.q[eng] if where is None else where).append((fn, [w for w in waits if w is not None], tok, table))
        if inc:
            self.last[eng] = tok
        return tok

    def dma_sem(self, name):
        self.dma[name] = [self.ctx.enter_context(self.nc.semaphore(name)), 0]
        return name

    def put_dma(self, eng, fn, name, waits, where=None):
        self.dma[name][1] += 16
        tok = Tok(name)
        tok.val = self.dma[name][1]
        (self.q[eng] if where is None else where).append((fn, [w for w in waits if w is not None], name, None))
        return tok

    def marker(self, eng):
        m = []
        self.q[eng].append(m)
        return m

    def flat(self, eng):
        for item in self.q[eng]:
            if isinstance(item, list):
                yield from item
            else:
                yield item

    def number(self):
        for eng in self.ENG:
            n = 0
            for _, _, tok, _ in self.flat(eng):
                if isinstance(tok, Tok):
                    n += 1
                    tok.val = n

    def play(self, eng, e):
        seen = {}
        loaded = None
        for fn, waits, tok, table in self.flat(eng):
            if table == "exp":
                table = "log_exp" if loaded == "log_exp" else "tanh"
            if table is not None and table != loaded:
                loaded = table
                if table == "log_exp":
                    e.preload_act_table_set("natural_log_exp_and_others")
            need = {}
            for w in waits:
                need[w.sem] = max(need.get(w.sem, 0), w.val)
            for s, v in need.items():
                if seen.get(s, 0) < v:
                    seen[s] = v
                    e.wait_ge(self.sem[s] if s in self.sem else self.dma[s][0], v)
            ins = fn(e)
            if isinstance(tok, Tok):
                ins.then_inc(self.sem[eng], 1)
            elif tok is not None:
                ins.then_inc(self.dma[tok][0], 16)


class Slots:

    def __init__(self, bufs):
        self.bufs = bufs
        self.free = [[] for _ in bufs]
        self.n = 0

    def take(self):
        i = self.n % len(self.bufs)
        assert self.n < len(self.bufs) or self.free[i], "taken again before its release was queued"
        self.n += 1
        waits = self.free[i]
        self.free[i] = []
        return self.bufs[i], waits, self.free[i]


def parted(slots, *sizes):
    out, a = [], 0
    for n in sizes:
        r = Slots(slots.bufs[a:a + n])
        r.free = slots.free[a:a + n]
        out.append(r)
        a += n
    return out


def rejoin(slots, *parts):
    slots.free = [f for r in parts for f in r.free]
    slots.n = len(slots.bufs) if all(slots.free) else 0


def interleave(*gens):
    gens = list(gens)
    while gens:
        for g in list(gens):
            if next(g, "end") == "end":
                gens.remove(g)


def blend(*pairs):
    rest = [[g, 0, n] for g, n in pairs]
    while rest:
        p = min(rest, key=lambda x: (x[1] + 0.5) / x[2])
        p[1] += 1
        if next(p[0], "end") == "end":
            rest.remove(p)


def build_program(nc, d, stages=STAGES):
    ctx = ExitStack()
    units = []
    with ctx:
        Q = Queues(nc, ctx)

        def V(fn, *w):
            return Q.put("dve", fn, w)

        def A(fn, *w, table=None):
            return Q.put("act", fn, w, table=table)

        def G(fn, *w):
            return Q.put("pool", fn, w)

        def PE(fn, *w, inc=False):
            return Q.put("pe", fn, w, inc=inc)

        def sb(c, name, shape, dt=F32):
            return c.enter_context(nc.sbuf_tensor(name, shape, dt))

        par = sb(ctx, "par", [P, NPAR])
        con = sb(ctx, "con", [P, NCON])
        h = sb(ctx, "h", [P, 8, T])
        xh = sb(ctx, "xh", [P, 8, T], R32)
        xl = sb(ctx, "xl", [P, 8, T], R32)
        RAW, NH, LA = 5, 3, 2
        raw = [sb(ctx, f"raw{i}", [P, 1024]) for i in range(RAW)]
        wh = [sb(ctx, f"wh{i}", [P, 1024], R32) for i in range(NH)]
        wl = [sb(ctx, f"wl{i}", [P, 1024], R32) for i in range(NH)]
        tmp = Slots([sb(ctx, f"tmp{i}", [P, T]) for i in range(5)])
        bank = Slots([ctx.enter_context(nc.psum_tensor(f"bank{i}", [P, T], F32)) for i in range(8)])

        def pc(name, i=0, n=1, rows=P):
            o = PCOL[name][0]
            return par[0:rows, o + i:o + i + n]

        def cc(name):
            o, n = CCOL[name]
            return con[:, o:o + n]

        Q.dma_sem("ld")
        for i in range(4):
            Q.dma_sem(f"ldx{i}")
        if stages[0] == "s5":
            ldx = [Q.put_dma("sp" if i % 2 else "act", lambda e, i=i: e.dma_start(
                h[:, 2 * i:2 * i + 2, :], d["xp"][:, 2 * i:2 * i + 2, :]), f"ldx{i}", []) for i in range(4)]
        ld = Q.put_dma("sp", lambda e: e.dma_start(par[:, :], d["par"]), "ld", [])
        ld = Q.put_dma("sp", lambda e: e.dma_start(con[:, :], d["con"]), "ld", [])

        for i in range(RAW):
            Q.dma_sem(f"raw{i}")
        marks = [(Q.marker("act"), Q.marker("dve"), Q.marker("sp"))]
        raw_free = {}
        w_free = {}

        def weights(key, cols):
            n = len(units)
            units.append((key, cols))
            off = sum(c for _, c in units[:-1]) * P
            ri, wi = n % RAW, n % NH
            marks.append((Q.marker("act"), Q.marker("dve"), Q.marker("sp")))
            ma, md, _ = marks[max(0, n + 1 - LA)]
            ms = marks[max(0, n + 2 - RAW)][2]
            src = d["w"][off:off + P * cols].rearrange("(p c) -> p c", p=P)
            got = Q.put_dma("sp", lambda e: e.dma_start(raw[ri][:, 0:cols], src), f"raw{ri}",
                            raw_free.get(n - RAW, []), where=ms)
            free = w_free.get(n - NH, [])
            last = Q.last.get("act"), Q.last.get("dve")
            hi = Q.put("act", lambda e: e.activation(wh[wi][:, 0:cols], raw[ri][:, 0:cols], ACT.Copy),
                       [got, *free], where=ma)
            lo = Q.put("dve", lambda e: e.tensor_tensor(wl[wi][:, 0:cols], raw[ri][:, 0:cols],
                                                        wh[wi][:, 0:cols].bitcast(F32), ALU.subtract),
                       [hi, *free], where=md)
            Q.last["act"], Q.last["dve"] = last
            raw_free[n] = [hi, lo]
            w_free[n] = []
            return wh[wi], wl[wi], hi, lo, w_free[n]

        def pieces(kts):
            return [(0, kts)] if kts <= 8 else [(0, (kts + 1) // 2), ((kts + 1) // 2, kts)]

        def group(name, m, kts, x, k0=0, ring=None):
            if (name, m) in paired:
                return paired.pop((name, m))
            b, bw, bf = (ring or bank).take()
            n = 0
            total = 3 * kts
            for a, z in pieces(kts):
                WH, WL, th, tl, wf = weights((name, "T", m, k0 + a, k0 + z), (z - a) * P)
                for k in range(a, z):
                    o = (k - a) * P
                    XH, XL, tx = x(k)
                    for W, X, tw in ((WH, XH, th), (WH, XL, th), (WL, XH, tl)):
                        last = n == total - 1
                        t = PE(lambda e, W=W, X=X, o=o, n=n, b=b: e.matmul(
                            b[:, :], W[:, o:o + P], X, start=(n == 0), stop=(n == total - 1)),
                            tw, *tx, *(bw if n == 0 else []), inc=last or (k == z - 1 and W is WL))
                        n += 1
                wf.append(t)
            return b, t, bf

        paired = {}

        def pair(keys, tx, ring=None):
            x = xin(tx)
            jobs = []
            for name, m in keys:
                b, bw, bf = (ring or bank).take()
                jobs.append((name, m, b, bw, bf, weights((name, "T", m, 0, 8), 8 * P)))
            for k in range(8):
                XH, XL, tk_ = x(k)
                for name, m, b, bw, bf, (WH, WL, th_, tl_, wf) in jobs:
                    for n, (W, X, tw) in enumerate(((WH, XH, th_), (WH, XL, th_), (WL, XH, tl_))):
                        last = k == 7 and n == 2
                        t = PE(lambda e, W=W, X=X, k=k, n=n, b=b: e.matmul(
                            b[:, :], W[:, k * P:(k + 1) * P], X, start=(k == 0 and n == 0),
                            stop=(k == 7 and n == 2)),
                            tw, *tk_, *(bw if k == 0 and n == 0 else []), inc=last)
                    if last:
                        wf.append(t)
                        paired[(name, m)] = b, t, bf

        def xin(tx):
            return lambda k: (xh[:, k, :], xl[:, k, :], tx[k])

        def split(k, src, waits, xw, hi=None, lo=None, eng=V):
            H = xh[:, k, :] if hi is None else hi
            L = xl[:, k, :] if lo is None else lo
            a = V(lambda e: e.tensor_copy(H, src), *waits, *xw)
            v = eng(lambda e: e.tensor_tensor(L, src, H.bitcast(F32), ALU.subtract), a, *xw)
            return [a, v]

        xrel = [[] for _ in range(8)]

        def xuse(t):
            for k in range(8):
                xrel[k][:] = [t]

        def rsqrt_start(b, tb, bf, n, eps, out=None):
            v, w1, f1 = tmp.take()
            y, w2, f2 = tmp.take()
            t1 = V(lambda e: e.tensor_scalar(v[:, :], b[:, :], 1.0 / n, eps, ALU.mult, ALU.add), tb, *w1)
            bf.append(t1)
            t2 = A(lambda e: e.activation(y[:, :], v[:, :], ACT.Ln), t1, *w2, table="log_exp")
            t3 = A(lambda e: e.activation(y[:, :], y[:, :], ACT.Exp, scale=-0.5), t2, table="log_exp")

            def finish():
                s, w3, f3 = tmp.take()
                t4 = V(lambda e: e.scalar_tensor_tensor(out=s[:, :], in0=y[:, :], scalar=-0.5, in1=y[:, :],
                                                        op0=ALU.mult, op1=ALU.mult), t3, *w3)
                t5 = V(lambda e: e.tensor_tensor(s[:, :], s[:, :], v[:, :], ALU.mult), t4)
                f1.append(t5)
                o = y if out is None else out
                t6 = V(lambda e: e.scalar_tensor_tensor(out=o[:, :], in0=s[:, :], scalar=1.5, in1=y[:, :],
                                                        op0=ALU.add, op1=ALU.mult), t5)
                f3.append(t6)
                if out is not None:
                    f2.append(t6)
                return y, t6, f2
            return finish

        def rsqrt(b, tb, bf, n, eps):
            return rsqrt_start(b, tb, bf, n, eps)()

        def square_sum(srcs, lhs, ring=None):
            b, bw, bf = (ring or bank).take()
            for i, (src, ts) in enumerate(srcs):
                q, w, f = tmp.take()
                ta = A(lambda e, q=q, src=src: e.activation(q[:, :], src, ACT.Square), *ts, *w)
                t = PE(lambda e, q=q, i=i: e.matmul(b[:, :], lhs, q[:, :], start=(i == 0),
                                                    stop=(i == len(srcs) - 1)),
                       ta, ld, *(bw if i == 0 else []), inc=True)
                f.append(t)
            return b, t, bf

        rs_keep = sb(ctx, "rs_keep", [P, T])
        rs_free = []
        squares = []

        def note(src, t):
            if not squares:
                squares.append(A(lambda e: e.activation(rs_keep[:, :], src, ACT.Square), t, *rs_free))
                rs_free.clear()
                return
            q, w, f = tmp.take()
            ta = A(lambda e: e.activation(q[:, :], src, ACT.Square), t, *w)
            tp = G(lambda e: e.tensor_tensor(rs_keep[:, :], rs_keep[:, :], q[:, :], ALU.add), ta, squares[-1])
            f.append(tp)
            squares.append(tp)

        def rms(eps):
            assert len(squares) == 8
            b, bw, bf = bank.take()
            t = PE(lambda e: e.matmul(b[:, :], cc("ones"), rs_keep[:, :], start=True, stop=True),
                   squares[-1], ld, *bw, inc=True)
            squares.clear()
            _, t, _ = rsqrt_start(b, t, bf, D, eps, rs_keep)()
            return t

        def normed(trs, gname, src=None, out=None):
            src = h if src is None else src
            tx = []
            for k in range(8):
                s, w, f = tmp.take()
                t = V(lambda e, k=k, s=s: e.scalar_tensor_tensor(
                    out=s[:, :], in0=src[:, k, :], scalar=pc(gname, k), in1=rs_keep[:, :],
                    op0=ALU.mult, op1=ALU.mult), trs, *w)
                rs_free.append(t)
                if out is None:
                    ts = split(k, s[:, :], [t], xrel[k], eng=G if k % 2 else V)
                    f.extend(ts)
                    tx.append(ts)
                else:
                    out(k, s, t, f)
            return tx

        def add_h(m, b, t, bf, th, final=True):
            t2 = V(lambda e: e.tensor_tensor(h[:, m, :], h[:, m, :], b[:, :], ALU.add), t, *th[m])
            bf.append(t2)
            if final:
                note(h[:, m, :], t2)
            return [t2]

        def barrier():
            return [Q.last[e] for e in ("pe", "act", "dve", "pool") if e in Q.last]

        def s5(th_in):
            c5 = ExitStack()
            with c5:
                NC, W = 64, NQ
                w = G5
                xp = h
                sm = sb(c5, "s5small", [P, 14, w])
                pw = sb(c5, "pw", [P, 2, w, 9])
                cb_ = sb(c5, "coefb", [P, 2, w, 8])
                quarter = sb(c5, "quarter", [P, 1])
                tau = sb(c5, "tau", [P, w])
                Bp = sb(c5, "Bp", [P, W, P])
                Bs = sb(c5, "Bs", [P, W, 9 * 16])
                ksb = sb(c5, "ksb", [16, W, P])
                rho = sb(c5, "rho", [P, W, NC])
                t0 = barrier()

                def ring(name, shape, n):
                    r = Slots([sb(c5, f"{name}{i}", shape) for i in range(n)])
                    for f in r.free:
                        f.extend(t0)
                    return r

                BTs = ring("BT", [P, W, P], 2)
                CAs = ring("CA", [P, W, 9 * 16], 3)
                Mts = ring("Mt", [P, W, P], 2)
                bcs = ring("bc", [P, 4, W, 16], 2)
                Us = ring("U", [P, W, NC], 3)
                rots = ring("rot", [P, 2, W, NC], 2)
                wk = ring("wk", [P, W, NC], 4)
                Vring = ring("V", [P, W, NC], 2)
                ust = ring("ust", [P, T], 2)
                for n in ("bc0", "bc1", "kd0", "kd1", "kdz", "mt0", "mt1", "ud0", "ud1", "ul0", "ul1", "ul2", "yd0", "yd1",
                          "ur0", "ur1", *(f"yl{m}" for m in range(8))):
                    Q.dma_sem(n)
                S = lambda i: sm[:, i, :]
                st = {}
                last = [ld]

                def v(fn, *ws):
                    last[0] = V(fn, last[0], *ws)
                    return last[0]

                def a(fn, *ws, table=None):
                    last[0] = A(fn, last[0], *ws, table=table)
                    return last[0]

                def tt(o, x, y, op):
                    return v(lambda e: e.tensor_tensor(o, x, y, op))

                def cmul(o, x, y, t1, t2):
                    tt(o[0], x[0], y[0], ALU.mult)
                    tt(t1, x[1], y[1], ALU.mult)
                    tt(o[1], x[0], y[1], ALU.mult)
                    tt(t2, x[1], y[0], ALU.mult)
                    tt(o[0], o[0], t1, ALU.subtract)
                    tt(o[1], o[1], t2, ALU.add)

                zt_ = V(lambda e: e.memset(Bs[0:16, :, :], 0.0), *t0)
                for q in range(G5 // W):
                    tz = Q.put_dma("pool", lambda e, q=q: e.dma_start(
                        d["kd"][:, q * W:(q + 1) * W, 0:112], Bs[0:16, :, 0:112]), "kdz", [zt_])

                MAGIC = 12582912.0
                TP = 2.0 * math.pi
                TP1 = 6.28125
                TP2 = float(np.float32(TP - TP1))
                TP3 = TP - TP1 - TP2

                def prep():
                    lre, lim, ldt = pc("lre", 0, w), pc("lim", 0, w), pc("ldt", 0, w)
                    last[0] = A(lambda e: e.activation(S(0), ldt, ACT.Exp), ld, *t0, table="log_exp")
                    tt(S(1), lre, S(0), ALU.mult)
                    tt(S(2), lim, S(0), ALU.mult)
                    a(lambda e: e.activation(S(3), S(1), ACT.Exp), table="log_exp")
                    a(lambda e: e.activation(S(6), S(1), ACT.Exp, scale=8.0), table="log_exp")
                    v(lambda e: e.tensor_scalar(S(10), S(2), 1.0 / TP, None, ALU.mult))
                    v(lambda e: e.tensor_scalar(S(10), S(10), MAGIC, -MAGIC, ALU.add, ALU.add))
                    for c, src in ((TP1, S(2)), (TP2, S(9)), (TP3, S(9))):
                        v(lambda e, c=c, src=src: e.scalar_tensor_tensor(
                            out=S(9), in0=S(10), scalar=-c, in1=src, op0=ALU.mult, op1=ALU.add))
                    v(lambda e: e.tensor_scalar(S(9), S(9), 3.1415925, -3.1415925, ALU.min, ALU.max))
                    a(lambda e: e.activation(S(4), S(9), ACT.Sin), table="sin")
                    a(lambda e: e.activation(S(10), S(9), ACT.Abs))
                    v(lambda e: e.tensor_scalar(S(10), S(10), -1.0, math.pi / 2, ALU.mult, ALU.add))
                    a(lambda e: e.activation(S(5), S(10), ACT.Sin), table="sin")
                    v(lambda e: e.tensor_scalar(S(10), S(9), 8.0 / TP, None, ALU.mult))
                    v(lambda e: e.tensor_scalar(S(11), S(10), MAGIC, -MAGIC, ALU.add, ALU.add))
                    st["tau"] = tt(tau[:, :], S(10), S(11), ALU.subtract)
                    yield
                    v(lambda e: e.memset(pw[:, 0, :, 0], 1.0))
                    v(lambda e: e.memset(pw[:, 1, :, 0], 0.0))
                    tt(pw[:, 0, :, 1], S(3), S(5), ALU.mult)
                    tt(pw[:, 1, :, 1], S(3), S(4), ALU.mult)
                    for k in (1, 2, 4):
                        def view(z, i, n):
                            return pw[:, z, :, i:i + n]
                        def bc(z, i, n):
                            return pw[:, z, :, i:i + 1].broadcast_to([P, w, n])
                        cmul((view(0, k + 1, k), view(1, k + 1, k)), (view(0, 1, k), view(1, 1, k)),
                             (bc(0, k, k), bc(1, k, k)), cb_[:, 0, :, 0:k], cb_[:, 1, :, 0:k])
                    yield
                    tt(S(7), lre, lre, ALU.mult)
                    tt(S(8), lim, lim, ALU.mult)
                    tt(S(7), S(7), S(8), ALU.add)
                    v(lambda e: e.reciprocal(S(7), S(7)))
                    v(lambda e: e.tensor_scalar(S(8), pw[:, 0, :, 1], -1.0, None, ALU.add))
                    tt(S(11), S(8), lre, ALU.mult)
                    tt(S(12), pw[:, 1, :, 1], lim, ALU.mult)
                    tt(S(11), S(11), S(12), ALU.add)
                    tt(S(12), pw[:, 1, :, 1], lre, ALU.mult)
                    tt(S(13), S(8), lim, ALU.mult)
                    tt(S(12), S(12), S(13), ALU.subtract)
                    tt(S(11), S(11), S(7), ALU.mult)
                    tt(S(12), S(12), S(7), ALU.mult)
                    yield
                    t1, t2 = (Bp[:, 4 * i:4 * i + 4, :].rearrange("p a b -> p (a b)")
                              .rearrange("p (g k) -> p g k", k=8) for i in range(2))
                    b8 = lambda i: S(i).unsqueeze(2).broadcast_to([P, w, 8])
                    cmul((cb_[:, 0], cb_[:, 1]), (pw[:, 0, :, 0:8], pw[:, 1, :, 0:8]), (b8(11), b8(12)), t1, t2)
                    yield
                    lo_, up = slice(0, 64), slice(64, 128)
                    def flip(z, n, s0, s1):
                        keep_ = Bp[up, 0:5, :].rearrange("p a b -> p (a b)")[:, 0:w * n].rearrange(
                            "p (g k) -> p g k", k=n)
                        v(lambda e: e.tensor_copy(keep_, z[up, 0, :, :]))
                        v(lambda e: e.tensor_scalar(z[up, 0, :, :], z[up, 1, :, :], s0, None, ALU.mult))
                        v(lambda e: e.tensor_scalar(z[up, 1, :, :], keep_, s1, None, ALU.mult))
                        v(lambda e: e.tensor_scalar(z[lo_, 1, :, :], z[lo_, 1, :, :], -1.0, None, ALU.mult))
                    flip(cb_, 8, 1.0, 1.0)
                    st["prep_b"] = last[0]
                    flip(pw, 9, -1.0, -1.0)
                    v(lambda e: e.memset(quarter[:, :], math.pi / 2))
                    st["prep"] = last[0]
                    yield

                def dense_u():
                    for k in range(8):
                        note(xp[:, k, :], ldx[k // 2])
                    marks[0] = Q.marker("act"), Q.marker("dve"), marks[0][2]
                    trs = rms(1e-6)
                    tx = normed(trs, "a_norm", xp)
                    for m in range(8):
                        b, t, bf = group("a_w_in", m, 8, xin(tx))
                        s, sw, sf = ust.take()
                        t2 = A(lambda e, b=b, s=s: e.activation(s[:, :], b[:, :], ACT.Copy), t, *sw)
                        bf.append(t2)
                        tw = Q.put_dma("sp", lambda e, m=m, s=s: e.dma_start(
                            d["ud"][m * P:(m + 1) * P, :], s[:, :]), f"ud{m % 2}", [t2])
                        sf.append(tw)
                        st[("ud", m)] = tw
                        if m in (3, 4):
                            load_u(m - 3)
                        yield
                    xuse(t)

                def load_bc(q):
                    bcin, w1, f1 = bcs.take()
                    tb = Q.put_dma("sp", lambda e: e.dma_start(
                        bcin[:, :, :, :], d["bc5"][:, :, q * W:(q + 1) * W, :]), f"bc{q % 2}", w1)
                    st[("bc", q)] = bcin, tb, f1

                def mats(q):
                    gs = slice(q * W, (q + 1) * W)
                    bcin, tb, f1 = st[("bc", q)]
                    l = [st["prep"]]

                    def vv(fn, *ws):
                        l[0] = V(fn, l[0], *ws)
                        return l[0]

                    def combine(K, out, n, i1, i2, *ws):
                        sh = [P, W, n, 16]
                        scr = hv(Bs, n)
                        tp = G(lambda e: e.tensor_tensor(scr, K[:, 1, gs, 0:n].unsqueeze(3).broadcast_to(sh),
                                                         bcin[:, i2].unsqueeze(2).broadcast_to(sh), ALU.mult),
                               tb, tz, st["prep"], *st.get("scr", []))
                        vv(lambda e: e.tensor_tensor(out, K[:, 0, gs, 0:n].unsqueeze(3).broadcast_to(sh),
                                                     bcin[:, i1].unsqueeze(2).broadcast_to(sh), ALU.mult), tb, *ws)
                        st["scr"] = [vv(lambda e: e.tensor_tensor(out, out, scr, ALU.add), tp)]

                    def hv(t, n):
                        return t[:, :, 0:n * 16].rearrange("p g (k h) -> p g k h", h=16)

                    combine(cb_, hv(Bp, 8), 8, 0, 1, *st.get("Bp", []))
                    tBp = l[0]
                    yield
                    BT, w2, fBT = BTs.take()
                    tBT = []
                    for j in range(W // 4):
                        b, bw, bf = bank.take()
                        for i in range(4):
                            g = 4 * j + i
                            t = PE(lambda e, g=g, i=i, b=b: e.transpose(
                                b[:, i * P:(i + 1) * P], Bp[:, g, :], cc("ident")),
                                tBp, *(bw if i == 0 else []), inc=(i == 3))
                        t2 = A(lambda e, j=j, b=b: e.activation(
                            BT[:, 4 * j:4 * j + 4, :], b[:, :].rearrange("p (g c) -> p g c", g=4), ACT.Copy),
                            t, *w2)
                        bf.append(t2)
                        tBT.append(t2)
                    yield
                    CA, w3, fCA = CAs.take()
                    combine(pw, hv(CA, 9), 9, 2, 3, *w3)
                    tCA = l[0]
                    f1.append(tCA)
                    yield
                    for j in range(W // 4):
                        b, bw, bf = bank.take()
                        for i in range(4):
                            g = 4 * j + i
                            t = PE(lambda e, g=g, i=i, b=b: e.matmul(
                                b[0:16, i * P:(i + 1) * P], Bp[:, g, 0:16], CA[:, g, 0:P],
                                start=(i == 0), stop=True, skip_group_check=True),
                                tCA, *(bw if i == 0 else []), inc=(i == 3))
                        t2 = A(lambda e, j=j, b=b: e.activation(
                            ksb[:, 4 * j:4 * j + 4, :], b[0:16, :].rearrange("p (g c) -> p g c", g=4), ACT.Copy),
                            t, *st.get("kd", []))
                        bf.append(t2)
                    st["Bp"] = [t]
                    tk = Q.put_dma("sp", lambda e: e.dma_start(d["kd"][:, gs, 112:240], ksb[:, :, :]),
                                   f"kd{q % 2}", [t2])
                    st["kd"] = [tk]
                    Mt, w4, fM = Mts.take()
                    for s in range(8):
                        tm = Q.put_dma("sp", lambda e, s=s: e.dma_start(
                            Mt[s * 16:(s + 1) * 16, :, :], d["kd"][:, gs, s * 16:s * 16 + P]),
                            f"mt{q % 2}", [tk, tz, *w4])
                    st[("m", q)] = (BT, tBT, fBT, CA, tCA, fCA, Mt, tm, fM)
                    yield

                def load_u(q):
                    U, w1, fU = Us.take()
                    src = d["ud"][q * P:(q + 1) * P, :].rearrange("(g h) (s c) -> s h g c", h=16, s=8)
                    for s in range(8):
                        tu = Q.put_dma("sp", lambda e, s=s: e.dma_start(
                            U[s * 16:(s + 1) * 16, :, :], src[7 - s]), f"ul{q % 3}", [st[("ud", q)], *w1])
                    st[("U", q)] = U, tu, fU

                def scan(q):
                    gs = slice(q * W, (q + 1) * W)
                    BT, tBT, fBT, CA, tCA, fCA, Mt, tm, fM = st[("m", q)]
                    U, tu, fU = st[("U", q)]
                    ro, w2, fro = rots.take()
                    rs_, rc_ = ro[:, 1], ro[:, 0]
                    l = [st["tau"]]

                    def vv(fn, *ws):
                        l[0] = V(fn, l[0], *ws)
                        return l[0]
                    rsc, w9, f9 = wk.take()
                    tg = V(lambda e: e.tensor_tensor(
                        rsc[:, :, :], tau[:, gs].unsqueeze(2).broadcast_to([P, W, NC]),
                        cc("count")[:, 0:NC].unsqueeze(1).broadcast_to([P, W, NC]), ALU.mult), st["prep"], *w9)
                    tg = V(lambda e: e.tensor_scalar(rc_, rsc[:, :, :], MAGIC, -MAGIC, ALU.add, ALU.add), tg, *w2)
                    tg = V(lambda e: e.tensor_tensor(rsc[:, :, :], rsc[:, :, :], rc_, ALU.subtract), tg)
                    t1 = A(lambda e: e.activation(rs_, rsc[:, :, :], ACT.Sin, scale=6.283185), tg, *w2,
                           table="sin")
                    t2 = A(lambda e: e.activation(rc_, rsc[:, :, :], ACT.Abs, scale=6.283185), tg)
                    t3 = A(lambda e: e.activation(rc_, rc_, ACT.Sin, scale=-1.0, bias=quarter[:, :]), t2,
                           table="sin")
                    f9.append(t2)
                    b, bw, bf = bank.take()
                    for i in range(8):
                        t = PE(lambda e, i=i, b=b: e.matmul(
                            b[:, i * NC:(i + 1) * NC], BT[:, i, :], U[:, i, :], start=(i == 0), stop=True,
                            skip_group_check=True), *tBT, tu, *(bw if i == 0 else []), inc=(i == 7))
                    fBT.append(t)
                    Vs, wv, fv = Vring.take()
                    fl = lambda x: x[:, :, :].rearrange("p g c -> p (g c)")
                    t4 = A(lambda e, b=b: e.activation(fl(Vs), b[:, :], ACT.Copy), t, *wv)
                    bf.append(t4)
                    yield
                    b2, bw, bf = bank.take()
                    t = PE(lambda e: e.matmul(b2[:, :], cc("mturn"), fl(Vs), start=True, stop=True), t4, *bw,
                           inc=True)
                    yield
                    vr, w3, f3 = wk.take()
                    bv = b2[:, :].rearrange("p (g c) -> p g c", g=W)
                    vv(lambda e: e.tensor_tensor(vr[:, :, :], bv, rs_, ALU.mult), t, t1, *w3)
                    bf.append(l[0])
                    vv(lambda e: e.tensor_tensor(Vs[:, :, :], Vs[:, :, :], rc_, ALU.mult), t3)
                    vv(lambda e: e.tensor_tensor(vr[:, :, :], vr[:, :, :], Vs[:, :, :], ALU.add))
                    fv.append(l[0])
                    Ss, w5, f5 = wk.take()
                    vv(lambda e: e.tensor_copy(rho[:, :, :], S(6)[:, gs].unsqueeze(2).broadcast_to([P, W, NC])),
                       *st.get("rho", []))
                    tr = vv(lambda e: e.memset(rho[:, :, 0:1], 0.0))
                    vv(lambda e: e.tensor_tensor_scan(fl(Ss), fl(rho), fl(vr), 0.0, ALU.mult, ALU.add), tr, *w5)
                    st["rho"] = [l[0]]
                    f3.append(l[0])
                    tS = l[0]
                    yield
                    b3, bw, bf = bank.take()
                    t = PE(lambda e: e.matmul(b3[:, :], cc("turn"), fl(Ss), start=True, stop=True), tS, *bw,
                           inc=True)
                    H, w6, f6 = wk.take()
                    bv3 = b3[:, :].rearrange("p (g c) -> p g c", g=W)
                    vv(lambda e: e.memset(H[:, :, 0:1], 0.0), *w6)
                    vv(lambda e: e.tensor_tensor(H[:, :, 1:NC], bv3[:, :, 0:NC - 1], rs_[:, :, 0:NC - 1],
                                                 ALU.mult), t)
                    bf.append(l[0])
                    vv(lambda e: e.tensor_tensor(Ss[:, :, 0:NC - 1], Ss[:, :, 0:NC - 1], rc_[:, :, 0:NC - 1],
                                                 ALU.mult), t)
                    fro.append(l[0])
                    vv(lambda e: e.tensor_tensor(H[:, :, 1:NC], H[:, :, 1:NC], Ss[:, :, 0:NC - 1], ALU.add))
                    f5.append(l[0])
                    yield
                    b4, bw, bf = bank.take()
                    for i in range(8):
                        for n, (L, R_) in enumerate(((Mt[:, i, :], U[:, i, :]), (CA[:, i, 16:144], H[:, i, :]))):
                            t = PE(lambda e, i=i, L=L, R_=R_, n=n: e.matmul(
                                b4[:, i * NC:(i + 1) * NC], L, R_, start=(i == 0 and n == 0), stop=(n == 1),
                                skip_group_check=True),
                                l[0], tm, *(bw if i == 0 and n == 0 else []), inc=(i == 7 and n == 1))
                    for f in (fU, fM, fCA, f6):
                        f.append(t)
                    Y, w7, f7 = wk.take()
                    t2 = A(lambda e: e.activation(fl(Y), b4[:, :], ACT.Copy), t, *w7)
                    bf.append(t2)
                    yv = d["yd"][q * P:(q + 1) * P, :].rearrange("(g h) (t c) -> t h g c", h=16, t=8)
                    for s in range(8):
                        tY = Q.put_dma("sp", lambda e, s=s: e.dma_start(yv[s], Y[s * 16:(s + 1) * 16, :, :]),
                                       f"yd{q % 2}", [t2])
                    f7.append(tY)
                    st[("yd", q)] = tY
                    yield

                txy = []

                def post(m):
                    y, w1, f1 = tmp.take()
                    u, w2, f2 = ust.take()
                    ty = Q.put_dma("pool", lambda e: e.dma_start(y[:, :], d["yd"][m * P:(m + 1) * P, :]),
                                   f"yl{m}", [st[("yd", m)], *w1])
                    tu = Q.put_dma("pool", lambda e: e.dma_start(u[:, :], d["ud"][m * P:(m + 1) * P, :]),
                                   f"ur{m % 2}", w2)
                    yield
                    t = V(lambda e: e.scalar_tensor_tensor(out=y[:, :], in0=u[:, :], scalar=pc("a_d", m),
                                                           in1=y[:, :], op0=ALU.mult, op1=ALU.add), ty, tu)
                    f2.append(t)
                    t = A(lambda e: e.activation(y[:, :], y[:, :], ACT.Gelu_apprx_tanh), t, table="gelu")
                    yield
                    ts = split(m, y[:, :], [t], xrel[m])
                    f1.extend(ts)
                    txy.append(ts)
                    yield

                def ahead():
                    load_bc(0)
                    load_bc(1)
                    yield from prep()
                    yield from mats(0)
                    load_bc(2)
                    yield from mats(1)

                interleave(dense_u(), ahead())
                posts = [post(m) for m in range(8)]
                at = {2: (0, 1), 3: (0, 1), 4: (0, 1, 2, 3), 5: (2, 3), 6: (2, 3, 4, 5), 7: (4, 5, 6, 7, 4, 5, 6, 7, 6, 7)}
                scans = [scan(q) for q in range(8)]
                next(scans[0])
                next(scans[0])
                for q in range(8):
                    ma = mats(q + 2) if q < 6 else iter(())
                    if q < 6:
                        load_u(q + 2)
                    if q < 7:
                        next(scans[q + 1])
                    next(scans[q])
                    next(ma, None)
                    next(scans[q])
                    next(ma, None)
                    if q < 7:
                        next(scans[q + 1])
                    next(ma, None)
                    next(scans[q])
                    if q < 5:
                        load_bc(q + 3)
                    next(ma, None)
                    for m in at.get(q, ()):
                        next(posts[m])
                pair([("a_w_glu", 0), ("a_w_glu", 8)], txy)
                th = []
                for m in range(8):
                    bv_, tv, fv = group("a_w_glu", m, 8, xin(txy))
                    bg, tg, fg = group("a_w_glu", 8 + m, 8, xin(txy))
                    s, sw, sf = tmp.take()
                    ta = A(lambda e, s=s, bg=bg: e.activation(s[:, :], bg[:, :], ACT.Sigmoid), tg, *sw,
                           table="sigmoid")
                    fg.append(ta)
                    t1 = V(lambda e, s=s, bv_=bv_: e.tensor_tensor(s[:, :], s[:, :], bv_[:, :], ALU.mult), ta, tv)
                    fv.append(t1)
                    t1 = V(lambda e, s=s, m=m: e.tensor_tensor(s[:, :], s[:, :], xp[:, m, :], ALU.add), t1)
                    t2 = V(lambda e, s=s, m=m: e.tensor_copy(
                        h[:, m, :].rearrange("p (c s) -> p s c", s=8),
                        s[:, :].rearrange("p (s c) -> p s c", s=8)), t1)
                    sf.append(t2)
                    note(h[:, m, :], t2)
                    th.append([t2])
                xuse(tg)
                return th

        def ffn(layer, th):
            cf = ExitStack()
            with cf:
                hi = sb(cf, f"fh{layer}", [P, 13, T], R32)
                lo = sb(cf, f"fl{layer}", [P, 13, T], R32)
                gts = [sb(cf, f"fg{layer}_{i}", [P, T]) for i in range(3)]
                t0 = barrier()
                act = Slots([(hi[:, i, :], lo[:, i, :]) for i in range(13)])
                gt = Slots(gts)
                for f in act.free:
                    f.extend(t0)
                for f in gt.free:
                    f.extend(t0)
                tx = normed(rms(1e-6), f"ffn_norm{layer}")
                pair([(f"up{layer}", NF), (f"up{layer}", 0)], tx)
                cw, cbn = f"fcw{layer}", f"fcb{layer}"

                for half in range(2):
                    xa = []
                    for f in range(half * HALF, (half + 1) * HALF):
                        bg, tg, fg = group(f"up{layer}", NF + f, 8, xin(tx))
                        raw_, w1, f1 = gt.take()
                        t1 = A(lambda e, r=raw_, b=bg: e.activation(r[:, :], b[:, :], ACT.Copy), tg, *w1)
                        fg.append(t1)
                        bv_, tv, fv = group(f"up{layer}", f, 8, xin(tx))
                        g, w2, f2 = tmp.take()
                        t2 = V(lambda e, g=g, r=raw_, f=f: e.tensor_scalar(
                            g[:, :], r[:, :], pc(cw, 2 * NF + f), pc(cbn, f), ALU.mult, ALU.add), t1, ld, *w2)
                        t3 = V(lambda e, g=g, r=raw_, f=f: e.scalar_tensor_tensor(
                            out=g[:, 1:T], in0=r[:, 0:T - 1], scalar=pc(cw, NF + f), in1=g[:, 1:T],
                            op0=ALU.mult, op1=ALU.add), t2)
                        t4 = V(lambda e, g=g, r=raw_, f=f: e.scalar_tensor_tensor(
                            out=g[:, 2:T], in0=r[:, 0:T - 2], scalar=pc(cw, f), in1=g[:, 2:T],
                            op0=ALU.mult, op1=ALU.add), t3)
                        f1.append(t4)
                        t5 = A(lambda e, g=g: e.activation(g[:, :], g[:, :], ACT.Silu), t4, table="silu")
                        t6 = V(lambda e, g=g, b=bv_: e.tensor_tensor(g[:, :], g[:, :], b[:, :], ALU.mult), t5, tv)
                        fv.append(t6)
                        (H, L), w3, f3 = act.take()
                        ts = split(0, g[:, :], [t6], w3, H, L)
                        f2.extend(ts)
                        xa.append((H, L, ts, f3))
                    for m in range(8):
                        b, t, bf = group(f"down{layer}", m, HALF, lambda k: xa[k][:3], k0=half * HALF)
                        th[m] = add_h(m, b, t, bf, th, half == 1)
                    for x in xa:
                        x[3].append(t)
                xuse(t)
                return th

        def values(name, c0, tx, Vt, tv_w):
            out = []
            for half in range(2):
                bs = [bank.take() for _ in range(4)]
                for u in range(4):
                    WH, WL, t1, t2, wf = weights((name, "N", c0 + half * 512, 2 * u, 2 * u + 2), 1024)
                    for kk_ in range(2):
                        k = 2 * u + kk_
                        for tt_ in range(4):
                            b, bw, bf = bs[tt_]
                            for n, (X, W) in enumerate(((xh, WH), (xl, WH), (xh, WL))):
                                last = k == 7 and n == 2
                                t = PE(lambda e, b=b, X=X, W=W, k=k, kk_=kk_, tt_=tt_, n=n: e.matmul(
                                    b[:, :], X[:, k, tt_ * P:(tt_ + 1) * P], W[:, kk_ * 512:(kk_ + 1) * 512],
                                    start=(k == 0 and n == 0), stop=(k == 7 and n == 2)),
                                    t1, t2, *tx[k], *(bw if k == 0 and n == 0 else []),
                                    inc=last or (kk_ == 1 and tt_ == 3 and n == 2))
                            if last:
                                bs[tt_] = (b, t, bf)
                    wf.append(t)
                for tt_ in range(4):
                    b, t, bf = bs[tt_]
                    t2 = A(lambda e, b=b, tt_=tt_, half=half: e.activation(
                        Vt[:, tt_, half * 512:(half + 1) * 512], b[:, :], ACT.Copy), t, *tv_w)
                    bf.append(t2)
                    out.append(t2)
            return out, t

        def att1(th):
            ca = ExitStack()
            with ca:
                kT = sb(ca, "kT", [P, 8, T])
                qT = sb(ca, "qT", [P, 8, T])
                Vt = sb(ca, "Vt", [P, 4, D])
                spb = [(sb(ca, f"sph{i}", [P, 1280], R32), sb(ca, f"spl{i}", [P, 1280], R32)) for i in range(2)]
                tri = sb(ca, "tri", [P, 2, P], R32)
                wwb = [sb(ca, f"ww{i}", [P, 1280]) for i in range(2)]
                idb = sb(ca, "idb", [P, P], BF16)
                mkb = sb(ca, "mkb", [P, P], BF16)
                t0 = barrier()
                V(lambda e: e.tensor_copy(idb[:, :], cc("ident")), ld, *t0)
                A(lambda e: e.activation(tri[:, 0, :], cc("ntri"), ACT.Copy), ld, *t0)
                ttri = A(lambda e: e.activation(tri[:, 1, :], cc("nones"), ACT.Copy), ld, *t0)
                tmk = V(lambda e: e.tensor_scalar(mkb[:, :], cc("ntri"), 1e30, None, ALU.mult), ld)

                def head_norm(dst, m, b, t, bf, gname, scale):
                    t1 = A(lambda e: e.activation(dst[:, m, :], b[:, :], ACT.Copy), t, *t0)
                    bf.append(t1)
                    b2, t2, f2 = square_sum([(dst[:, m, :], [t1])], cc("bd64"))
                    y, t3, yf = rsqrt(b2, t2, f2, 64, 1e-6)
                    t4 = V(lambda e: e.scalar_tensor_tensor(out=dst[:, m, :], in0=dst[:, m, :],
                                                            scalar=pc(gname), in1=y[:, :],
                                                            op0=ALU.mult, op1=ALU.mult), t3)
                    yf.append(t4)
                    if scale:
                        t4 = V(lambda e: e.tensor_scalar(dst[:, m, :], dst[:, m, :], scale, None, ALU.mult), t4)
                    return t4

                trs = rms(1e-6)
                tx = normed(trs, "kv_norm")
                pair([("w_kv", 0), ("w_kv", 1)], tx)
                tk = []
                for m in range(8):
                    b, t, bf = group("w_kv", m, 8, xin(tx))
                    tk.append(head_norm(kT, m, b, t, bf, "k_norm", None))
                tv, t = values("w_kv", D, tx, Vt, t0)
                xuse(t)
                tx = normed(trs, "b_norm")
                pair([("b_w_q", 0), ("b_w_q", 1)], tx)
                tq = []
                for m in range(8):
                    b, t, bf = group("b_w_q", m, 8, xin(tx))
                    tq.append(head_norm(qT, m, b, t, bf, "q_norm", 0.125))
                xuse(t)

                PL = {0: (0, 0), 1: (1, 0), 3: (1, 384), 2: (2, 0)}
                OF = {0: 0, 1: 512, 3: 896, 2: 1024}
                N = {j: T - P * j for j in range(4)}
                sps, wws = Slots(spb), Slots(wwb)
                for s_ in (sps, wws):
                    for f in s_.free:
                        f.extend(t0)
                txo = []
                st = {}

                def scores(hd):
                    r = slice(64 * (hd % 2), 64 * (hd % 2) + 64)
                    m = hd // 2
                    bs = [bank.take() for _ in range(3)]
                    for j in (0, 1, 3, 2):
                        bi, o = PL[j]
                        b, bw, bf = bs[bi]
                        t = PE(lambda e, b=b, o=o, j=j, r=r, m=m: e.matmul(
                            b[:, o:o + N[j]], kT[r, m, j * P:(j + 1) * P], qT[r, m, j * P:T],
                            start=(o == 0), stop=False, skip_group_check=True),
                            tk[m], tq[m], *(bw if o == 0 else []))
                        t = PE(lambda e, b=b, o=o: e.matmul(
                            b[:, o:o + P], idb[:, :], mkb[:, :], start=False, stop=False, skip_group_check=True),
                            tmk, inc=True)
                        bs[bi] = b, t, bf
                    parts = sps.take()
                    st[hd] = bs, parts, []

                def softplus(hd, bi):
                    bs, parts, out = st[hd]
                    o, n = ((0, 512), (512, 512), (1024, 256))[bi]
                    b, t, _ = bs[bi]
                    s, sw, sf = tmp.take()
                    t1 = A(lambda e: e.activation(s[:, 0:n], b[:, 0:n], ACT.Abs), t, *sw)
                    t2 = A(lambda e: e.activation(s[:, 0:n], s[:, 0:n], ACT.Exp, scale=-1.0), t1, table="log_exp")
                    t3 = A(lambda e: e.activation(s[:, 0:n], s[:, 0:n], ACT.Ln, bias=1.0), t2, table="log_exp")
                    t4 = V(lambda e: e.scalar_tensor_tensor(
                        out=s[:, 0:n], in0=b[:, 0:n], scalar=0.0, in1=s[:, 0:n], op0=ALU.max, op1=ALU.add), t3)
                    out.append((s, sf, t4, o, n))

                late = {}

                def halves(hd, bi):
                    bs, ((sph, spl), w, f), out = st[hd]
                    for s, sf, t4, o, n in out[bi:bi + 1]:
                        t5 = V(lambda e, s=s, n=n, o=o: e.tensor_copy(sph[:, o:o + n], s[:, 0:n]), t4, *w)
                        t6 = V(lambda e, s=s, n=n, o=o: e.tensor_tensor(
                            spl[:, o:o + n], s[:, 0:n], sph[:, o:o + n].bitcast(F32), ALU.subtract), t5, *w)
                        sf.append(t6)
                        late[hd] = late.get(hd, []) + [t4, t5, t6]

                def sums(hd):
                    bs, (sp, _, f), _ = st[hd]
                    tg = late[hd]
                    for i in range(4):
                        bi, o = PL[i]
                        b = bs[bi][0]
                        for j in range(i, 4):
                            oo = o + P * (j - i)
                            for part in range(2):
                                t = PE(lambda e, b=b, oo=oo, j=j, i=i, part=part: e.matmul(
                                    b[:, oo:oo + N[j]], tri[:, int(j != i), :], sp[part][:, OF[j]:OF[j] + N[j]],
                                    start=False, stop=(j == 3 and part == 1), skip_group_check=True),
                                    ttri, *tg, inc=True)
                    f.append(t)
                    st[hd] = bs, t

                def weigh(hd):
                    bs, t = st[hd]
                    ww, w, f2 = wws.take()
                    for bi, (o, n) in enumerate(((0, 512), (512, 512), (1024, 256))):
                        b, _, bf = bs[bi]
                        t1 = A(lambda e, b=b, n=n, o=o: e.activation(ww[:, o:o + n], b[:, 0:n], ACT.Exp), t, *w, table="log_exp")
                        bf.append(t1)
                    st[hd] = (ww, f2, [t1])

                def mix(hd):
                    ww, f, tg = st[hd]
                    r = slice(64 * (hd % 2), 64 * (hd % 2) + 64)
                    if hd % 2 == 0:
                        st["o"] = bank.take()
                    b, bw, bf = st["o"]
                    for j in range(4):
                        t = PE(lambda e, j=j, b=b, r=r, hd=hd: e.matmul(
                            b[r, j * P:T], Vt[:, j, hd * 64:(hd + 1) * 64], ww[:, OF[j]:OF[j] + N[j]],
                            start=(j == 0), stop=(j == 3), skip_group_check=True),
                            *tg, *tv, *(bw if j == 0 and hd % 2 == 0 else []), inc=(j == 3))
                    f.append(t)
                    if hd % 2:
                        m = hd // 2
                        a = A(lambda e: e.activation(xh[:, m, :], b[:, :], ACT.Copy), t, *xrel[m])
                        v = V(lambda e: e.tensor_tensor(xl[:, m, :], b[:, :], xh[:, m, :].bitcast(F32),
                                                        ALU.subtract), a, *xrel[m])
                        bf.append(v)
                        txo.append([a, v])

                for s in range(18):
                    if s < 16:
                        scores(s)
                    if 1 <= s < 17:
                        sums(s - 1)
                    if s < 16:
                        softplus(s, 0)
                    if s < 16:
                        halves(s, 0)
                    if s < 16:
                        softplus(s, 1)
                    if s < 16:
                        halves(s, 1)
                    if s < 16:
                        softplus(s, 2)
                    if s < 16:
                        halves(s, 2)
                    if 1 <= s < 17:
                        weigh(s - 1)
                    if s >= 2:
                        mix(s - 2)
                for m in range(8):
                    b, t, bf = group("b_w_o", m, 8, xin(txo))
                    th[m] = add_h(m, b, t, bf, th)
                xuse(t)
                return th

        def mamba(th):
            cm = ExitStack()
            with cm:
                xs = [sb(cm, f"mx{i}", [P, 2, T]) for i in range(2)]
                xt = [sb(cm, f"mxt{i}", [P, 4, 256]) for i in range(2)]
                zs = [sb(cm, f"mz{i}", [P, 2, T]) for i in range(2)]
                cbs = [sb(cm, f"mcb{i}", [P, 10, P]) for i in range(2)]
                Eb = [sb(cm, f"mE{i}", [P, 10, P]) for i in range(3)]
                bcT = [sb(cm, f"mbc{i}", [P, T]) for i in range(2)]
                uh = sb(cm, "muh", [P, 8, T], R32)
                ul = sb(cm, "mul", [P, 8, T], R32)
                dtk = sb(cm, "dtk", [P, 4, 32])
                adt = sb(cm, "adt", [P, 4, 32])
                aneg = sb(cm, "aneg", [P, 32])
                bias = sb(cm, "mbias", [P, 10, 32])
                acsH = sb(cm, "acsH", [32, T], R32)
                acsL = sb(cm, "acsL", [32, T], R32)
                pick = sb(cm, "pick", [32, 32], R32)
                t0 = barrier()
                E_, cbS, bcS, uS = Slots(Eb), Slots(cbs), Slots(bcT), Slots(list(range(8)))
                for s_ in (E_, cbS, bcS, uS):
                    for f in s_.free:
                        f.extend(t0)
                gS = Slots([0, 1])
                for f in gS.free:
                    f.extend(t0)
                half = par[:, PCOL["m_cw"][0]:PCOL["m_cb"][0] + 32]
                tcw = V(lambda e: e.tensor_scalar(half, half, 0.5, None, ALU.mult), ld)
                tx = normed(rms(1e-5), "m_norm")

                bk, bm, br, by = parted(bank, 3, 2, 1, 2)

                pair([("a_w_in_2", 32), ("a_w_in_2", 40)], tx, bk)

                WH, WL, w1, w2, wf = weights(("a_w_in_2", "N32", 6144, 0, 8), 256)
                b, bw, bf = bm.take()
                for tb in range(4):
                    for k in range(8):
                        for n, (X, W) in enumerate(((xh, WH), (xl, WH), (xh, WL))):
                            t = PE(lambda e, tb=tb, k=k, n=n, X=X, W=W, b=b: e.matmul(
                                b[:, tb * 32:(tb + 1) * 32], X[:, k, tb * P:(tb + 1) * P],
                                W[:, k * 32:(k + 1) * 32], start=(tb == 0 and k == 0 and n == 0),
                                stop=(k == 7 and n == 2), skip_group_check=True),
                                w1, w2, *tx[k], *(bw if tb == 0 and k == 0 and n == 0 else []),
                                inc=(k == 7 and n == 2))
                wf.append(t)
                s, sw, sf = tmp.take()
                xb = s[:, 0:128].rearrange("p (t h) -> p t h", t=4)
                xe = s[:, 128:256].rearrange("p (t h) -> p t h", t=4)
                t = V(lambda e, b=b: e.tensor_tensor(xb, b[:, 0:128].rearrange("p (t h) -> p t h", t=4),
                                                pc("m_dtb", 0, 32).unsqueeze(1).broadcast_to([P, 4, 32]),
                                                ALU.add), t, ld, *sw)
                bf.append(t)
                t = A(lambda e: e.activation(xe, xb, ACT.Abs), t)
                t = A(lambda e: e.activation(xe, xe, ACT.Exp, scale=-1.0), t, table="log_exp")
                t = A(lambda e: e.activation(xe, xe, ACT.Ln, bias=1.0), t, table="log_exp")
                t = V(lambda e: e.scalar_tensor_tensor(out=dtk[:, :, :], in0=xb, scalar=0.0, in1=xe,
                                                       op0=ALU.max, op1=ALU.add), t, *t0)
                sf.append(t)
                tdt = t
                t = A(lambda e: e.activation(aneg[:, :], pc("m_al", 0, 32), ACT.Exp), ld, *t0, table="log_exp")
                t = V(lambda e: e.scalar_tensor_tensor(
                    out=adt[:, :, :], in0=dtk[:, :, :], scalar=-1.0,
                    in1=aneg[:, :].unsqueeze(1).broadcast_to([P, 4, 32]), op0=ALU.mult, op1=ALU.mult), t, tdt)
                tadt = t
                OFF = {}
                n = 4
                for j in range(4):
                    for i in range(j + 1, 4):
                        OFF[(j, i)] = n
                        n += 1
                b, bw, bf = bm.take()
                first = True
                for j in range(4):
                    t = PE(lambda e, j=j, b=b, first=first: e.matmul(
                        b[:, j * 32:(j + 1) * 32], cc("nupper"), adt[:, j, :], start=first, stop=True,
                        skip_group_check=True), tadt, *(bw if first else []), inc=True)
                    first = False
                for (j, i), n in OFF.items():
                    mids = list(range(j + 1, i))
                    t = PE(lambda e, j=j, n=n, mids=mids, b=b: e.matmul(
                        b[:, n * 32:(n + 1) * 32], cc("slower"), adt[:, j, :], start=False, stop=not mids,
                        skip_group_check=True), inc=True)
                    for m_ in mids:
                        t = PE(lambda e, n=n, m_=m_, mids=mids, b=b: e.matmul(
                            b[:, n * 32:(n + 1) * 32], cc("ones"), adt[:, m_, :], start=False,
                            stop=(m_ == mids[-1]), skip_group_check=True), inc=True)
                tbias = A(lambda e, b=b: e.activation(bias[:, :, :], b[:, 0:320].rearrange("p (n h) -> p n h", h=32),
                                                 ACT.Copy), t, *t0)
                bf.append(tbias)
                b, bw, bf = bm.take()
                for j in range(4):
                    t = PE(lambda e, j=j, b=b: e.matmul(
                        b[0:32, j * P:(j + 1) * P], adt[:, j, :], cc("upper"), start=(j == 0), stop=True,
                        skip_group_check=True), tadt, *(bw if j == 0 else []), inc=(j == 3))
                tacs = A(lambda e, b=b: e.activation(acsH[:, :], b[0:32, :], ACT.Copy), t, *t0)
                tacs = V(lambda e, b=b: e.tensor_tensor(acsL[:, :], b[0:32, :], acsH[:, :].bitcast(F32),
                                                        ALU.subtract), tacs, *t0)
                bf.append(tacs)
                tpick = V(lambda e: e.tensor_copy(pick[:, :], cc("ident")[0:32, 0:32]), ld, *t0)

                def conv(ch, b, t, bf, dst, wdst):
                    t2 = A(lambda e: e.activation(dst, b[:, :], ACT.Identity, scale=pc("m_cw", 3 * 32 + ch),
                                                  bias=pc("m_cb", ch)), t, tcw, *wdst)
                    for j in range(1, 4):
                        t2 = V(lambda e, j=j: e.scalar_tensor_tensor(
                            out=dst[:, j:T], in0=b[:, 0:T - j], scalar=pc("m_cw", (3 - j) * 32 + ch),
                            in1=dst[:, j:T], op0=ALU.mult, op1=ALU.add), t2)
                    bf.append(t2)

                    def finish():
                        r, w1, f1 = tmp.take()
                        ta = A(lambda e: e.activation(r[:, :], dst, ACT.Tanh), t2, *w1, table="tanh")
                        tb = G(lambda e: e.tensor_tensor(r[:, :], r[:, :], dst, ALU.mult), ta)
                        tb = G(lambda e: e.tensor_tensor(dst, dst, r[:, :], ALU.add), tb)
                        f1.append(tb)
                        return tb
                    return finish

                gst = {}

                def dense_g(g):
                    def conv_later(tile, ch, dst, wdst):
                        b, t, bf = group("a_w_in_2", tile, 8, xin(tx), ring=bk)
                        return lambda: conv(ch, b, t, bf, dst, wdst)
                    Bt, w1, fB = bcS.take()
                    cB = conv_later(32 + g, 16 + g, Bt[:, :], w1)
                    yield
                    Ct, w2, fC = bcS.take()
                    fin_b = cB()
                    cC = conv_later(40 + g, 24 + g, Ct[:, :], w2)
                    yield
                    gi, gw, gf = gS.take()
                    X, XT, Z = xs[gi], xt[gi], zs[gi]
                    tX = []
                    tB = fin_b()
                    fin_c = cC()
                    c0 = conv_later(16 + 2 * g, 2 * g, X[:, 0, :], gw)
                    yield
                    tC = fin_c()
                    fin_0 = c0()
                    c1 = conv_later(17 + 2 * g, 2 * g + 1, X[:, 1, :], gw)
                    yield
                    tX.append(fin_0())
                    fin_1 = c1()
                    zb = [group("a_w_in_2", 2 * g, 8, xin(tx), ring=bk)]
                    cb, w3, fcb = cbS.take()
                    tcb = []
                    pieces_ = [[(j, j, j * P) for j in range(4)],
                               [(0, 1, 0), (0, 2, P), (0, 3, 2 * P)],
                               [(1, 2, 0), (1, 3, P), (2, 3, 2 * P)]]
                    for pi, pcs in enumerate(pieces_):
                        bb, bw, bbf = bm.take()
                        runs = []
                        for j, i_, o in pcs:
                            if pi and runs and runs[-1][0] == j:
                                runs[-1][2] += 1
                            else:
                                runs.append([j, i_, 1, o])
                        for n, (j, i_, cnt, o) in enumerate(runs):
                            t = PE(lambda e, j=j, i_=i_, cnt=cnt, o=o, n=n, bb=bb: e.matmul(
                                bb[:, o:o + cnt * P], Bt[:, j * P:(j + 1) * P],
                                Ct[:, i_ * P:(i_ + cnt) * P], start=(n == 0), stop=True,
                                skip_group_check=True), tB, tC, *(bw if n == 0 else []),
                                inc=(n == len(runs) - 1))
                        n0 = (0, 4, 7)[pi]
                        n1 = (4, 7, 10)[pi]
                        tc = A(lambda e, bb=bb, n0=n0, n1=n1: e.activation(
                            cb[:, n0:n1, :], bb[:, 0:(n1 - n0) * P].rearrange("p (n c) -> p n c", c=P),
                            ACT.Copy), t, *w3)
                        bbf.append(tc)
                        tcb.append(tc)
                    fB.append(t)
                    fC.append(t)
                    yield
                    tXT = []
                    tZ = []

                    def token_major(i):
                        bb, bw, bbf = bm.take()
                        for tb in range(4):
                            tp = PE(lambda e, tb=tb: e.transpose(
                                bb[:, tb * P:(tb + 1) * P], X[:, i, tb * P:(tb + 1) * P], cc("ident")),
                                tX[i], *(bw if tb == 0 else []), inc=(tb == 3))

                        def scaled():
                            for hh in range(2):
                                hd = 4 * g + 2 * i + hh
                                t2 = V(lambda e, hh=hh, hd=hd: e.tensor_tensor(
                                    XT[:, :, (2 * i + hh) * 64:(2 * i + hh + 1) * 64],
                                    bb[:, :].rearrange("p (t c) -> p t c", t=4)[:, :, hh * 64:(hh + 1) * 64],
                                    dtk[:, :, hd:hd + 1].broadcast_to([P, 4, 64]), ALU.mult), tp, tdt, *gw)
                            bbf.append(t2)
                            tXT.append(t2)
                        return scaled

                    def gate(i):
                        b, t, bf = zb[i]
                        r, w1, f1 = tmp.take()
                        t1 = A(lambda e: e.activation(r[:, :], b[:, :], ACT.Tanh, scale=0.5), t, *w1,
                               table="tanh")
                        t2 = V(lambda e: e.scalar_tensor_tensor(
                            out=Z[:, i, :], in0=r[:, :], scalar=1.0, in1=b[:, :], op0=ALU.add, op1=ALU.mult),
                            t1, *gw)
                        bf.append(t2)
                        f1.append(t2)
                        tZ.append(t2)
                    gate(0)
                    tX.append(fin_1())
                    zb.append(group("a_w_in_2", 2 * g + 1, 8, xin(tx), ring=bk))
                    if g == 7:
                        xuse(zb[1][1])
                    sc0 = token_major(0)
                    yield
                    sc0()
                    token_major(1)()
                    gate(1)
                    gst[g] = (X, XT, Z, cb, tX, tXT, tZ, tcb, fcb, gf)
                    yield

                txu = {}
                est = {}

                def spread(hd):
                    rb, rw, rf = br.take()
                    for part, a in enumerate((acsH, acsL)):
                        t = PE(lambda e, part=part, a=a: e.matmul(
                            rb[:, :], pick[:, hd:hd + 1].broadcast_to([32, P]), a[:, :], start=(part == 0),
                            stop=(part == 1)), tpick, tacs, *rw, inc=(part == 1))
                    est[hd] = rb, t, rf

                def decay(hd):
                    rb, t, rf = est[hd]
                    E, ew, ef = E_.take()
                    R = rb[:, :].rearrange("p (i c) -> p i c", i=4)
                    for j in range(4):
                        t1 = V(lambda e, j=j: e.scalar_tensor_tensor(
                            out=E[:, j, :], in0=R[:, j, :], scalar=bias[:, j, hd:hd + 1], in1=cc("low"),
                            op0=ALU.add, op1=ALU.add), t, tbias, *ew)
                    for n0, cnt, i0 in ((4, 3, 1), (7, 2, 2), (9, 1, 3)):
                        for i in range(cnt):
                            ta = A(lambda e, n=n0 + i, i=i0 + i: e.activation(
                                E[:, n, :], R[:, i, :], ACT.Exp, bias=bias[:, n, hd:hd + 1]),
                                t1, tbias, *ew, table="exp")
                    rf.append(ta)
                    ta = A(lambda e: e.activation(E[:, 0:4, :], E[:, 0:4, :], ACT.Exp), t1, table="exp")
                    est[hd] = (E, [ta], ef)

                def ssd(g):
                    X, XT, Z, cb, tX, tXT, tZ, tcb, fcb, gf = gst[g]
                    us, ybs, ty = [], {}, {}

                    def update(i):
                        yb, yf = ybs[i]
                        t6 = V(lambda e: e.scalar_tensor_tensor(
                            out=X[:, i, :], in0=X[:, i, :], scalar=pc("m_d", 2 * g + i), in1=yb[:, :],
                            op0=ALU.mult, op1=ALU.add), ty[i], tX[i])
                        yf.append(t6)
                        us.append(V(lambda e: e.scalar_tensor_tensor(
                            out=X[:, i, :], in0=X[:, i, :], scalar=0.5, in1=Z[:, i, :], op0=ALU.mult,
                            op1=ALU.mult), t6, tZ[i]))

                    for r in range(4):
                        hd = 4 * g + r
                        if hd < 31:
                            decay(hd + 1)
                        if r == 2:
                            update(0)
                        yield
                        E, t2, ef = est[hd]
                        t4 = V(lambda e, E=E: e.tensor_tensor(E[:, 0:6, :], E[:, 0:6, :], cb[:, 0:6, :], ALU.mult),
                               *t2, *tcb)
                        tq4 = G(lambda e, E=E: e.tensor_tensor(E[:, 6:10, :], E[:, 6:10, :], cb[:, 6:10, :],
                                                               ALU.mult), *t2, *tcb)
                        if hd < 30:
                            spread(hd + 2)
                        if r % 2 == 0:
                            yb, yw, yf = by.take()
                        ybs[r // 2] = yb, yf
                        ro_ = slice(64 * (r % 2), 64 * (r % 2) + 64)
                        for j in range(4):
                            for (o, cnt, n0) in ((j, 1, j), (j + 1, 3 - j, OFF.get((j, j + 1)))):
                                if cnt == 0:
                                    continue
                                t5 = PE(lambda e, j=j, o=o, cnt=cnt, n0=n0, yb=yb, E=E, r=r, ro_=ro_: e.matmul(
                                    yb[ro_, o * P:(o + cnt) * P], XT[:, j, r * 64:(r + 1) * 64],
                                    E[:, n0:n0 + cnt, :].rearrange("p n c -> p (n c)"),
                                    start=(j == 0 and o == 0), stop=(j == min(o + cnt - 1, 3)),
                                    skip_group_check=True), t4, tq4, tXT[r // 2],
                                    *(yw if j == 0 and o == 0 and r % 2 == 0 else []), inc=(j == 3))
                        ef.append(t5)
                        ty[r // 2] = t5
                        yield
                    update(1)
                    fcb.extend([t4, tq4])
                    sq, w1, f1 = tmp.take()
                    sq2, w2, f2 = tmp.take()
                    t = G(lambda e: e.tensor_tensor(sq[:, :], X[:, 0, :], X[:, 0, :], ALU.mult), us[0], *w1)
                    ta = A(lambda e: e.activation(sq2[:, :], X[:, 1, :], ACT.Square), us[1], *w2)
                    t = G(lambda e: e.tensor_tensor(sq[:, :], sq[:, :], sq2[:, :], ALU.add), t, ta)
                    f2.append(t)
                    yield
                    b, bw, bf = by.take()
                    t = PE(lambda e: e.matmul(b[:, :], cc("ones"), sq[:, :], start=True, stop=True), t, ld, *bw,
                           inc=True)
                    f1.append(t)
                    yield
                    newton = rsqrt_start(b, t, bf, 256, 1e-5)
                    yield
                    y, ty, yf = newton()
                    for i in range(2):
                        t8 = V(lambda e, i=i, y=y, g=g: e.scalar_tensor_tensor(
                            out=X[:, i, :], in0=X[:, i, :], scalar=pc("m_gn", 2 * g + i), in1=y[:, :],
                            op0=ALU.mult, op1=ALU.mult), ty)
                        kslot, uw, uf = uS.take()
                        ts = split(0, X[:, i, :], [t8], uw, uh[:, kslot, :], ul[:, kslot, :], G)
                        gf.extend(ts)
                        txu[2 * g + i] = (uh[:, kslot, :], ul[:, kslot, :], ts, uf)
                    yf.append(t8)
                    gf.append(t5)
                    yield

                def out_part(q, ms):
                    late = None
                    for m in ms:
                        if late:
                            th[late[0]] = add_h(*late, th, q == 3)
                        b, t, bf = group("a_w_out_2", m, 4, lambda k: txu[4 * q + k][:3], k0=4 * q, ring=bk)
                        if m == 7:
                            for k in range(4):
                                txu[4 * q + k][3].append(t)
                        late = m, b, t, bf
                        yield
                    th[late[0]] = add_h(*late, th, q == 3)
                    yield

                interleave(dense_g(0))
                spread(0)
                decay(0)
                spread(1)
                for g in range(8):
                    q = g // 2 - 1
                    blend((ssd(g), 13), *([(dense_g(g + 1), 7)] if g < 7 else []),
                          *([(out_part(q, range(4 * (g % 2), 4 * (g % 2) + 4)), 5)] if q >= 0 else []))
                interleave(out_part(3, range(8)))
                rejoin(bank, bk, bm, br, by)
                return th

        def att2(th):
            ca = ExitStack()
            with ca:
                kT = sb(ca, "k2T", [P, 8, T])
                qT = sb(ca, "q2T", [P, 8, T])
                Vt = sb(ca, "V2t", [P, 4, D])
                oB = qT
                Sb = Slots([sb(ca, f"S{i}", [P, 2, T]) for i in range(2)])
                wb = Slots([sb(ca, f"w2_{i}", [P, T]) for i in range(2)])
                wT = Slots([sb(ca, f"wT{i}", [P, 4, 4, P]) for i in range(2)])
                gS2 = Slots([sb(ca, f"gate2_{i}", [P, T]) for i in range(4)])
                small = sb(ca, "small2", [P, 16, 8])
                sml = Slots([small[:, i, :] for i in range(16)])
                lam = sb(ca, "lam", [P, 8])
                t0 = barrier()
                for s_ in (Sb, wb, wT, sml, gS2):
                    for f in s_.free:
                        f.extend(t0)

                s, sw, sf = tmp.take()
                ll = pc("lam", 0, 256).rearrange("p (a b c) -> p a b c", a=2, b=2)
                pr = s[:, 0:128].rearrange("p (a c) -> p a c", a=2)
                t = V(lambda e: e.tensor_tensor(pr, ll[:, :, 0, :], ll[:, :, 1, :], ALU.mult), ld, *sw)
                t = V(lambda e: e.tensor_reduce(lam[:, 0:2], pr, AX.X, ALU.add), t, *t0)
                sf.append(t)
                t = A(lambda e: e.activation(lam[:, 2:4], lam[:, 0:2], ACT.Exp), t, table="log_exp")
                t = V(lambda e: e.tensor_tensor(lam[:, 4:5], lam[:, 3:4], lam[:, 2:3], ALU.subtract), t)
                tlam = V(lambda e: e.tensor_scalar(lam[:, 5:6], lam[:, 4:5], -LAMBDA_INIT, None, ALU.add), t)
                tsub = V(lambda e: e.tensor_scalar(lam[:, 6:7], pc("sub_g"), 0.5 * (1.0 - LAMBDA_INIT), None, ALU.mult),
                         *t0, ld)

                trs = rms(1e-5)
                tx = normed(trs, "kv2_norm")
                pair([("w_kv_2", 0), ("w_kv_2", 1)], tx)
                tk, tq = [], []
                for m in range(8):
                    b, t, bf = group("w_kv_2", m, 8, xin(tx))
                    t1 = A(lambda e, b=b, m=m: e.activation(kT[:, m, :], b[:, :], ACT.Copy), t, *t0)
                    bf.append(t1)
                    tk.append(t1)
                tv, t = values("w_kv_2", D, tx, Vt, t0)
                xuse(t)
                tx = normed(trs, "b2_norm")
                bd, bs, bt, bo = parted(bank, 2, 4, 1, 1)
                pair([("b_w_in_2", 0), ("b_w_in_2", 1)], tx, bd)
                gates = {}
                done = []

                def query(m):
                    b, t, bf = group("b_w_in_2", m, 8, xin(tx), ring=bd)
                    yield
                    t1 = A(lambda e: e.activation(qT[:, m, :], b[:, :], ACT.Copy, scale=0.125), t, *t0)
                    bf.append(t1)
                    tq.append(t1)
                    yield

                def gate(hd):
                    b, t, bf = group("b_w_in_2", 8 + hd, 8, xin(tx), ring=bd)
                    if hd == 7:
                        xuse(t)
                        done.append(-1)
                    yield
                    s, sw, sf = gS2.take()
                    t1 = A(lambda e: e.activation(s[:, :], b[:, :], ACT.Tanh, scale=0.5), t, *sw, table="tanh")
                    t2 = V(lambda e: e.scalar_tensor_tensor(out=s[:, :], in0=s[:, :], scalar=1.0, in1=b[:, :],
                                                            op0=ALU.add, op1=ALU.mult), t1)
                    bf.append(t2)
                    gates[hd] = (s, t2, sf)
                    yield

                pairs = [(hd, i) for hd in range(8) for i in range(4)]
                st = {}
                txo = {}
                wts = {}

                def scores(n):
                    hd, i = pairs[n]
                    nk = P * (i + 1)
                    out = []
                    for c in range(2):
                        b, bw, bf = bs.take()
                        r = slice(64 * c, 64 * c + 64)
                        t = PE(lambda e, b=b, r=r: e.matmul(
                            b[:, 0:nk], qT[r, hd, i * P:(i + 1) * P], kT[r, hd, 0:nk], start=True,
                            stop=True), tq[hd], tk[hd], *bw, inc=True)
                        out.append((b, t, bf))
                    st[n] = out

                def exps(n):
                    hd, i = pairs[n]
                    nk = P * (i + 1)
                    slope = 2.0 ** (-(hd + 1))
                    S_, sw, sf = Sb.take()
                    for c, (b, t, bf) in enumerate(st[n]):
                        t1 = V(lambda e, b=b, c=c: e.scalar_tensor_tensor(
                            out=S_[:, c, 0:nk], in0=cc("alibi")[:, T - nk:T], scalar=slope, in1=b[:, 0:nk],
                            op0=ALU.mult, op1=ALU.add), t, ld, *sw)
                        bf.append(t1)
                    sv, vw, vf = sml.take()
                    t1 = V(lambda e: e.tensor_reduce(sv[:, 0:2], S_[:, :, 0:nk], AX.X, ALU.max, negate=True),
                           t1, *vw)
                    for c in range(2):
                        t2 = A(lambda e, c=c: e.activation(
                            S_[:, c, 0:nk], S_[:, c, 0:nk], ACT.Exp, bias=sv[:, c:c + 1],
                            accum_out=sv[:, 2 + c:3 + c]), t1, table="exp")
                    st[n] = S_, sv, t2, sf, vf

                def combine(n):
                    hd, i = pairs[n]
                    nk = P * (i + 1)
                    S_, sv, t2, sf, vf = st[n]
                    t3 = V(lambda e: e.reciprocal(sv[:, 4:6], sv[:, 2:4]), t2)
                    t4 = V(lambda e: e.tensor_tensor(sv[:, 6:7], sv[:, 5:6], lam[:, 5:6], ALU.mult), t3, tlam)
                    w_, w2, f2 = wb.take()
                    t5 = V(lambda e: e.tensor_scalar(w_[:, 0:nk], S_[:, 0, 0:nk], sv[:, 4:5], None, ALU.mult),
                           t4, *w2)
                    t6 = V(lambda e: e.scalar_tensor_tensor(
                        out=w_[:, 0:nk], in0=S_[:, 1, 0:nk], scalar=sv[:, 6:7], in1=w_[:, 0:nk],
                        op0=ALU.mult, op1=ALU.add), t5)
                    sf.append(t6)
                    vf.append(t6)
                    st[n] = w_, t6, f2

                def turn(n):
                    hd, i = pairs[n]
                    w_, t6, f2 = st[n]
                    b, bw, bf = bt.take()
                    for j in range(i + 1):
                        t7 = PE(lambda e, j=j: e.transpose(
                            b[:, j * P:(j + 1) * P], w_[:, j * P:(j + 1) * P], cc("ident")),
                            t6, *(bw if j == 0 else []), inc=(j == i))
                    f2.append(t7)
                    st[n] = b, t7, bf

                def keep(n):
                    hd, i = pairs[n]
                    b, t7, bf = st[n]
                    if i == 0:
                        wts[hd] = wT.take()
                    wt, ww, wf = wts[hd]
                    t8 = A(lambda e: e.activation(
                        wt[:, 0:i + 1, i, :], b[:, 0:(i + 1) * P].rearrange("p (j c) -> p j c", c=P), ACT.Copy),
                        t7, *ww)
                    bf.append(t8)
                    return t8

                def tail(hd, tT):
                    wt, _, wf = wts[hd]
                    ob, ow, of = bo.take()
                    for j in range(4):
                        t = PE(lambda e, j=j: e.matmul(
                            ob[:, j * P:T], Vt[:, j, hd * P:(hd + 1) * P],
                            wt[:, j, j:4, :].rearrange("p n c -> p (n c)"),
                            start=(j == 0), stop=(j == 3), skip_group_check=True),
                            tT, *tv, *(ow if j == 0 else []), inc=(j == 3))
                    wf.append(t)
                    yield
                    o = oB[:, hd, :]
                    t1 = A(lambda e: e.activation(o, ob[:, :], ACT.Copy), t)
                    of.append(t1)
                    q, qw, qf = tmp.take()
                    t = A(lambda e: e.activation(q[:, :], o, ACT.Square), t1, *qw)
                    b2, bw, bf = bo.take()
                    t = PE(lambda e: e.matmul(b2[:, :], cc("ones"), q[:, :], start=True, stop=True), t, *bw,
                           inc=True)
                    qf.append(t)
                    yield
                    newton = rsqrt_start(b2, t, bf, 128, 1e-5)
                    yield
                    y, ty, yf = newton()
                    t3 = V(lambda e: e.scalar_tensor_tensor(
                        out=o, in0=o, scalar=lam[:, 6:7], in1=y[:, :], op0=ALU.mult, op1=ALU.mult), ty, tsub)
                    yf.append(t3)
                    s, t4, sf = gates[hd]
                    t5 = V(lambda e: e.tensor_tensor(o, o, s[:, :], ALU.mult), t3, t4)
                    sf.append(t5)
                    while not done or done[-1] == n:
                        yield
                    done.append(n)
                    txo[hd] = split(hd, o, [t5], xrel[hd], eng=G)
                    yield

                def out_tile(m, k0, k1, ring=bd):
                    b, t, bf = group("b_w_out_2", m, k1 - k0, lambda k: xin(txo)(k + k0), k0=k0, ring=ring)
                    yield
                    th[m] = add_h(m, b, t, bf, th, k1 == 8)
                    yield

                running = [query(0)]
                interleave(*running)
                running = [query(1)]
                dense = [f for m in range(8) for f in ([query(m + 2)] if m < 6 else []) + [gate(m)]]
                outs = [out_tile(m, 0, 4) for m in range(8)]
                n = 0
                while n < len(pairs) + 4 or running:
                    for g in list(running):
                        if next(g, "end") == "end":
                            running.remove(g)
                    if 0 <= n - 4 < 32:
                        t = keep(n - 4)
                        if (n - 4) % 4 == 3:
                            running.append(tail((n - 4) // 4, t))
                    if 0 <= n - 1 < 32:
                        exps(n - 1)
                    if 0 <= n - 2 < 32:
                        combine(n - 2)
                    if n < 32:
                        scores(n)
                    if dense and n % 2 == 0:
                        g = dense.pop(0)
                        next(g)
                        running.append(g)
                    if n >= 31 and outs:
                        g = outs.pop(0)
                        next(g)
                        running.append(g)
                    if 0 <= n - 3 < 32:
                        turn(n - 3)
                    n += 1
                while outs:
                    interleave(outs.pop(0))
                rejoin(bank, bd, bs, bt, bo)
                for m in range(8):
                    interleave(out_tile(m, 4, 8, bank))
                return th

        th = [[] for _ in range(8)]
        if stages[0] != "s5":
            t = Q.put_dma("sp", lambda e: e.dma_start(h[:, :, :], d["xn"]), "ldx0", [])
            th = [[t] for _ in range(8)]
            for k in range(8):
                note(h[:, k, :], t)
        for s in stages:
            if s == "s5":
                th = s5(th)
            elif s in ("ffn0", "ffn1"):
                th = ffn(int(s[-1]), th)
            elif s == "att1":
                th = att1(th)
            elif s == "mamba":
                th = mamba(th)
            elif s == "att2":
                th = att2(th)
        for k in range(8):
            Q.dma_sem(f"out{k}")
        ov = d["out"].rearrange("(k p) t -> p k t", p=P)
        if stages[-1] == "att2":
            def store(k, s, t, f):
                f.append(Q.put_dma("sp", lambda e: e.dma_start(ov[:, k, :], s[:, :]), f"out{k}", [t]))
            normed(rms(1e-5), "fin", out=store)
        else:
            for k in range(8):
                Q.put_dma("sp", lambda e, k=k: e.dma_start(ov[:, k, :], h[:, k, :]), f"out{k}", th[k])
        Q.number()

        block = ctx.enter_context(nc.Block())

        @block.tensor
        def _(e):
            Q.play("pe", e)

        @block.scalar
        def _(e):
            Q.play("act", e)

        @block.vector
        def _(e):
            Q.play("dve", e)

        @block.gpsimd
        def _(e):
            Q.play("pool", e)

        @block.sync
        def _(e):
            Q.play("sp", e)
            for name in (*(f"out{k}" for k in range(8)), "ud0", "ud1", "kd0", "kd1", "kdz", "yd0", "yd1"):
                if name in Q.dma:
                    e.wait_ge(Q.dma[name][0], Q.dma[name][1])
    return units


def _pack(inputs):
    f = {n: np.asarray(a) for n, a in inputs.items()}

    def cols(v):
        return np.ascontiguousarray(np.reshape(v, (-1, P)).T)

    def rep(v):
        return np.broadcast_to(np.reshape(v, (1, -1)), (P, np.size(v)))

    pp = {
        "a_norm": cols(f["a_norm"]), "kv_norm": cols(f["kv_norm"]), "b_norm": cols(f["b_norm"]),
        "ffn_norm0": cols(f["ffn_norm"][0]), "ffn_norm1": cols(f["ffn_norm"][1]), "a_d": cols(f["a_d"]),
        "k_norm": np.tile(f["k_norm"].reshape(64, 1), (2, 1)), "q_norm": np.tile(f["b_q_norm"].reshape(64, 1), (2, 1)),
        "fcw0": cols(f["ffn_conv_w"][0]), "fcw1": cols(f["ffn_conv_w"][1]),
        "fcb0": cols(f["ffn_conv_b"][0]), "fcb1": cols(f["ffn_conv_b"][1]),
        "m_norm": cols(f["a_norm_g_2"]), "m_cw": cols(f["a_conv_w_2"]), "m_cb": cols(f["a_conv_b_2"]),
        "m_d": cols(np.repeat(f["a_d_skip_2"].reshape(-1), 64)), "m_gn": cols(f["a_gate_norm_g_2"]),
        "m_dtb": rep(f["a_dt_bias_2"]), "m_al": rep(f["a_a_log_2"]),
        "kv2_norm": cols(f["kv_norm_g_2"]), "b2_norm": cols(f["b_norm_g_2"]), "sub_g": cols(f["b_sub_g_2"]),
        "fin": cols(f["final_norm_g_2"]), "lam": rep(f["b_lambda_2"]),
        "lre": np.tile(f["a_lam_re"][0].T, (2, 1)), "lim": np.tile(f["a_lam_im"][0].T, (2, 1)),
        "ldt": rep(f["a_log_dt"]),
    }
    par = np.ascontiguousarray(np.concatenate([pp[n] for n, _ in PARAMS], axis=1), dtype=np.float32)
    b = [np.tile(np.transpose(f[n][0], (1, 0, 2)), (2, 1, 1)) for n in ("a_b_re", "a_b_im")]
    c = [np.tile(np.transpose(f[n][0], (2, 0, 1)), (2, 1, 1)) for n in ("a_c_re", "a_c_im")]
    bc5 = np.ascontiguousarray(np.stack(b + c, axis=1))
    xT = f["x"][0].T
    xn = np.ascontiguousarray(xT.reshape(8, P, T).transpose(1, 0, 2))
    xp = np.ascontiguousarray(xn.reshape(P, 8, 64, 8).transpose(0, 1, 3, 2).reshape(P, 8, T))
    return par, bc5, xn, xp


def _weights(inputs, units):
    src = {n: np.asarray(inputs[n][0]) for n in ("a_w_in", "a_w_glu", "b_w_q", "b_w_o", "a_w_in_2", "a_w_out_2",
                                                 "b_w_in_2", "b_w_out_2")}
    src["w_kv"] = np.asarray(inputs["w_kv"])
    src["w_kv_2"] = np.asarray(inputs["w_kv_2"])
    for i in range(2):
        src[f"up{i}"] = np.asarray(inputs["ffn_w_up"][i])
        src[f"down{i}"] = np.asarray(inputs["ffn_w_down"][i])
    width = {"N": 512, "N32": 32}
    flat = np.empty(sum(c for _, c in units) * P, np.float32)
    o = 0
    for (name, kind, m, k0, k1), cols in units:
        w = src[name]
        c0, cw = (m * P, P) if kind == "T" else (m, width[kind])
        blk = w[k0 * P:k1 * P, c0:c0 + cw].reshape(k1 - k0, P, cw).transpose(1, 0, 2)
        flat[o:o + P * cols] = blk.reshape(-1)
        o += P * cols
    return flat


def total_weights(stages):
    n = {"s5": 3 * D * D, "ffn0": 3 * D * F_FF, "ffn1": 3 * D * F_FF, "att1": 4 * D * D,
         "mamba": D * 6176 + 2 * D * D, "att2": 5 * D * D}
    return sum(n[s] for s in stages)


def make(nc, stages=STAGES):
    d = {}
    for name, shape in (("w", [total_weights(stages)]), ("par", [P, NPAR]), ("con", [P, NCON]),
                        ("bc5", [P, 4, G5, 16]), ("xn", [P, 8, T]), ("xp", [P, 8, T])):
        if (name in ("xp", "bc5")) != (stages[0] == "s5") and name in ("xp", "bc5", "xn"):
            if not (name == "xn" and stages[0] != "s5"):
                continue
        if name == "xn" and stages[0] == "s5":
            continue
        d[name] = nc.dram_tensor("d_" + name, shape, F32, kind="ExternalInput").ap()
    if stages[0] == "s5":
        for name, shape in (("ud", [D, T]), ("yd", [D, T]), ("kd", [16, G5, 240])):
            d[name] = nc.dram_tensor("d_" + name, shape, F32, kind="Internal").ap()
    d["out"] = nc.dram_tensor("d_out", [D, T], F32, kind="ExternalOutput").ap()
    return build_program(nc, d, stages)


def arrays_for(inputs, units, stages=STAGES):
    par, bc5, xn, xp = _pack(inputs)
    a = {"w": _weights(inputs, units), "par": par, "con": constants()}
    if stages[0] == "s5":
        a.update(bc5=bc5, xp=xp)
    else:
        a.update(xn=xn)
    return {"d_" + n: v for n, v in a.items()}


def kernel(**inputs):
    import concourse.bacc as _bacc
    from concourse.bass_utils import run_bass_kernel_spmd as _run

    nc = _bacc.Bacc("TRN2", target_bir_lowering=False, num_devices=1)
    units = make(nc)
    r = _run(nc, [arrays_for(inputs, units)], core_ids=[0])
    return np.ascontiguousarray(np.asarray(r.results[0]["d_out"]).T)[None]
```
